# Optimizing a Trainium2 kernel written in Bass

```python
import jax, jax.numpy as jnp
from jax import lax
import numpy as np
import jax
import jax.numpy as jnp

D_MODEL = 1024
BATCH = 1
SEQ = 256
DEPTH = 1

HEAD_DIM = 64
N_ATTN_HEADS = 8
ATTN_WIDTH = N_ATTN_HEADS * HEAD_DIM
N_SGU_GROUPS = 8
SGU_GROUP_DIM = 64
SGU_WIDTH = N_SGU_GROUPS * SGU_GROUP_DIM
MIX_WIDTH = ATTN_WIDTH + SGU_WIDTH
IN_WIDTH = 3 * ATTN_WIDTH + 2 * SGU_WIDTH
DILATION_PATTERNS = ((128, 1), (512, 4), (2048, 16))
SGU_CHUNK = 128
ROPE_THETA = 500000.0
ROT_DIM = HEAD_DIM // 4
N_GROUPS = 4
EXPERTS_PER_GROUP = 8
TOP_K = 2
EXPERT_FF = 256
LN_EPS = 1e-5
NEG_INF = -1e30
DEEPNORM_ALPHA = (2 * DEPTH) ** 0.25
DEEPNORM_BETA = (8 * DEPTH) ** -0.25


def layer_norm(x, g, b):
    xf = x.astype(jnp.float32)
    mu = jnp.mean(xf, -1, keepdims=True)
    xc = xf - mu
    var = jnp.mean(xc * xc, -1, keepdims=True)
    return xc * lax.rsqrt(var + LN_EPS) * g.astype(jnp.float32) + b.astype(jnp.float32)

def rope_tables(positions):
    inv = ROPE_THETA ** (-jnp.arange(0, ROT_DIM, 2, dtype=jnp.float32) / ROT_DIM)
    ang = positions.astype(jnp.float32)[..., None] * inv
    return jnp.cos(ang)[:, :, None, :], jnp.sin(ang)[:, :, None, :]

def apply_partial_rope(t, cos, sin):
    half = ROT_DIM // 2
    t1, t2 = t[..., :half], t[..., half:ROT_DIM]
    return jnp.concatenate([t1 * cos - t2 * sin, t2 * cos + t1 * sin, t[..., ROT_DIM:]], -1)

def dilated_window_attention(q, k, v, window, dilation):
    B, S, H, Dh = q.shape
    d = dilation
    L = S // d
    w_sub = window // d
    blk = min(w_sub, L)
    nb = -(-L // blk)
    Lp = nb * blk

    def to_blocks(t):
        t = t.reshape(B, L, d, H, Dh)
        t = jnp.pad(t, ((0, 0), (0, Lp - L), (0, 0), (0, 0), (0, 0)))
        return t.reshape(B, nb, blk, d, H, Dh)

    qb, kb, vb = to_blocks(q), to_blocks(k), to_blocks(v)

    def with_prev(t):
        prev = jnp.pad(t, ((0, 0), (1, 0), (0, 0), (0, 0), (0, 0), (0, 0)))[:, :nb]
        return jnp.concatenate([prev, t], axis=2)

    kk, vv = with_prev(kb), with_prev(vb)
    s = jnp.einsum('bnqrhe,bnkrhe->bnrhqk', qb, kk) * (Dh ** -0.5)
    qi = jnp.arange(blk)[:, None]
    kj = jnp.arange(2 * blk)[None, :]
    dist = qi + blk - kj
    key_pos = jnp.arange(nb)[:, None, None] * blk - blk + kj[None]
    valid = (dist >= 0) & (dist <= w_sub) & (key_pos >= 0)
    valid = valid[None, :, None, None]
    s = jnp.where(valid, s, NEG_INF)
    m = jnp.max(s, -1)
    p = jnp.where(valid, jnp.exp(s - m[..., None]), 0.0)
    l = jnp.sum(p, -1)
    m_t = jnp.moveaxis(m, -1, 2)
    l_t = jnp.moveaxis(l, -1, 2)
    o = jnp.einsum('bnrhqk,bnkrhe->bnqrhe', p, vv) / l_t[..., None]
    o = o.reshape(B, Lp, d, H, Dh)[:, :L].reshape(B, S, H, Dh)
    m_t = m_t.reshape(B, Lp, d, H)[:, :L].reshape(B, S, H)
    l_t = l_t.reshape(B, Lp, d, H)[:, :L].reshape(B, S, H)
    return o, m_t, l_t

def dilated_mixture_attention(q, k, v):
    res = [dilated_window_attention(q, k, v, w, d) for (w, d) in DILATION_PATTERNS]
    m_all = jnp.stack([r[1] for r in res], 0)
    l_all = jnp.stack([r[2] for r in res], 0)
    o_all = jnp.stack([r[0] for r in res], 0)
    wts = l_all * jnp.exp(m_all - jnp.max(m_all, 0, keepdims=True))
    o = jnp.sum(wts[..., None] * o_all, 0) / jnp.sum(wts, 0)[..., None]
    B, S, H, Dh = q.shape
    return o.reshape(B, S, H * Dh)

def spatial_gating(u, vs, ln_g, ln_b, w_spatial, b_spatial):
    B, S, _ = u.shape
    u = jax.nn.gelu(u.astype(jnp.float32), approximate=False)
    vs = layer_norm(jax.nn.gelu(vs.astype(jnp.float32), approximate=False), ln_g, ln_b)
    vc = vs.reshape(B, S // SGU_CHUNK, SGU_CHUNK, N_SGU_GROUPS, SGU_GROUP_DIM)
    causal = jnp.tril(jnp.ones((SGU_CHUNK, SGU_CHUNK), jnp.float32))
    w = w_spatial.astype(jnp.float32) * causal
    z = jnp.einsum('gts,bcsge->bctge', w, vc)
    z = z + b_spatial.astype(jnp.float32).T[None, None, :, :, None]
    return u * z.reshape(B, S, SGU_WIDTH)

def hierarchical_moe(h, w_group, b_group, w_expert, b_expert, w_gate_up, w_down):
    B, S, D = h.shape
    t = h.reshape(B * S, D)
    g_logits = (t @ w_group + b_group).astype(jnp.float32)
    p_group = jax.nn.softmax(g_logits, -1)
    g_onehot = jax.nn.one_hot(jnp.argmax(g_logits, -1), N_GROUPS, dtype=jnp.float32)
    p_sel = jnp.sum(p_group * g_onehot, -1)
    e_logits = (jnp.einsum('td,gde->tge', t, w_expert) + b_expert).astype(jnp.float32)
    e_sel = jnp.einsum('tge,tg->te', e_logits, g_onehot)
    top_vals, top_idx = lax.top_k(e_sel, TOP_K)
    top_w = jax.nn.softmax(top_vals, -1)
    e_gate = jnp.einsum('tk,tke->te', top_w,
                        jax.nn.one_hot(top_idx, EXPERTS_PER_GROUP, dtype=jnp.float32))
    gate = g_onehot[:, :, None] * e_gate[:, None, :] * p_sel[:, None, None]
    y = jnp.zeros((B * S, D), jnp.float32)
    for g in range(N_GROUPS):
        gu = jnp.einsum('td,edf->tef', t, w_gate_up[g]).astype(jnp.float32)
        a, b = gu[..., :EXPERT_FF], gu[..., EXPERT_FF:]
        act = jax.nn.silu(a) * b * gate[:, g, :, None]
        y = y + jnp.einsum('tef,efd->td', act, w_down[g].astype(jnp.float32))
    return y.reshape(B, S, D)

def first_inputs(seed: int = 0) -> dict:
    key = jax.random.key(seed)
    ks = jax.random.split(key, 18)
    f32 = jnp.float32
    x = jax.random.normal(ks[0], (BATCH, SEQ, D_MODEL), f32)
    positions = (jax.random.randint(ks[1], (BATCH, 1), 0, 4096, dtype=jnp.int32)
                 + jnp.arange(SEQ, dtype=jnp.int32)[None, :])
    col_scale = jnp.concatenate([jnp.ones((2 * ATTN_WIDTH,), f32),
                                 jnp.full((ATTN_WIDTH,), DEEPNORM_BETA, f32),
                                 jnp.ones((2 * SGU_WIDTH,), f32)])
    w_in = jax.random.normal(ks[2], (DEPTH, D_MODEL, IN_WIDTH), f32) * (D_MODEL ** -0.5) * col_scale
    sgu_ln_g = 1.0 + 0.1 * jax.random.normal(ks[3], (DEPTH, SGU_WIDTH), f32)
    sgu_ln_b = 0.02 * jax.random.normal(ks[4], (DEPTH, SGU_WIDTH), f32)
    w_spatial = jax.random.normal(ks[5], (DEPTH, N_SGU_GROUPS, SGU_CHUNK, SGU_CHUNK), f32) * (SGU_CHUNK ** -0.5)
    b_spatial = 1.0 + 0.1 * jax.random.normal(ks[6], (DEPTH, N_SGU_GROUPS, SGU_CHUNK), f32)
    w_out = jax.random.normal(ks[7], (DEPTH, MIX_WIDTH, D_MODEL), f32) * (MIX_WIDTH ** -0.5) * DEEPNORM_BETA
    ln1_g = 1.0 + 0.1 * jax.random.normal(ks[8], (DEPTH, D_MODEL), f32)
    ln1_b = 0.02 * jax.random.normal(ks[9], (DEPTH, D_MODEL), f32)
    w_group = jax.random.normal(ks[10], (DEPTH, D_MODEL, N_GROUPS), f32) * (D_MODEL ** -0.5)
    b_group = 0.01 * jax.random.normal(ks[11], (DEPTH, N_GROUPS), f32)
    w_expert = jax.random.normal(ks[12], (DEPTH, N_GROUPS, D_MODEL, EXPERTS_PER_GROUP), f32) * (D_MODEL ** -0.5)
    b_expert = 0.01 * jax.random.normal(ks[13], (DEPTH, N_GROUPS, EXPERTS_PER_GROUP), f32)
    w_gate_up = jax.random.normal(ks[14], (DEPTH, N_GROUPS, EXPERTS_PER_GROUP, D_MODEL, 2 * EXPERT_FF), f32) * (D_MODEL ** -0.5)
    w_down = jax.random.normal(ks[15], (DEPTH, N_GROUPS, EXPERTS_PER_GROUP, EXPERT_FF, D_MODEL), f32) * (EXPERT_FF ** -0.5) * DEEPNORM_BETA
    ln2_g = 1.0 + 0.1 * jax.random.normal(ks[16], (DEPTH, D_MODEL), f32)
    ln2_b = 0.02 * jax.random.normal(ks[17], (DEPTH, D_MODEL), f32)
    return {"x": x, "positions": positions, "w_in": w_in, "sgu_ln_g": sgu_ln_g,
            "sgu_ln_b": sgu_ln_b, "w_spatial": w_spatial, "b_spatial": b_spatial,
            "w_out": w_out, "ln1_g": ln1_g, "ln1_b": ln1_b, "w_group": w_group,
            "b_group": b_group, "w_expert": w_expert, "b_expert": b_expert,
            "w_gate_up": w_gate_up, "w_down": w_down, "ln2_g": ln2_g, "ln2_b": ln2_b}

def first_block(x, positions, w_in, sgu_ln_g, sgu_ln_b, w_spatial, b_spatial, w_out,
              ln1_g, ln1_b, w_group, b_group, w_expert, b_expert, w_gate_up, w_down,
              ln2_g, ln2_b):
    B, S, _ = x.shape
    cos, sin = rope_tables(positions)
    h = x.astype(jnp.float32)
    for layer in range(DEPTH):
        proj = h @ w_in[layer]
        a0 = ATTN_WIDTH
        q = proj[..., 0:a0].reshape(B, S, N_ATTN_HEADS, HEAD_DIM).astype(jnp.float32)
        k = proj[..., a0:2 * a0].reshape(B, S, N_ATTN_HEADS, HEAD_DIM).astype(jnp.float32)
        v = proj[..., 2 * a0:3 * a0].reshape(B, S, N_ATTN_HEADS, HEAD_DIM).astype(jnp.float32)
        u = proj[..., 3 * a0:3 * a0 + SGU_WIDTH]
        vs = proj[..., 3 * a0 + SGU_WIDTH:]
        q = apply_partial_rope(q, cos, sin)
        k = apply_partial_rope(k, cos, sin)
        attn_out = dilated_mixture_attention(q, k, v)
        sgu_out = spatial_gating(u, vs, sgu_ln_g[layer], sgu_ln_b[layer],
                                 w_spatial[layer], b_spatial[layer])
        mix = jnp.concatenate([attn_out, sgu_out], -1) @ w_out[layer].astype(jnp.float32)
        h = layer_norm(DEEPNORM_ALPHA * h + mix, ln1_g[layer], ln1_b[layer])
        moe = hierarchical_moe(h, w_group[layer], b_group[layer], w_expert[layer],
                               b_expert[layer], w_gate_up[layer], w_down[layer])
        h = layer_norm(DEEPNORM_ALPHA * h + moe, ln2_g[layer], ln2_b[layer])
    return h.astype(x.dtype)


GRID_W = 64
CTX_LEN = 256
N_MOD = 6
EPS = 1e-6
ROPE_BASE = 10000.0
Q_BLOCK = 128
RET_CHUNK = 128

MLA_HEADS = 8
MLA_NOPE = 64
MLA_ROPE = 32
MLA_QK = MLA_NOPE + MLA_ROPE
MLA_V = 64
Q_LORA = 256
KV_LORA = 128
RET_HEADS = 4
RET_DK = 64
RET_DV = 128
MIX_WIDTH_2 = MLA_HEADS * MLA_V + RET_HEADS * RET_DV

OFF_Q = 0
OFF_KV = OFF_Q + Q_LORA
OFF_PE = OFF_KV + KV_LORA
OFF_RQ = OFF_PE + MLA_ROPE
OFF_RK = OFF_RQ + RET_HEADS * RET_DK
OFF_RV = OFF_RK + RET_HEADS * RET_DK
OFF_RG = OFF_RV + RET_HEADS * RET_DV
D_IN = OFF_RG + RET_HEADS * RET_DV

N_EXPERTS = 32
TOP_K_2 = 4
D_FF = D_MODEL
SWIGLU_LIMIT = 7.0
SWIGLU_ALPHA = 1.702
MOE_BLOCK = 128


def rms_norm(x, w):
    xf = x.astype(jnp.float32)
    y = xf * lax.rsqrt(jnp.mean(xf * xf, axis=-1, keepdims=True) + EPS)
    return (y * w.astype(jnp.float32)).astype(x.dtype)

def modulate(h, shift, scale):
    return h * (1 + scale) + shift

def axial_rope_tables(L, dim):
    rows = L // GRID_W
    nf = dim // 4
    inv = jnp.power(ROPE_BASE, -jnp.arange(nf, dtype=jnp.float32) / nf)
    row = jnp.repeat(jnp.arange(rows, dtype=jnp.float32), GRID_W)
    col = jnp.tile(jnp.arange(GRID_W, dtype=jnp.float32), rows)
    pos = jnp.stack([row, col], axis=-1)
    ang = pos[:, :, None] * inv
    ang = jnp.broadcast_to(ang[:, :, None, :], (L, 2, 2, nf)).reshape(L, dim)
    return jnp.cos(ang), jnp.sin(ang)

def apply_axial_rope(x, cos, sin):
    d = x.shape[-1]
    xa = x.reshape(x.shape[:-1] + (2, 2, d // 4))
    rot = jnp.stack([-xa[..., 1, :], xa[..., 0, :]], axis=-2).reshape(x.shape)
    return (x.astype(jnp.float32) * cos + rot.astype(jnp.float32) * sin).astype(x.dtype)

def merge_heads(o):
    B, H, L, dv = o.shape
    return o.transpose(0, 2, 1, 3).reshape(B, L, H * dv)

def mla_q(p, g_q_lora, w_q_up, g_q_head, rope):
    B, L, _ = p.shape
    c_q = rms_norm(p[..., OFF_Q:OFF_Q + Q_LORA], g_q_lora)
    q = (c_q @ w_q_up).reshape(B, L, MLA_HEADS, MLA_QK)
    q = rms_norm(q, g_q_head).transpose(0, 2, 1, 3)
    if rope is not None:
        q = jnp.concatenate([q[..., :MLA_NOPE], apply_axial_rope(q[..., MLA_NOPE:], *rope)], axis=-1)
    return q

def mla_kv(p, g_kv_lora, w_kv_up, g_k_head, rope):
    B, L, _ = p.shape
    c_kv = rms_norm(p[..., OFF_KV:OFF_KV + KV_LORA], g_kv_lora)
    k_pe = p[..., OFF_PE:OFF_PE + MLA_ROPE]
    kv = (c_kv @ w_kv_up).reshape(B, L, MLA_HEADS, MLA_NOPE + MLA_V)
    k_nope, v = kv[..., :MLA_NOPE], kv[..., MLA_NOPE:]
    k_pe = jnp.broadcast_to(k_pe[:, :, None, :], (B, L, MLA_HEADS, MLA_ROPE))
    k = rms_norm(jnp.concatenate([k_nope, k_pe], axis=-1), g_k_head).transpose(0, 2, 1, 3)
    if rope is not None:
        k = jnp.concatenate([k[..., :MLA_NOPE], apply_axial_rope(k[..., MLA_NOPE:], *rope)], axis=-1)
    return k, v.transpose(0, 2, 1, 3)

def attend_blocks(q, k, v):
    B, H, Lq, dq = q.shape
    nb = Lq // Q_BLOCK
    scale = dq ** -0.5
    qb = q.reshape(B, H, nb, Q_BLOCK, dq).transpose(2, 0, 1, 3, 4)

    def one_block(qi):
        s = jnp.einsum('bhqd,bhkd->bhqk', qi, k).astype(jnp.float32) * scale
        pr = jax.nn.softmax(s, axis=-1).astype(v.dtype)
        return jnp.einsum('bhqk,bhkd->bhqd', pr, v)

    o = lax.map(one_block, qb)
    return o.transpose(1, 2, 0, 3, 4).reshape(B, H, Lq, v.shape[-1])

def ret_q(p, rope):
    B, L, _ = p.shape
    q = p[..., OFF_RQ:OFF_RK].reshape(B, L, RET_HEADS, RET_DK).transpose(0, 2, 1, 3)
    return q if rope is None else apply_axial_rope(q, *rope)

def ret_kv(p, rope):
    B, L, _ = p.shape
    k = p[..., OFF_RK:OFF_RV].reshape(B, L, RET_HEADS, RET_DK).transpose(0, 2, 1, 3) * (RET_DK ** -0.5)
    v = p[..., OFF_RV:OFF_RG].reshape(B, L, RET_HEADS, RET_DV).transpose(0, 2, 1, 3)
    if rope is not None:
        k = apply_axial_rope(k, *rope)
    return k, v

def retention_state(k, v, log_gamma, reverse):
    L = k.shape[2]
    j = jnp.arange(L, dtype=jnp.float32)
    expo = j if reverse else (L - 1) - j
    w = jnp.exp(expo[None, :] * log_gamma[:, None])
    return jnp.einsum('bhld,bhle->bhde', k.astype(jnp.float32) * w[None, :, :, None],
                      v.astype(jnp.float32))

def retention_scan(q, k, v, log_gamma, s0):
    B, H, L, DK = q.shape
    DV = v.shape[-1]
    C = RET_CHUNK
    n = L // C
    to_chunks = lambda t: t.astype(jnp.float32).reshape(B, H, n, C, t.shape[-1]).transpose(2, 0, 1, 3, 4)
    i = jnp.arange(C, dtype=jnp.float32)
    diff = i[:, None] - i[None, :]
    causal = diff >= 0
    decay_mask = jnp.where(causal, jnp.exp(jnp.where(causal, diff, 0.0)[None] * log_gamma[:, None, None]), 0.0)
    q_decay = jnp.exp((i + 1.0)[None, :] * log_gamma[:, None])[..., None]
    k_decay = jnp.exp(((C - 1.0) - i)[None, :] * log_gamma[:, None])[..., None]
    chunk_decay = jnp.exp(C * log_gamma)[:, None, None]

    def step(s, inp):
        qc, kc, vc = inp
        inner = jnp.einsum('bhid,bhjd->bhij', qc, kc) * decay_mask
        o = jnp.einsum('bhij,bhje->bhie', inner, vc) + jnp.einsum('bhid,bhde->bhie', qc * q_decay, s)
        s_new = s * chunk_decay + jnp.einsum('bhjd,bhje->bhde', kc * k_decay, vc)
        return s_new, o

    _, o = lax.scan(step, s0.astype(jnp.float32), (to_chunks(q), to_chunks(k), to_chunks(v)))
    return o.transpose(1, 2, 0, 3, 4).reshape(B, H, L, DV)

def retention_bidir(q, k, v, log_gamma, s0_f, s0_b):
    flip = lambda t: jnp.flip(t, axis=2)
    o_f = retention_scan(q, k, v, log_gamma[0], s0_f)
    o_b = flip(retention_scan(flip(q), flip(k), flip(v), log_gamma[1], s0_b))
    return o_f + o_b

def ret_output(o, p, g_ret_out):
    B, H, L, DV = o.shape
    o = rms_norm(o.transpose(0, 2, 1, 3), g_ret_out.reshape(H, DV)).reshape(B, L, H * DV)
    gate = p[..., OFF_RG:D_IN].astype(jnp.float32)
    return (o * jax.nn.silu(gate)).astype(p.dtype)

def moe_ffn(h, w_router, b_router, w1, b1, w2, b2):
    T, D = h.shape
    N = T * TOP_K_2
    logits = (h @ w_router).astype(jnp.float32) + b_router.astype(jnp.float32)
    top_val, top_idx = lax.top_k(logits, TOP_K_2)
    gates = jax.nn.softmax(top_val, axis=-1)
    flat_e = top_idx.reshape(N).astype(jnp.int32)
    flat_g = gates.reshape(N)
    ar = jnp.arange(N, dtype=jnp.int32)
    flat_tok = ar // TOP_K_2
    order = jnp.argsort(flat_e)
    sorted_e = flat_e[order]
    counts = jax.ops.segment_sum(jnp.ones((N,), jnp.int32), flat_e, num_segments=N_EXPERTS)
    padded = ((counts + MOE_BLOCK - 1) // MOE_BLOCK) * MOE_BLOCK
    pad_end = jnp.cumsum(padded)
    pad_start = pad_end - padded
    start = jnp.cumsum(counts) - counts
    dest = pad_start[sorted_e] + (ar - start[sorted_e])
    n_blocks = -(-N // MOE_BLOCK) + N_EXPERTS
    n_pad = n_blocks * MOE_BLOCK
    buf_tok = jnp.full((n_pad,), T, jnp.int32).at[dest].set(flat_tok[order])
    buf_g = jnp.zeros((n_pad,), jnp.float32).at[dest].set(flat_g[order])
    block_e = jnp.minimum(jnp.searchsorted(pad_end, jnp.arange(n_blocks, dtype=jnp.int32) * MOE_BLOCK,
                                           side='right'), N_EXPERTS - 1).astype(jnp.int32)
    h_pad = jnp.concatenate([h, jnp.zeros((1, D), h.dtype)], axis=0)

    def expert_block(args):
        tok, g, e = args
        xb = h_pad[tok]
        u = (xb @ w1[e] + b1[e]).astype(jnp.float32)
        glu = jnp.minimum(u[:, 0::2], SWIGLU_LIMIT)
        lin = jnp.clip(u[:, 1::2], -SWIGLU_LIMIT, SWIGLU_LIMIT)
        act = glu * jax.nn.sigmoid(SWIGLU_ALPHA * glu) * (lin + 1.0)
        y = act.astype(xb.dtype) @ w2[e] + b2[e]
        return y.astype(jnp.float32) * g[:, None]

    ys = lax.map(expert_block, (buf_tok.reshape(n_blocks, MOE_BLOCK),
                                buf_g.reshape(n_blocks, MOE_BLOCK), block_e))
    out = jnp.zeros((T + 1, D), jnp.float32).at[buf_tok].add(ys.reshape(n_pad, D))[:T]
    return out.astype(h.dtype)

def second_inputs(seed: int = 0) -> dict:
    key = jax.random.key(seed)
    ks = jax.random.split(key, 24)
    f32 = jnp.float32

    def nrm(k, shape, scale):
        return jax.random.normal(k, shape, f32) * scale

    def gain(k, shape):
        return 1.0 + 0.1 * jax.random.normal(k, shape, f32)

    dec0 = jnp.log(jnp.power(2.0, 5.0 + jnp.arange(RET_HEADS, dtype=f32)) - 1.0)
    return {
        'x': nrm(ks[0], (BATCH, SEQ, D_MODEL), 1.0),
        'c': nrm(ks[1], (BATCH, D_MODEL), 1.0),
        'ctx': nrm(ks[2], (BATCH, CTX_LEN, D_MODEL), 1.0),
        'c_ctx': nrm(ks[3], (D_MODEL,), 1.0),
        'g_attn': gain(ks[4], (DEPTH, D_MODEL)),
        'g_ffn': gain(ks[5], (DEPTH, D_MODEL)),
        'w_ada': nrm(ks[6], (DEPTH, D_MODEL, N_MOD * D_MODEL), 0.5 * D_MODEL ** -0.5),
        'b_ada': nrm(ks[7], (DEPTH, N_MOD * D_MODEL), 0.02),
        'w_in': nrm(ks[8], (DEPTH, D_MODEL, D_IN), D_MODEL ** -0.5),
        'g_q_lora': gain(ks[9], (DEPTH, Q_LORA)),
        'w_q_up': nrm(ks[10], (DEPTH, Q_LORA, MLA_HEADS * MLA_QK), Q_LORA ** -0.5),
        'g_q_head': gain(ks[11], (DEPTH, MLA_QK)),
        'g_kv_lora': gain(ks[12], (DEPTH, KV_LORA)),
        'w_kv_up': nrm(ks[13], (DEPTH, KV_LORA, MLA_HEADS * (MLA_NOPE + MLA_V)), KV_LORA ** -0.5),
        'g_k_head': gain(ks[14], (DEPTH, MLA_QK)),
        'ret_decay_logit': dec0 + nrm(ks[15], (DEPTH, 2, RET_HEADS), 0.1),
        'g_ret_out': gain(ks[16], (DEPTH, RET_HEADS * RET_DV)),
        'w_out': nrm(ks[17], (DEPTH, MIX_WIDTH_2, D_MODEL), MIX_WIDTH_2 ** -0.5),
        'w_router': nrm(ks[18], (DEPTH, D_MODEL, N_EXPERTS), D_MODEL ** -0.5),
        'b_router': nrm(ks[19], (DEPTH, N_EXPERTS), 0.01),
        'w_mlp1': nrm(ks[20], (DEPTH, N_EXPERTS, D_MODEL, 2 * D_FF), D_MODEL ** -0.5),
        'b_mlp1': nrm(ks[21], (DEPTH, N_EXPERTS, 2 * D_FF), 0.02),
        'w_mlp2': nrm(ks[22], (DEPTH, N_EXPERTS, D_FF, D_MODEL), D_FF ** -0.5),
        'b_mlp2': nrm(ks[23], (DEPTH, N_EXPERTS, D_MODEL), 0.02),
    }

def second_block(x, c, ctx, c_ctx, g_attn, g_ffn, w_ada, b_ada, w_in, g_q_lora, w_q_up, g_q_head,
              g_kv_lora, w_kv_up, g_k_head, ret_decay_logit, g_ret_out, w_out,
              w_router, b_router, w_mlp1, b_mlp1, w_mlp2, b_mlp2):
    B, L, D = x.shape
    Lc = ctx.shape[1]
    rope_mla = axial_rope_tables(L, MLA_ROPE)
    rope_ret = axial_rope_tables(L, RET_DK)
    for l in range(DEPTH):
        last = l == DEPTH - 1
        mod = (jax.nn.silu(c) @ w_ada[l] + b_ada[l]).reshape(B, N_MOD, 1, D)
        mod_c = (jax.nn.silu(c_ctx) @ w_ada[l] + b_ada[l]).reshape(N_MOD, 1, D)

        h = modulate(rms_norm(x, g_attn[l]), mod[:, 0], mod[:, 1])
        hc = modulate(rms_norm(ctx, g_attn[l]), mod_c[0], mod_c[1])
        p = h @ w_in[l]
        pc = hc @ w_in[l]

        k_c, v_c = mla_kv(pc, g_kv_lora[l], w_kv_up[l], g_k_head[l], None)
        k_x, v_x = mla_kv(p, g_kv_lora[l], w_kv_up[l], g_k_head[l], rope_mla)
        q_x = mla_q(p, g_q_lora[l], w_q_up[l], g_q_head[l], rope_mla)
        o_mla = attend_blocks(q_x, jnp.concatenate([k_c, k_x], axis=2), jnp.concatenate([v_c, v_x], axis=2))

        log_gamma = jax.nn.log_sigmoid(ret_decay_logit[l].astype(jnp.float32))
        kr_c, vr_c = ret_kv(pc, None)
        s0_f = retention_state(kr_c, vr_c, log_gamma[0], reverse=False)
        s0_b = retention_state(kr_c, vr_c, log_gamma[1], reverse=True)
        kr_x, vr_x = ret_kv(p, rope_ret)
        o_ret = retention_bidir(ret_q(p, rope_ret), kr_x, vr_x, log_gamma, s0_f, s0_b)

        mix = jnp.concatenate([merge_heads(o_mla), ret_output(o_ret, p, g_ret_out[l])], axis=-1)
        x = x + mod[:, 2] * (mix @ w_out[l])
        if not last:
            o_mla_c = attend_blocks(mla_q(pc, g_q_lora[l], w_q_up[l], g_q_head[l], None), k_c, v_c)
            s_zero = jnp.zeros((B, RET_HEADS, RET_DK, RET_DV), jnp.float32)
            o_ret_c = retention_bidir(ret_q(pc, None), kr_c, vr_c, log_gamma, s_zero, s_zero)
            mix_c = jnp.concatenate([merge_heads(o_mla_c), ret_output(o_ret_c, pc, g_ret_out[l])], axis=-1)
            ctx = ctx + mod_c[2] * (mix_c @ w_out[l])

        hf = modulate(rms_norm(x, g_ffn[l]), mod[:, 3], mod[:, 4]).reshape(B * L, D)
        moe_w = (w_router[l], b_router[l], w_mlp1[l], b_mlp1[l], w_mlp2[l], b_mlp2[l])
        if last:
            x = x + mod[:, 5] * moe_ffn(hf, *moe_w).reshape(B, L, D)
        else:
            hcf = modulate(rms_norm(ctx, g_ffn[l]), mod_c[3], mod_c[4]).reshape(B * Lc, D)
            y = moe_ffn(jnp.concatenate([hf, hcf], axis=0), *moe_w)
            x = x + mod[:, 5] * y[:B * L].reshape(B, L, D)
            ctx = ctx + mod_c[5] * y[B * L:].reshape(B, Lc, D)
    return x


def setup_inputs(seed=0):
    out = dict(first_inputs(seed))
    for name, value in second_inputs(seed + 1).items():
        if name != "x":
            out[name + "_2"] = value
    return out


def reference(
    x, positions, w_in, sgu_ln_g, sgu_ln_b, w_spatial, b_spatial, w_out, ln1_g, ln1_b, w_group,
    b_group, w_expert, b_expert, w_gate_up, w_down, ln2_g, ln2_b, c_2, ctx_2, c_ctx_2, g_attn_2,
    g_ffn_2, w_ada_2, b_ada_2, w_in_2, g_q_lora_2, w_q_up_2, g_q_head_2, g_kv_lora_2, w_kv_up_2,
    g_k_head_2, ret_decay_logit_2, g_ret_out_2, w_out_2, w_router_2, b_router_2, w_mlp1_2,
    b_mlp1_2, w_mlp2_2, b_mlp2_2,
):
    x = first_block(
        x, positions, w_in, sgu_ln_g, sgu_ln_b, w_spatial, b_spatial, w_out, ln1_g, ln1_b,
        w_group, b_group, w_expert, b_expert, w_gate_up, w_down, ln2_g, ln2_b,
    )
    return second_block(
        x, c_2, ctx_2, c_ctx_2, g_attn_2, g_ffn_2, w_ada_2, b_ada_2, w_in_2, g_q_lora_2,
        w_q_up_2, g_q_head_2, g_kv_lora_2, w_kv_up_2, g_k_head_2, ret_decay_logit_2,
        g_ret_out_2, w_out_2, w_router_2, b_router_2, w_mlp1_2, b_mlp1_2, w_mlp2_2, b_mlp2_2,
    )


_drawn_inputs = setup_inputs


def setup_inputs(seed=0):
    import zlib

    import numpy as np

    out = dict(_drawn_inputs(seed))
    spreads = {}
    factors = {'sgu_ln_b': 7.584,
     'b_group': 6.218,
     'b_expert': 6.58,
     'g_q_lora_2': 8.0,
     'g_q_head_2': 8.0,
     'g_kv_lora_2': 6.081,
     'g_k_head_2': 8.0,
     'b_router_2': 19.812,
     'b_mlp1_2': 23.599,
     'b_mlp2_2': 29.154,
     'g_ret_out_2': 4.728}
    for name, (base, spread) in spreads.items():
        noise = np.random.default_rng([zlib.crc32(name.encode()), seed]).standard_normal(out[name].shape)
        drawn = base * np.exp(spread * noise) if base else spread * noise
        out[name] = jnp.asarray(drawn.astype(out[name].dtype))
    for name, factor in factors.items():
        out[name] = (out[name] * factor).astype(out[name].dtype)
    return out
```

```python
from contextlib import ExitStack

import numpy as np

import concourse.bass as bass
from concourse import mybir

ALU = mybir.AluOpType
ACT = mybir.ActivationFunctionType
AX = mybir.AxisListType.X
F32, BF16, I32, U32 = mybir.dt.float32, mybir.dt.bfloat16, mybir.dt.int32, mybir.dt.uint32

P = 128
S, D = 256, 1024
TT, KT = S // P, D // P
HALF = D // 2
H1, DH1, AW = 8, 64, 512
SG, SGW = 8, 512
ROT1 = 8
NE = 32
FF1 = 256
NGRP, EPG = 4, 8
ALPHA = 2.0 ** 0.25
LN_EPS, RMS_EPS = 1e-5, 1e-6
NEG = -1e30
MH, NOPE, PE_W, MV = 8, 64, 32, 64
QK = NOPE + PE_W
QL, KVL = 256, 128
RH, RDK, RDV = 4, 64, 128
O_KV, O_PE, O_RQ = QL, QL + KVL, QL + KVL + PE_W
O_RK = O_RQ + RH * RDK
O_RV = O_RK + RH * RDK
O_RG = O_RV + RH * RDV
PIN = O_RG + RH * RDV
CW = O_RQ - O_KV + O_RG - O_RK
FF2 = 1024
LIMIT, SWA = 7.0, 1.702
SLOTS = 64
M1_UNITS, M1_CAP = NE // 2, 32
M2_UNITS, M2_CAP = NE, 64
M1_ROWS = M1_UNITS * (S // M1_CAP - 1)
M2_ROWS = M2_UNITS * (S // M2_CAP - 1)
OVER = 16
SMALL = 840
BANKS = 6


def host_constants():
    f = np.float32
    p = np.arange(P)
    c = {}
    c["ident"] = np.eye(P)
    c["upper"] = p[:, None] < p[None, :]
    c["ones"] = np.ones((P, P))
    c["tri"] = p[:, None] <= p[None, :]
    for t in range(TT):
        dist = (t * P + p)[:, None] - np.arange((t + 1) * P)[None, :]
        causal = dist >= 0
        count = causal * ((dist <= 128) * 1 + (dist % 4 == 0) + (dist % 16 == 0))
        c[f"cnt{t}"] = count
        c[f"neg{t}"] = np.where(count > 0, 0.0, NEG)
    c["iota32"] = np.tile(np.arange(32), (P, 1))
    c["iota64"] = np.tile(np.arange(64), (P, 1))
    c["iota16"] = np.tile(np.arange(16), (P, 1))
    c["m1_off"] = (M1_CAP * (p // M1_UNITS + 1))[:, None]
    c["m1_unit"] = (p % M1_UNITS)[:, None]
    c["m2_off"] = (M2_CAP * (p // M2_UNITS + 1))[:, None]
    c["m2_unit"] = (p % M2_UNITS)[:, None]
    c["eye3"] = (p[:, None] % 32 == np.arange(32)[None, :]) & (p[:, None] < 96)
    c["inv8"] = np.tile(500000.0 ** (-np.arange(8) / 8.0), (P, 1))
    pos = np.arange(S)
    grid = np.stack([pos // 64, pos % 64], -1).astype(f)
    for name, dim in (("M", PE_W), ("R", RDK)):
        nf = dim // 4
        inv = (10000.0 ** (-np.arange(nf) / nf)).astype(f)
        ang = (grid[:, :, None] * inv).astype(f)
        ang = np.broadcast_to(ang[:, :, None, :], (S, 2, 2, nf)).astype(np.float64)
        sign = np.array([-1.0, 1.0])[None, None, :, None]
        c["cos" + name] = np.cos(ang).reshape(TT, P, dim).transpose(1, 0, 2).reshape(P, -1)
        c["sin" + name] = (np.sin(ang) * sign).reshape(TT, P, dim).transpose(1, 0, 2).reshape(P, -1)
    early = ["tri", "cosM", "sinM", "cosR", "sinR"]
    masks = ["cnt0", "neg0", "cnt1", "neg1"]
    groups = [[k for k in c if k not in early + masks], early, masks]
    at, arrays = {}, []
    for i, names in enumerate(groups):
        w = 0
        for k in names:
            at[k] = (i, w, c[k].shape[1])
            w += c[k].shape[1]
        arrays.append(np.ascontiguousarray(np.concatenate([np.asarray(c[k], f) for k in names], 1)))
    kt, i = np.arange(4)[None, :, None], pos[None, None, :]
    j = kt * P + p[:, None, None] - S
    ahead = np.where(j < 0, i - j, np.maximum(i - j, 0))
    behind = np.where(j < 0, 2 * S + j - i, np.maximum(j - i, 0))
    seen_f, seen_b = (i >= j) * 1.0, (j >= i) * 1.0
    decay = np.concatenate([ahead.reshape(P, -1), behind.reshape(P, -1),
                            seen_f[:, 2:].reshape(P, -1), seen_b[:, 2:].reshape(P, -1)], 1).astype(f)
    return at, arrays, decay


class Outputs:

    def __init__(self, plan):
        self.at, self.by, self.nth = {}, [], []
        done = {"act": 0, "dve": 0}
        for name, count, engine in plan:
            first = len(self.by)
            for _ in range(count):
                done[engine] += 1
                self.by.append(engine)
                self.nth.append(done[engine])
            self.at.setdefault(name, []).extend(range(first, first + count))

    def bank(self, name, j):
        return self.at[name][j] % BANKS

    def filled(self, name, j):
        return self.at[name][j] + 1

    def before(self, name, j):
        n = self.at[name][j] - BANKS
        return (self.by[n], self.nth[n]) if n >= 0 else None

    def emptied(self, name, engine):
        last = self.at[name][-1]
        return max([self.nth[n] for n in range(last + 1) if self.by[n] == engine], default=0)


PLAN = (
    [("xT", 4, "act")]
    + [("proj", 4, "act"), ("ada", 1, "dve"), ("proj", 4, "act"), ("ada", 1, "dve"), ("proj", 2, "act"),
       ("ada", 1, "dve")]
    + [("wsT", 2, "dve"), ("bsT", 1, "dve"), ("qkT", 4, "act"), ("sc", 6, "dve"), ("z", 2, "dve"), ("ET", 6, "act")]
    + [("mT", 2, "act"), ("wo", 4, "dve"), ("hT", 4, "act")]
    + [("lg1", 1, "dve"), ("rk1", 1, "dve"), ("cn1", 1, "dve"), ("ps1", 1, "dve"), ("tb1", 1, "dve")]
    + [("mb", 8, "act"), ("hT4", 8, "act"), ("px", 8, "act"), ("pc", 6, "act"), ("cT", 2, "act"), ("kv", 8, "act"),
       ("qu", 4, "act")]
    + [("rT", 3, "act"), ("rs", 8, "dve"), ("ro", 2, "dve"), ("kqT", 12, "act"), ("rmT", 2, "act")]
    + [("s2", 2, "act")] + [("s2", 2, "act"), ("eT", 2, "dve")] * (MH - 1) + [("eT", 2, "dve")]
    + [("mb2", 6, "act"), ("wo2", 4, "dve"), ("hfT", 4, "act")]
    + [("lg2", 1, "dve"), ("rk2", 1, "dve"), ("cn2", 1, "dve"), ("ps2", 1, "dve"), ("tb2", 1, "dve")]
)


def build(nc, t, out, const_at):
    ctx = ExitStack()
    with ctx:
        def sb(name, shape, dt=F32):
            return ctx.enter_context(nc.sbuf_tensor(name, shape, dt))

        sems = {}

        def sem(name):
            if name not in sems:
                sems[name] = ctx.enter_context(nc.semaphore(name))
            return sems[name]

        outs = Outputs(PLAN)
        ps = ctx.enter_context(nc.psum_tensor("ps", [P, 8, 512], F32))

        wbig = sb("wbig", [P, 24576])
        wfront = sb("wfront", [P, 16384])
        xs = sb("xs", [P, TT, D])
        tT = sb("tT", [P, KT, S])
        act_ = sb("act_", [P, 5120])
        consts = sb("consts", [P, t["consts"].shape[1]])
        modrow = sb("modrow", [P, 3, 512])
        small = sb("small", [P, SMALL])
        pos_i = sb("pos_i", [P, TT], I32)
        idx_u = sb("idx_u", [P, TT, 8], U32)
        table_i = [sb(f"table_i{m}", [P, 32], I32) for m in range(2)]

        def const(name):
            i, o, w = const_at[name]
            return (consts[:, :], wbig[:, 23744:24256], wbig[:, 16384:17152])[i][:, o:o + w]

        ident = const("ident")
        ones = const("ones")

        free_small = [0]

        def cols(w):
            o = free_small[0]
            free_small[0] += w
            assert free_small[0] <= SMALL, free_small
            return small[:, o:o + w]

        def three(ap, n):
            return ap.rearrange("p (t c) -> p t c", t=n)

        w_in = three(wbig[:, 0:5 * 4096], 5)
        sgu_v = wbig[:, 20480:21504]
        w_sp = wbig[:, 21504:22528]
        b_sp = wbig[0:SG, 22528:22656]
        ln_v = wbig[:, 12288:16384]
        ada = wfront[:, :].rearrange("p (v k c) -> p v k c", v=2, k=KT)
        wo_w = wfront[:, 0:8192].rearrange("p (k c) -> p k c", k=KT)
        E0 = wfront[:, 8192:9216].rearrange("p (h k) -> p h k", h=H1)
        E1 = wfront[:, 9216:11264].rearrange("p (h k) -> p h k", h=H1)
        ET = wfront[:, 11264:15360].rearrange("p (k h q) -> p k h q", k=TT, h=H1)
        qk = three(act_[:, 0:2048], TT)
        mixT = act_[:, 0:2048].rearrange("p (k q) -> p k q", k=KT)
        v1 = three(act_[:, 2048:3072], TT)
        u1 = three(act_[:, 3072:4096], TT)
        vs1 = three(act_[:, 4096:5120], TT)
        wsT = wfront[:, 15360:16384].rearrange("p (g t) -> p g t", g=SG)
        wr1 = wbig[:, 22656:22944].rearrange("p (k c) -> p k c", k=KT)
        wr2 = wbig[:, 23104:23360].rearrange("p (k c) -> p k c", k=KT)
        ccT = wbig[:, 23360:23616].rearrange("p (k c) -> p k c", k=KT)
        cc = wbig[0:16, 23616:23744]
        rb1 = cols(NGRP + NE)
        rb2 = cols(NE)

        gu_w = wbig[:, 0:8192].rearrange("p (q k h c f) -> p q k h c f", q=2, k=KT, h=2, c=2)
        dn_w = wbig[:, 8192:12288].rearrange("p (q k f) -> p q k f", q=2, k=FF1 // P)
        w1_w = wbig[:, 0:16384].rearrange("p (k f) -> p k f", k=KT)
        w2_w = wbig[:, 16384:24576].rearrange("p (k f) -> p k f", k=FF2 // P)
        m_at = [0]

        def mbuf(w):
            o = m_at[0]
            m_at[0] += w
            assert m_at[0] <= 5120
            return act_[:, o:o + w]

        xg, xgT, m_t, m_l, m_s, m_a, m_aT, m_y = (mbuf(512) for _ in range(8))
        pgT = [mbuf(256), mbuf(256)]
        hot = mbuf(TT * SLOTS).rearrange("p (t s) -> p t s", t=TT)
        hotg = mbuf(TT * 2 * SLOTS).rearrange("p (t d s) -> p t d s", t=TT, d=2)
        keyc, gatec = mbuf(4), mbuf(4)

        def row_sel(q, tt, rows):
            return act_[:, 256 * q + P * tt:256 * q + P * tt + rows]

        bsel = wfront[0:96, 1536:1536 + SLOTS // 2].bitcast(BF16)
        b1p = wfront[0:96, 0:FF2].bitcast(BF16)
        b2p = wfront[0:96, FF2:FF2 + HALF].bitcast(BF16)
        braw = wfront[0:96, 2048:2048 + 3072]
        brem = wfront[0:96, 5120:5120 + 3072]
        bpart = wfront[0:96, 8192:8192 + 1536].bitcast(BF16)

        mb = wbig[:, 0:4096].rearrange("p (v c) -> p v c", v=4)
        cx = three(wbig[:, 4096:6144], TT)
        hT4 = wbig[:, 6144:10240].rearrange("p (k q) -> p k q", k=KT)
        hn = wbig[:, 10240:14336].rearrange("p (t c) -> p t c", t=4)
        sq = wbig[:, 14336:15360]
        px = three(wbig[:, 10240:10240 + TT * PIN], TT)
        pc = three(wbig[:, 14144:14144 + TT * CW], TT)
        K2 = wbig[:, 6144:6144 + 4 * MH * QK].rearrange("p (t h e) -> p t h e", t=4, h=MH)
        kT2 = wbig[0:QK, 0:4096].rearrange("p (h k) -> p h k", h=MH)
        qT2 = tT[0:QK, :, :]
        Q2 = act_[:, 0:TT * MH * QK].rearrange("p (t h e) -> p t h e", t=TT, h=MH)
        V2 = act_[:, 1536:3584].rearrange("p (t c) -> p t c", t=4)
        cn_ = act_[:, 3584:4608]
        cT = wbig[:, 4096:5120].rearrange("p (b q) -> p b q", b=8)
        vec2_at = 16384
        g_at = wbig[:, vec2_at:vec2_at + 1024]
        g_ff = wbig[:, vec2_at + 1024:vec2_at + 2048]
        g_ql = wbig[:, vec2_at + 2048:vec2_at + 2304]
        g_kvl = wbig[:, vec2_at + 2304:vec2_at + 2432]
        g_qh = wbig[:, vec2_at + 2432:vec2_at + 2528]
        g_kh = wbig[:, vec2_at + 2528:vec2_at + 2624]
        g_ro = wbig[:, vec2_at + 2624:vec2_at + 3136]
        VEC2 = 3136
        wqu = wbig[:, 19520:21056].rearrange("p (k c) -> p k c", k=2)
        wkvu = wbig[:, 21056:22080]
        mb2 = wbig[:, 22080:23104]
        mb34 = wbig[:, 4096:6144].rearrange("p (v c) -> p v c", v=2)
        w_in2 = wfront[:, 0:KT * PIN].rearrange("p (k c) -> p k c", k=KT)
        dext = wfront[:, 0:4096].rearrange("p (h k q) -> p h k q", h=RH, k=4)
        decay = wfront[:, 4096:7168]
        dtmp = wfront[:, 7168:8192]
        E2 = wfront[:, 0:8192].rearrange("p (s k) -> p s k", s=2 * MH)
        wo2_w = wfront[:, 8192:16384].rearrange("p (k c) -> p k c", k=KT)
        ET2 = wbig[:, 6144:10240].rearrange("p (s k q) -> p s k q", s=4, k=4)
        sd = wbig[:, 0:4096].rearrange("p (h k q) -> p h k q", h=RH, k=4)
        rT = act_[:, 3584:5120]
        rqT = rT[:, 0:512].rearrange("p (b q) -> p b q", b=2)
        rkT = rT[:, 512:1536].rearrange("p (b k) -> p b k", b=2)
        ro = wbig[:, 4096:5120].rearrange("p (t c) -> p t c", t=TT)
        mixT2 = wbig[:, 10240:12288].rearrange("p (k q) -> p k q", k=KT)
        scr = wbig[:, 5120:6144]
        hf = tT[:, :, :].rearrange("p k q -> p (k q)").rearrange("p (t c) -> p t c", t=TT)
        hfT = wbig[:, 6144:8192].rearrange("p (k q) -> p k q", k=KT)
        lgam = cols(2 * RH)
        lgt = cols(4 * 2 * RH)

        stats, mv = cols(12), cols(2 * TT)
        rstd = cols(64)
        ssum = cols(64)
        cs1 = cols(TT * 2 * ROT1).rearrange("p (f t e) -> p f t e", f=2, t=TT)
        rot = cols(5 * TT * ROT1)
        mx, mneg = cols(16), cols(16)
        lg = cols(TT * 36).rearrange("p (t c) -> p t c", t=TT)
        g8 = cols(TT * 8).rearrange("p (t c) -> p t c", t=TT)
        top8 = cols(TT * 8).rearrange("p (t c) -> p t c", t=TT)
        idxf = cols(TT * 8).rearrange("p (t c) -> p t c", t=TT)
        topw = cols(TT * 4).rearrange("p (t c) -> p t c", t=TT)
        psel = cols(TT)
        goh = cols(TT * NGRP).rearrange("p (t c) -> p t c", t=TT)
        sel, gate, key, oh = (cols(TT * NE).rearrange("p (t c) -> p t c", t=TT) for _ in range(4))
        flag = cols(2)
        ovq = cols(18)
        off = cols(OVER)
        pos_f = cols(TT)

        d_win = t["w_in"].rearrange("(k p) (c f) -> c p k f", p=P, f=512)
        d_ada = t["w_ada_2"].rearrange("(k p) (v f) -> v p k f", p=P, f=D)
        d_gu = t["w_gate_up"].rearrange("e (k p) f -> e p k f", p=P)
        d_dn = t["w_down"].rearrange("e (k p) f -> e p k f", p=P)
        d_w1 = t["w_mlp1_2"].rearrange("e (k p) f -> e k p f", p=P)
        d_w2 = t["w_mlp2_2"].rearrange("e (k p) f -> e k p f", p=P)

        def row(ap, n=P):
            return ap.partition_broadcast(n)

        block = ctx.enter_context(nc.Block())

        @block.sync
        def _(sp):
            def load(dst, src, name):
                sp.dma_start(dst, src).then_inc(sem(name), 16)

            load(consts[:, :], t["consts"], "ld_consts")
            load(wbig[:, 23744:24256], t["early"], "ld_early")
            load(xs[:, :, :], t["x"].rearrange("(t p) d -> p t d", p=P), "ld_x")
            load(cc, t["cc"], "ld_cc")

            def load_w_in(c):
                load(w_in[:, c, :].rearrange("p (k f) -> p k f", k=KT), d_win[c], f"ld_win{c}")

            def load_ada(r):
                for v in range(2):
                    load(ada[:, v], d_ada[2 * r + v], f"ld_ada{v}")

            load_w_in(0)
            load(pos_i[:, :], t["pos"], "ld_pos")
            load_w_in(1)
            load_ada(0)
            load_w_in(2)
            load_w_in(3)
            load(sgu_v, row(t["vec1"][0:1024]), "ld_sgu")
            load(w_sp.rearrange("p (g s) -> p g s", g=SG), t["w_spatial"].rearrange("g t s -> t g s"), "ld_wsp")
            load(b_sp, t["b_spatial"], "ld_bsp")
            load(rb1, row(t["rb1"]), "ld_rb1")
            load(rb2, row(t["rb2"]), "ld_rb2")
            load(wr1, t["wr1"].rearrange("(k p) c -> p k c", p=P), "ld_wr1")
            load(wr2, t["wr2"].rearrange("(k p) c -> p k c", p=P), "ld_wr2")
            load(lgt[:, 0:8], row(t["decay_logit"]), "ld_dl")
            sp.wait_ge(sem("modrow_zeroed"), 1)
            for g in range(4):
                load(modrow[32 * g:32 * g + 2, :, :], row(t["b_ada"][:, g, :], 2), "ld_bada")
            sp.wait_ge(sem("filled"), outs.filled("ada", 0))
            load_ada(1)
            load_w_in(4)
            sp.wait_ge(sem("filled"), outs.filled("ada", 1))
            load_ada(2)
            sp.wait_ge(sem("filled"), outs.filled("ada", 2))
            load(wo_w, t["w_out"].rearrange("(k p) c -> p k c", p=P), "ld_wo")
            sp.wait_ge(sem("filled"), outs.filled("proj", 9))
            load(wbig[:, 16384:17152], t["masks"], "ld_masks")
            load(ln_v, row(t["vec1"][1024:5120]), "ld_ln")

            def load_pair(u):
                for q in range(2):
                    e = u * 2 + q
                    for h in range(2):
                        yield (gu_w[:, q, 4 * h:4 * h + 4].rearrange("p k h c f -> p k (h c f)"),
                               d_gu[bass.ds(e, 1), :, 4 * h:4 * h + 4].rearrange("a p k f -> (a p) k f"),
                               f"ld_gu{q}{h}")
                for q in range(2):
                    e = u * 2 + q
                    yield (dn_w[:, q], d_dn[bass.ds(e, 1)].rearrange("a p k f -> (a p) k f"), f"ld_dn{q}")

            for dst, src, name in load_pair(0):
                load(dst, src, name)
            sp.wait_ge(sem("filled"), outs.filled("wo", 3))
            load(w_in2, t["w_in_2"].rearrange("(k p) c -> p k c", p=P), "ld_win2")
            load(wbig[:, vec2_at:vec2_at + VEC2], row(t["vec2"]), "ld_vec2")
            load(wqu, t["w_q_up_2"].rearrange("(k p) c -> p k c", p=P), "ld_wqu")
            load(wkvu, t["w_kv_up_2"], "ld_wkvu")

            def next_pair(u, n):
                for i, (dst, src, name) in enumerate(load_pair(u)):
                    if i < 4:
                        if i % 2 == 0:
                            sp.wait_ge(sem("m1_up_used"), n * 2)
                    else:
                        sp.wait_ge(sem("m1_dn_mm"), n)
                    load(dst, src, name)

            with sp.Fori(1, M1_UNITS) as u:
                next_pair(u, u)
            sp.wait_ge(sem("table_ready"), 1)
            n_over = sp.value_load(table_i[0][0:1, 16:17], min_val=0, max_val=OVER)
            with sp.If(n_over > 0):
                with sp.Fori(0, n_over) as i:
                    u = sp.value_load(table_i[0][0:1, bass.ds(i, 1)], min_val=0, max_val=M1_UNITS - 1)
                    next_pair(u, i + M1_UNITS)
            sp.wait_ge(sem("x1_ready"), 1)
            load(cx, t["ctx"].rearrange("(t p) d -> p t d", p=P), "ld_ctx")
            sp.wait_ge(sem("filled"), outs.filled("pc", 5))
            load(decay, t["decay"], "ld_decay")
            load(wo2_w, t["w_out_2"].rearrange("(k p) c -> p k c", p=P), "ld_wo2")

            def load_expert(e):
                for k in range(KT):
                    yield (w1_w[:, k, :], d_w1[bass.ds(e, 1), k].rearrange("a p f -> (a p) f"), f"ld_w1_{k}")
                for k in range(FF2 // P):
                    yield (w2_w[:, k, :], d_w2[bass.ds(e, 1), k].rearrange("a p f -> (a p) f"), f"ld_w2_{k}")

            sp.wait_ge(sem("wo2_added"), 4)
            for i in range(3):
                load(braw[32 * i:32 * i + 32, 0:2 * FF2], t["b_mlp1_2"], "ld_b")
                load(braw[32 * i:32 * i + 32, 2 * FF2:], t["b_mlp2_2"], "ld_b")
            sp.wait_ge(sem("filled"), outs.filled("lg2", 0))
            sp.wait_ge(sem("hf_ready"), 1)
            for dst, src, name in load_expert(0):
                load(dst, src, name)

            def next_expert(e, n):
                for i, (dst, src, name) in enumerate(load_expert(e)):
                    sp.wait_ge(sem("m2_w1_used" if i < KT else "m2_w2_used"), (n - 1) * KT + i % KT + 1)
                    load(dst, src, name)

            with sp.Fori(1, M2_UNITS) as e:
                next_expert(e, e)
            sp.wait_ge(sem("table_ready"), 2)
            n_over = sp.value_load(table_i[1][0:1, 16:17], min_val=0, max_val=OVER)
            with sp.If(n_over > 0):
                with sp.Fori(0, n_over) as i:
                    e = sp.value_load(table_i[1][0:1, bass.ds(i, 1)], min_val=0, max_val=M2_UNITS - 1)
                    next_expert(e, i + M2_UNITS)
            sp.wait_ge(sem("y_ready"), 1)
            sp.dma_start(out.rearrange("(t p) d -> p t d", p=P), xs[:, :, :]).then_inc(sem("stored"), 16)
            sp.wait_ge(sem("stored"), 16)

        @block.scalar
        def _(act):
            freed = sem("freed_act")
            emptied = [0]
            steps = [0]

            def step(ins):
                steps[0] += 1
                ins.then_inc(sem("act_step"), 1)
                act.wait_ge(sem("act_step"), steps[0])

            def empty(name, j, dst, view, func=ACT.Copy, **kw):
                act.wait_ge(sem("filled"), outs.filled(name, j))
                src = view(ps[:, outs.bank(name, j), :])
                emptied[0] += 1
                assert emptied[0] == outs.nth[outs.at[name][j]]
                return nc.scalar.activation(dst, src, func, **kw).then_inc(freed, 1)

            roots = [0]

            def root(n):
                roots[0] += 1
                act.wait_ge(sem("var_ready"), roots[0])
                nc.scalar.activation(rstd[:, 0:n], rstd[:, 0:n], ACT.Sqrt).then_inc(sem("root_ready"), 1)

            def four(ap):
                return ap.rearrange("p (b q) -> p b q", b=4)

            def same(ap):
                return ap

            act.wait_ge(sem("ld_cc"), 16)
            nc.scalar.activation(cc, cc, ACT.Silu).then_inc(sem("cc_ready"), 1)
            for j in range(4):
                tt, h = j // 2, j % 2
                empty("xT", j, tT[:, 4 * h:4 * h + 4, P * tt:P * tt + P], four)
            for j in range(10):
                c, tt = j // 2, j % 2
                if c < 2:
                    dst, f = qk[:, tt, 512 * c:512 * c + 512], ACT.Copy
                elif c == 2:
                    dst, f = v1[:, tt, :], ACT.Copy
                else:
                    dst, f = (u1 if c == 3 else vs1)[:, tt, :], ACT.Gelu
                empty("proj", j, dst, same, f)
            act.wait_ge(sem("angles"), 1)
            nc.scalar.activation(cs1[:, :, :, :].rearrange("p f t e -> p (f t e)"), rot[:, 0:2 * TT * ROT1],
                                 ACT.Sin).then_inc(sem("sincos"), 1)
            root(TT)
            for j in range(4):
                tt, h = j // 2, j % 2
                empty("qkT", j, tT[:, 4 * h:4 * h + 4, P * tt:P * tt + P], four)
            act.wait_ge(sem("sc_shift"), 2)
            nc.scalar.activation(E0, E0, ACT.Exp).then_inc(sem("sc_exp"), 1)
            nc.scalar.activation(E1, E1, ACT.Exp).then_inc(sem("sc_exp"), 1)
            for j in range(6):
                (qt, kt), h = ((0, 0), (1, 0), (1, 1))[j // 2], j % 2
                empty("ET", j, ET[:, kt, 4 * h:4 * h + 4, P * qt:P * qt + P], four)
            for m in range(2):
                act.wait_ge(sem("oT_mm"), m + 1)
                nc.scalar.activation(mixT[:, 2 * m:2 * m + 2, :], ps[:, 6 + m, :].rearrange("p (b q) -> p b q", b=2),
                                     ACT.Copy).then_inc(sem("oT_taken"), 1)
            for tt in range(TT):
                empty("mT", tt, mixT[:, 4:8, P * tt:P * tt + P], four)
            root(TT)
            for j in range(4):
                tt, h = j // 2, j % 2
                empty("hT", j, tT[:, 4 * h:4 * h + 4, P * tt:P * tt + P], four)

            def route_exps(m):
                if m == 0:
                    act.wait_ge(sem("grp_shift"), 1)
                    nc.scalar.activation(g8[:, :, 0:NGRP], g8[:, :, 0:NGRP], ACT.Exp).then_inc(sem("grp_exp"), 1)
                k = 2 if m == 0 else 4
                act.wait_ge(sem("top_shift"), m + 1)
                nc.scalar.activation(topw[:, :, 0:k], topw[:, :, 0:k], ACT.Exp).then_inc(sem("top_exp"), 1)

            def unit(m, n):
                p = f"m{m + 1}_"
                act.wait_ge(sem(p + "gathered"), n + 1)
                nc.scalar.activation(xg, ps[:, 6, :], ACT.Copy).then_inc(sem(p + "xg"), 1)
                act.wait_ge(sem(p + "xg_turned"), n + 1)
                nc.scalar.activation(xgT, ps[:, 6, :], ACT.Copy).then_inc(sem(p + "xgT"), 1)
                if m == 0:
                    act.wait_ge(sem(p + "up_mm"), n + 1)
                    nc.scalar.activation(m_s[:, 0:P], ps[:, 4, 0:P], ACT.Silu).then_inc(sem(p + "sig"), 1)
                else:
                    act.wait_ge(sem(p + "glu"), n + 1)
                    nc.scalar.activation(m_s, m_t, ACT.Sigmoid, scale=SWA).then_inc(sem(p + "sig"), 1)
                w = P if m == 0 else 512
                act.wait_ge(sem(p + "a_turned"), n + 1)
                nc.scalar.activation(m_aT[:, 0:w], ps[:, 4, 0:w], ACT.Copy).then_inc(sem(p + "aT"), 1)
                act.wait_ge(sem(p + "dn_mm"), n + 1)
                nc.scalar.activation(m_y, ps[:, 7, :], ACT.Copy).then_inc(sem(p + "y"), 1)

            def mixture(m):
                with act.Fori(0, (M1_UNITS, M2_UNITS)[m]) as u:
                    unit(m, u)
                act.wait_ge(sem("table_ready"), m + 1)
                n_over = act.value_load(table_i[m][0:1, 16:17], min_val=0, max_val=OVER)
                with act.If(n_over > 0):
                    with act.Fori(0, n_over) as i:
                        unit(m, i + (M1_UNITS, M2_UNITS)[m])

            route_exps(0)
            mixture(0)
            root(TT)

            act.wait_ge(sem("x1_ready"), 1)
            for j in range(8):
                empty("mb", j, mb[:, j // 2, 512 * (j % 2):512 * (j % 2) + 512], same)
            root(4)
            for j in range(8):
                tt, h = j // 2, j % 2
                empty("hT4", j, hT4[:, 4 * h:4 * h + 4, P * tt:P * tt + P], four)
            for j in range(8):
                c, tt = j // 2, j % 2
                w = min(512, PIN - 512 * c)
                empty("px", j, px[:, tt, 512 * c:512 * c + w], lambda a: a[:, 0:w])
            for j in range(6):
                c, tt = j // 2, j % 2
                o, w = ((0, 160), (160, 512), (672, 256))[c]
                empty("pc", j, pc[:, tt, o:o + w], lambda a: a[:, 0:w])
            step(nc.scalar.activation(px[:, :, O_RG:PIN], px[:, :, O_RG:PIN], ACT.Silu))
            act.wait_ge(sem("lg_neg"), 1)
            step(nc.scalar.activation(lgt[:, 8:16], lgt[:, 8:16], ACT.Exp))
            act.wait_ge(sem("lg_neg"), 2)
            nc.scalar.activation(lgt[:, 24:32], lgt[:, 16:24], ACT.Ln).then_inc(sem("lg_ln"), 1)
            root(4 + TT)
            for j in range(2):
                empty("cT", j, cT[:, 4 * j:4 * j + 4, :], four)
            for j in range(8):
                tile, h = j // 2, j % 2
                act.wait_ge(sem("filled"), outs.filled("kv", j))
                src = ps[:, outs.bank("kv", j), :].rearrange("p (h e) -> p h e", h=4)
                step(nc.scalar.activation(K2[:, tile, 4 * h:4 * h + 4, 0:NOPE], src[:, :, 0:NOPE], ACT.Copy))
                empty("kv", j, V2[:, tile, 256 * h:256 * h + 256].rearrange("p (h e) -> p h e", h=4),
                      lambda a: a.rearrange("p (h e) -> p h e", h=4)[:, :, NOPE:])
            for j in range(4):
                tt, h = j // 2, j % 2
                empty("qu", j, Q2[:, tt, 4 * h:4 * h + 4, :],
                      lambda a: a[:, 0:4 * QK].rearrange("p (h e) -> p h e", h=4))
            act.wait_ge(sem("ld_decay"), 16)
            act.wait_ge(sem("lg_ready"), 1)
            for h in range(RH):
                if h:
                    act.wait_ge(sem("dext_done"), h)
                nc.scalar.activation(dext[:, h].rearrange("p k q -> p (k q)"), decay[:, 0:1024], ACT.Exp,
                                     scale=lgam[:, h:h + 1]).then_inc(sem("dext_exp"), 1)
                nc.scalar.activation(dtmp, decay[:, 1024:2048], ACT.Exp,
                                     scale=lgam[:, RH + h:RH + h + 1]).then_inc(sem("dext_exp"), 1)
            for tt in range(TT):
                act.wait_ge(sem("filled"), outs.filled("rT", tt))
                b = four(ps[:, outs.bank("rT", tt), :])
                step(nc.scalar.activation(rqT[:, :, P * tt:P * tt + P], b[:, 0:2, :], ACT.Copy))
                empty("rT", tt, rkT[:, :, S + P * tt:S + P * tt + P], lambda a: four(a)[:, 2:4, :], ACT.Copy,
                      scale=RDK ** -0.5)
            empty("rT", 2, rkT[:, :, 0:S], lambda a: a.rearrange("p (b k) -> p b k", b=2), ACT.Copy,
                  scale=RDK ** -0.5)
            root(TT * RH)
            root(6 * MH)
            for j in range(12):
                tile, h = j // 2, j % 2
                dst = (kT2[:, 4 * h:4 * h + 4, P * tile:P * tile + P] if tile < 4 else
                       qT2[:, 4 * h:4 * h + 4, P * (tile - 4):P * (tile - 4) + P])
                empty("kqT", j, dst, lambda a: four(a)[0:QK])
            for tt in range(TT):
                empty("rmT", tt, mixT2[:, 4:8, P * tt:P * tt + P], four)
            act.wait_ge(sem("dext_used"), 1)
            for s in range(2 * MH):
                act.wait_ge(sem("s2_max"), s + 1)
                empty("s2", s, E2[:, s, :], same, ACT.Exp, bias=mneg[:, s:s + 1], scale=QK ** -0.5,
                      accum_out=mx[:, s:s + 1])
                if s in (11, 2 * MH - 1):
                    m = int(s > 11)
                    act.wait_ge(sem("oT2_mm"), m + 1)
                    nc.scalar.activation(mixT2[:, 2 * m:2 * m + 2, :],
                                         ps[:, 6 + m, :].rearrange("p (b q) -> p b q", b=2),
                                         ACT.Copy).then_inc(sem("oT2_taken"), 1)
            for j in range(6):
                v, h = j // 2, j % 2
                dst = mb2[:, 512 * h:512 * h + 512] if v == 0 else mb34[:, v - 1, 512 * h:512 * h + 512]
                empty("mb2", j, dst, same)
            root(TT)
            for j in range(4):
                tt, h = j // 2, j % 2
                empty("hfT", j, hfT[:, 4 * h:4 * h + 4, P * tt:P * tt + P], four)
            route_exps(1)
            mixture(1)
            for h in range(2):
                act.wait_ge(sem("mb5_mm"), h + 1)
                nc.scalar.activation(act_[:, 512 * h:512 * h + 512], ps[:, 6 + h, :], ACT.Copy)\
                    .then_inc(sem("mb5_taken"), 1)

        @block.vector
        def _(dve):
            freed = sem("freed_dve")
            count = {}

            def step(ins, name="dve_step"):
                count[name] = count.get(name, 0) + 1
                ins.then_inc(sem(name), 1)
                dve.wait_ge(sem(name), count[name])

            def take(name, j, w=512):
                dve.wait_ge(sem("filled"), outs.filled(name, j))
                return ps[:, outs.bank(name, j), 0:w]

            def emptied(ins, name, j):
                step(ins, "freed_dve")
                assert count["freed_dve"] == outs.nth[outs.at[name][j]]

            def bc(ap, shape, axis):
                return ap.unsqueeze(axis).to_broadcast(shape)

            def inverse_root(n):
                step(nc.vector.memset(ssum[:, 63:64], 0.0), "var_ready")
                dve.wait_ge(sem("root_ready"), count["var_ready"])
                step(nc.vector.reciprocal(rstd[:, 0:n], rstd[:, 0:n]))

            def layer_norms(x, g, b, last):
                halves = x.shape[-1] // 512
                for tt in range(TT):
                    for h in range(halves):
                        step(nc.vector.bn_stats(stats[:, 6 * h:6 * h + 6], x[:, tt, 512 * h:512 * h + 512]))
                    step(nc.vector.bn_aggr(mv[:, 2 * tt:2 * tt + 2], stats[:, 0:6 * halves]))
                    step(nc.vector.tensor_scalar(rstd[:, tt:tt + 1], mv[:, 2 * tt + 1:2 * tt + 2], LN_EPS, None, ALU.add))
                inverse_root(TT)
                for tt in range(TT):
                    y = x[:, tt, :]
                    step(nc.vector.tensor_scalar(y, y, mv[:, 2 * tt:2 * tt + 1], rstd[:, tt:tt + 1], ALU.subtract, ALU.mult))
                    step(nc.vector.tensor_tensor(y, y, g, ALU.mult))
                    step(nc.vector.tensor_tensor(y, y, b, ALU.add), last)

            step(nc.vector.memset(modrow[:, :, :], 0.0), "modrow_zeroed")
            step(nc.vector.memset(ccT, 0.0))
            dve.wait_ge(sem("ccT_mm"), 1)
            step(nc.vector.tensor_copy(ccT[:, :, 0:2], ps[:, 7, 0:16].rearrange("p (r k) -> p k r", r=2)), "ccT_ready")
            dve.wait_ge(sem("ld_pos"), 16)
            dve.wait_ge(sem("ld_consts"), 16)
            n = TT * ROT1
            two_pi = 2 * np.pi
            p1 = 6.28125
            p2 = float(np.floor((two_pi - p1) * 2 ** 21) / 2 ** 21)
            p3 = two_pi - p1 - p2
            magic = 1.5 * 2 ** 23
            ang, turns, cosang = rot[:, 0:n], rot[:, 2 * n:3 * n], rot[:, n:2 * n]
            step(nc.vector.tensor_copy(pos_f, pos_i[:, :]))
            step(nc.vector.tensor_tensor(three(ang, TT), bc(pos_f, [P, TT, ROT1], 2), bc(const("inv8"), [P, TT, ROT1], 1),
                                         ALU.mult))
            step(nc.vector.tensor_scalar(turns, ang, 1.0 / two_pi, None, ALU.mult))
            step(nc.vector.tensor_scalar(turns, turns, magic, None, ALU.add))
            step(nc.vector.tensor_scalar(turns, turns, -magic, None, ALU.add))
            for part in (p1, p2, p3):
                step(nc.vector.scalar_tensor_tensor(out=ang, in0=turns, scalar=-part, in1=ang, op0=ALU.mult, op1=ALU.add))
            step(nc.vector.tensor_scalar(cosang, ang, np.pi / 2, None, ALU.add))
            step(nc.vector.tensor_scalar(turns, cosang, np.pi, -two_pi, ALU.is_gt, ALU.mult))
            step(nc.vector.tensor_tensor(cosang, cosang, turns, ALU.add))
            lim = float(np.nextafter(np.float32(np.pi), np.float32(0)))
            step(nc.vector.tensor_scalar(rot[:, 0:2 * n], rot[:, 0:2 * n], lim, -lim, ALU.min, ALU.max), "angles")
            dve.wait_ge(sem("ld_bada"), 64)
            for r in range(3):
                emptied(nc.vector.tensor_tensor(modrow[:, r, :], take("ada", r), modrow[:, r, :], ALU.add), "ada", r)
            dve.wait_ge(sem("ld_early"), 16)
            for j in range(2):
                emptied(nc.vector.tensor_tensor(wsT[:, 4 * j:4 * j + 4, :], take("wsT", j).rearrange("p (g t) -> p g t", g=4),
                                                bc(const("tri"), [P, 4, P], 1), ALU.mult), "wsT", j)
            bsT = ssum[:, 0:SG]
            emptied(nc.vector.tensor_copy(bsT, take("bsT", 0, SG)), "bsT", 0)
            dve.wait_ge(sem("sincos"), 1)
            dve.wait_ge(sem("freed_act"), outs.nth[outs.at["proj"][3]])
            heads = qk.rearrange("p t (h e) -> p t h e", e=DH1)
            r1, r2 = heads[:, :, :, 0:ROT1], heads[:, :, :, ROT1:2 * ROT1]
            shape = [P, TT, 16, ROT1]
            sin_b, cos_b = (bc(cs1[:, f], shape, 2) for f in range(2))
            a, b, c2, d = (wfront[:, 8192 + 256 * i:8192 + 256 * (i + 1)].rearrange("p (t h e) -> p t h e", t=TT, h=16)
                           for i in range(4))
            for dst, x, y in ((a, r1, cos_b), (b, r2, sin_b), (c2, r2, cos_b), (d, r1, sin_b)):
                step(nc.vector.tensor_tensor(dst, x, y, ALU.mult))
            step(nc.vector.tensor_tensor(r1, a, b, ALU.subtract))
            step(nc.vector.tensor_tensor(r2, c2, d, ALU.add), "roped1")
            dve.wait_ge(sem("ld_sgu"), 16)
            dve.wait_ge(sem("freed_act"), outs.nth[outs.at["proj"][9]])
            layer_norms(vs1, sgu_v[:, 0:SGW], sgu_v[:, SGW:], "vs_ready")
            dve.wait_ge(sem("ld_masks"), 16)
            for j in range(6):
                if j < 2:
                    dst, m, hs, w = E0[:, 4 * j:4 * j + 4, :], const("neg0"), 4, P
                else:
                    dst, m, hs, w = E1[:, 2 * (j - 2):2 * (j - 2) + 2, :], const("neg1"), 2, S
                emptied(nc.vector.scalar_tensor_tensor(
                    out=dst, in0=take("sc", j).rearrange("p (h k) -> p h k", h=hs), scalar=DH1 ** -0.5,
                    in1=bc(m, [P, hs, w], 1), op0=ALU.mult, op1=ALU.add), "sc", j)
            for i, (e, w) in enumerate(((E0, P), (E1, S))):
                m8 = mx[:, 8 * i:8 * i + 8]
                step(nc.vector.tensor_reduce(m8, e, AX, ALU.max))
                step(nc.vector.tensor_tensor(e, e, bc(m8, [P, H1, w], 2), ALU.subtract), "sc_shift")
            for j in range(2):
                z = take("z", j).rearrange("p (g c e) -> p c g e", g=4, c=TT)
                for tt in range(TT):
                    dst = vs1[:, tt, 256 * j:256 * j + 256].rearrange("p (g e) -> p g e", g=4)
                    ins = nc.vector.tensor_tensor(dst, z[:, tt], bc(bsT[:, 4 * j:4 * j + 4], [P, 4, 64], 2), ALU.add)
                    if tt == 0:
                        step(ins)
                    else:
                        emptied(ins, "z", j)
            step(nc.vector.tensor_tensor(u1, u1, vs1, ALU.mult), "sgu_ready")
            for i, (e, w) in enumerate(((E0, P), (E1, S))):
                m8, r8 = mx[:, 8 * i:8 * i + 8], rstd[:, 8 * i:8 * i + 8]
                dve.wait_ge(sem("sc_exp"), i + 1)
                step(nc.vector.tensor_tensor(e, e, bc(const(f"cnt{i}"), [P, H1, w], 1), ALU.mult))
                step(nc.vector.tensor_reduce(m8, e, AX, ALU.add))
                step(nc.vector.reciprocal(r8, m8))
                step(nc.vector.tensor_tensor(e, e, bc(r8, [P, H1, w], 2), ALU.mult), "E_ready")
            dve.wait_ge(sem("ld_x"), 16)
            for j in range(4):
                x = xs[:, j // 2, 512 * (j % 2):512 * (j % 2) + 512]
                emptied(nc.vector.scalar_tensor_tensor(out=x, in0=x, scalar=ALPHA, in1=take("wo", j), op0=ALU.mult,
                                                       op1=ALU.add), "wo", j)
            dve.wait_ge(sem("ld_ln"), 16)
            layer_norms(xs, ln_v[:, 0:D], ln_v[:, D:2 * D], "h1_ready")

            def route(m):
                k = 2 if m == 0 else 4
                w = NGRP + NE if m == 0 else NE
                dve.wait_ge(sem(f"ld_rb{m + 1}"), 16)
                src = take(f"lg{m + 1}", 0, 2 * 64).rearrange("p (t c) -> p t c", t=TT)[:, :, 0:w]
                emptied(nc.vector.tensor_tensor(lg[:, :, 0:w], src, bc((rb1, rb2)[m], [P, TT, w], 1), ALU.add),
                        f"lg{m + 1}", 0)

                def best(vals):
                    for tt in range(TT):
                        step(nc.vector.max(top8[:, tt, :], vals[:, tt, :]))
                        step(nc.vector.max_index(idx_u[:, tt, :], top8[:, tt, :], vals[:, tt, :]))
                    step(nc.vector.tensor_copy(idxf, idx_u[:, :, :]))

                if m == 0:
                    step(nc.vector.memset(g8, -3e38))
                    step(nc.vector.tensor_copy(g8[:, :, 0:NGRP], lg[:, :, 0:NGRP]))
                    best(g8)
                    step(nc.vector.tensor_tensor(g8[:, :, 0:NGRP], lg[:, :, 0:NGRP],
                                                 top8[:, :, 0:1].to_broadcast([P, TT, NGRP]), ALU.subtract), "grp_shift")
                    step(nc.vector.tensor_tensor(goh, bc(const("iota32")[:, 0:NGRP], [P, TT, NGRP], 1),
                                                 idxf[:, :, 0:1].to_broadcast([P, TT, NGRP]), ALU.is_equal))
                    step(nc.vector.tensor_scalar(goh, goh, -1.0, -NEG, ALU.add, ALU.mult))
                    e4 = lg[:, :, NGRP:].rearrange("p t (g e) -> p t g e", g=NGRP)
                    step(nc.vector.tensor_tensor(e4, e4, bc(goh, [P, TT, NGRP, EPG], 3), ALU.add))
                    dve.wait_ge(sem("grp_exp"), 1)
                    step(nc.vector.tensor_reduce(psel, g8[:, :, 0:NGRP], AX, ALU.add))
                    step(nc.vector.reciprocal(psel, psel))
                    logits = lg[:, :, NGRP:]
                else:
                    logits = lg[:, :, 0:NE]
                best(logits)
                tw = topw[:, :, 0:k]
                step(nc.vector.tensor_tensor(tw, top8[:, :, 0:k], top8[:, :, 0:1].to_broadcast([P, TT, k]), ALU.subtract),
                     "top_shift")
                dve.wait_ge(sem("top_exp"), m + 1)
                den = ssum[:, 0:TT]
                step(nc.vector.tensor_reduce(den, tw, AX, ALU.add))
                step(nc.vector.reciprocal(den, den))
                if m == 0:
                    step(nc.vector.tensor_tensor(den, den, psel, ALU.mult))
                step(nc.vector.tensor_tensor(tw, tw, bc(den, [P, TT, k], 2), ALU.mult))
                step(nc.vector.memset(sel, 0.0))
                step(nc.vector.memset(gate, 0.0))
                for i in range(k):
                    shape = [P, TT, NE]
                    step(nc.vector.tensor_tensor(oh, bc(const("iota32"), shape, 1), idxf[:, :, i:i + 1].to_broadcast(shape),
                                                 ALU.is_equal))
                    step(nc.vector.tensor_tensor(sel, sel, oh, ALU.add))
                    step(nc.vector.tensor_tensor(oh, oh, topw[:, :, i:i + 1].to_broadcast(shape), ALU.mult))
                    step(nc.vector.tensor_tensor(gate, gate, oh, ALU.add))
                rows = (M1_ROWS, M2_ROWS)[m]
                units = (M1_UNITS, M2_UNITS)[m]
                for q in range(2 - m):
                    for tt in range(TT):
                        s = sel[:, tt, :].rearrange("p (u q) -> p q u", q=2 - m)[:, q, :]
                        step(nc.vector.tensor_copy(row_sel(q, tt, rows).rearrange("p (b u) -> p b u", u=units),
                                                   bc(s, [P, rows // units, units], 1)))
                step(nc.vector.memset(ovq, 0.0), "sel_ready")
                rank = take(f"rk{m + 1}", 0, TT * NE).rearrange("p (t c) -> p t c", t=TT)
                emptied(nc.vector.scalar_tensor_tensor(out=key, in0=rank, scalar=1.0, in1=sel, op0=ALU.add, op1=ALU.mult),
                        f"rk{m + 1}", 0)
                step(nc.vector.tensor_scalar(key, key, -1.0, None, ALU.add))
                o_col = const(f"m{m + 1}_off")[0:rows]
                cn = take(f"cn{m + 1}", 0, 4)
                f0 = flag[0:rows, 0:1]
                if m == 0:
                    step(nc.vector.tensor_copy(f0, cn[0:rows, 2:3]))
                    emptied(nc.vector.tensor_tensor(f0, cn[0:rows, 0:1], f0, ALU.max), "cn1", 0)
                else:
                    emptied(nc.vector.tensor_copy(f0, cn[0:rows, 0:1]), "cn2", 0)
                step(nc.vector.tensor_tensor(f0, f0, o_col, ALU.is_gt))
                step(nc.vector.tensor_copy(flag[0:rows, 1:2], f0), "flags")
                pl = take(f"ps{m + 1}", 0, 1)
                place = rstd[0:rows, 0:1]
                emptied(nc.vector.tensor_copy(place, pl[0:rows]), f"ps{m + 1}", 0)
                step(nc.vector.tensor_scalar(ovq[0:rows, 0:OVER], const("iota16")[0:rows], place, f0, ALU.is_equal, ALU.mult))
                step(nc.vector.tensor_copy(ovq[0:rows, OVER:OVER + 1], f0), "ovq_ready")
                tb = take(f"tb{m + 1}", 0, 96)
                step(nc.vector.tensor_copy(off, tb[:, 32:32 + OVER]))
                step(nc.vector.tensor_copy(table_i[m][:, 0:OVER], tb[:, 0:OVER]))
                emptied(nc.vector.tensor_copy(table_i[m][:, OVER:OVER + 1], tb[:, 64 + OVER:64 + OVER + 1]), f"tb{m + 1}", 0)
                step(nc.vector.memset(pgT[0], 0.0))
                step(nc.vector.memset(pgT[1], 0.0), "table_ready")

            UNIT_STEPS = (2, 4)

            def unit(m, u, n, over=None):
                p = f"m{m + 1}_"
                done = [0]

                def link(ins):
                    done[0] += 1
                    ins.then_inc(sem(p + "dve_step"), 1)
                    dve.wait_ge(sem(p + "dve_step"), n * UNIT_STEPS[m] + done[0])

                w = 2 if m == 0 else 1
                kc = keyc[:, 0:TT * w].rearrange("p (t c) -> p t c", t=TT)
                gc = gatec[:, 0:TT * w].rearrange("p (t c) -> p t c", t=TT)
                ksrc, gsrc = (x[:, :, bass.ds(u * w, w)] for x in (key, gate))
                if over is None:
                    link(nc.vector.tensor_copy(kc, ksrc))
                else:
                    link(nc.vector.tensor_scalar(kc, ksrc, over, None, ALU.subtract))
                link(nc.vector.tensor_copy(gc, gsrc))
                cap = SLOTS // w
                shape = [P, TT, w, cap]
                iota = const("iota64")[:, 0:cap].unsqueeze(1).unsqueeze(1).to_broadcast(shape)
                h4 = hot.rearrange("p t (c s) -> p t c s", c=w)
                nc.vector.tensor_tensor(h4, iota, bc(kc, shape, 3), ALU.is_equal).then_inc(sem(p + "hot"), 1)
                dve.wait_ge(sem(p + "hot"), n + 1)
                for i in range(2):
                    nc.vector.tensor_tensor(hotg[:, :, i, :].rearrange("p t (c s) -> p t c s", c=w), h4, bc(gc, shape, 3),
                                            ALU.mult).then_inc(sem(p + "hotg"), 1)
                if m == 1:
                    dve.wait_ge(sem("m2_bsel_free"), n + 1)
                    nc.vector.tensor_copy(bsel, const("eye3")[0:96, bass.ds(u, 1)].to_broadcast([96, SLOTS]))\
                        .then_inc(sem("m2_bsel"), 1)
                dve.wait_ge(sem(p + "hot_turned"), n + 1)
                for i in range(2):
                    h = slice(64 * i, 64 * i + 64)
                    nc.vector.tensor_copy(pgT[i][h, :], ps[h, 7, 0:2 * P]).then_inc(sem(p + "pgT"), 1)
                dve.wait_ge(sem(p + "up_mm"), n + 1)
                if m == 0:
                    dve.wait_ge(sem(p + "sig"), n + 1)
                    nc.vector.tensor_tensor(m_a[:, 0:P], m_s[:, 0:P], ps[:, 4, P:2 * P], ALU.mult)\
                        .then_inc(sem(p + "act"), 1)
                else:
                    uu = ps[:, 4:6, :].rearrange("p b (f g) -> p (b f) g", g=2)
                    nc.vector.tensor_scalar(m_t, uu[:, :, 0], LIMIT, None, ALU.min).then_inc(sem(p + "glu"), 1)
                    link(nc.vector.tensor_scalar(m_l, uu[:, :, 1], LIMIT, -LIMIT, ALU.min, ALU.max))
                    dve.wait_ge(sem(p + "glu"), n + 1)
                    link(nc.vector.scalar_tensor_tensor(out=m_l, in0=m_l, scalar=1.0, in1=m_t, op0=ALU.add, op1=ALU.mult))
                    dve.wait_ge(sem(p + "sig"), n + 1)
                    nc.vector.tensor_tensor(m_a, m_l, m_s, ALU.mult).then_inc(sem(p + "act"), 1)
                assert done[0] == UNIT_STEPS[m]

            def mixture(m):
                units = (M1_UNITS, M2_UNITS)[m]
                with dve.Fori(0, units) as u:
                    unit(m, u, u)
                n_over = dve.value_load(table_i[m][0:1, 16:17], min_val=0, max_val=OVER)
                with dve.If(n_over > 0):
                    with dve.Fori(0, n_over) as i:
                        u = dve.value_load(table_i[m][0:1, bass.ds(i, 1)], min_val=0, max_val=units - 1)
                        unit(m, u, i + units, off[:, bass.ds(i, 1)])

            route(0)
            mixture(0)
            dve.wait_ge(sem("m1_scattered"), 1)
            for tt in range(TT):
                x = xs[:, tt, :]
                step(nc.vector.scalar_tensor_tensor(out=x, in0=x, scalar=ALPHA,
                                                    in1=ps[:, 2 * tt:2 * tt + 2, :].rearrange("p b c -> p (b c)"),
                                                    op0=ALU.mult, op1=ALU.add))
            layer_norms(xs, ln_v[:, 2 * D:3 * D], ln_v[:, 3 * D:4 * D], "dve_step")
            step(nc.vector.memset(mneg, 0.0), "x1_ready")

            def mean_sq(x, width, at, lead):
                dst = rstd[:, at:at + lead]
                sqv = scr[:, 0:lead * width].rearrange("p (a b) -> p a b", a=lead)
                step(nc.vector.tensor_tensor(sqv, x, x, ALU.mult))
                step(nc.vector.tensor_reduce(dst, sqv, AX, ALU.add))
                step(nc.vector.tensor_scalar(dst, dst, 1.0 / width, RMS_EPS, ALU.mult, ALU.add))

            def mean_sq_row(x, at, scratch):
                dst = rstd[:, at:at + 1]
                step(nc.vector.tensor_tensor_reduce(out=scratch, in0=x, in1=x, scale=1.0 / x.shape[-1], scalar=RMS_EPS,
                                                    op0=ALU.mult, op1=ALU.add, accum_out=dst))

            dve.wait_ge(sem("ld_vec2"), 16)
            dve.wait_ge(sem("freed_act"), outs.emptied("mb", "act"))
            for v in (1, 3):
                step(nc.vector.scalar_tensor_tensor(out=mb[:, v, :], in0=mb[:, v, :], scalar=1.0, in1=g_at, op0=ALU.add,
                                                    op1=ALU.mult))
            dve.wait_ge(sem("ld_ctx"), 16)
            tiles = [cx[:, 0, :], cx[:, 1, :], xs[:, 0, :], xs[:, 1, :]]
            for j, x in enumerate(tiles):
                mean_sq_row(x, j, sq)
            inverse_root(4)
            for j, x in enumerate(tiles):
                v = 2 if j < 2 else 0
                step(nc.vector.scalar_tensor_tensor(out=hn[:, j, :], in0=x, scalar=rstd[:, j:j + 1], in1=mb[:, v + 1, :],
                                                    op0=ALU.mult, op1=ALU.mult))
                step(nc.vector.tensor_tensor(hn[:, j, :], hn[:, j, :], mb[:, v, :], ALU.add), "hn_ready")
            dve.wait_ge(sem("ld_dl"), 16)
            x, e, one, ln = (lgt[:, 8 * i:8 * i + 8] for i in range(4))
            fix = lgam
            step(nc.vector.tensor_scalar(fix, x, -1.0, None, ALU.mult))
            step(nc.vector.tensor_tensor(fix, fix, x, ALU.max))
            step(nc.vector.tensor_scalar(e, fix, -1.0, None, ALU.mult), "lg_neg")
            dve.wait_ge(sem("act_step"), 2)
            step(nc.vector.tensor_scalar(one, e, 1.0, None, ALU.add), "lg_neg")
            dve.wait_ge(sem("lg_ln"), 1)
            step(nc.vector.tensor_scalar(fix, one, 1.0, None, ALU.is_equal))
            step(nc.vector.tensor_tensor(ln, ln, fix, ALU.add))
            step(nc.vector.scalar_tensor_tensor(out=one, in0=one, scalar=-1.0, in1=fix, op0=ALU.add, op1=ALU.add))
            step(nc.vector.reciprocal(one, one))
            step(nc.vector.tensor_tensor(ln, ln, e, ALU.mult))
            step(nc.vector.tensor_tensor(ln, ln, one, ALU.mult))
            step(nc.vector.tensor_scalar(fix, x, 0.0, None, ALU.min))
            step(nc.vector.tensor_tensor(lgam, fix, ln, ALU.subtract), "lg_ready")
            dve.wait_ge(sem("freed_act"), outs.emptied("pc", "act"))
            lat = [pc[:, 0, 0:KVL], pc[:, 1, 0:KVL], px[:, 0, O_KV:O_PE], px[:, 1, O_KV:O_PE]]
            for j, x in enumerate(lat):
                mean_sq_row(x, j, scr[:, 0:KVL])
            for j in range(TT):
                mean_sq_row(px[:, j, 0:QL], 4 + j, scr[:, 0:QL])
            inverse_root(4 + TT)
            for j, x in enumerate(lat):
                step(nc.vector.scalar_tensor_tensor(out=cn_[:, KVL * j:KVL * j + KVL], in0=x, scalar=rstd[:, j:j + 1],
                                                    in1=g_kvl, op0=ALU.mult, op1=ALU.mult))
            for j in range(TT):
                step(nc.vector.scalar_tensor_tensor(out=cn_[:, 512 + QL * j:512 + QL * j + QL], in0=px[:, j, 0:QL],
                                                    scalar=rstd[:, 4 + j:5 + j], in1=g_ql, op0=ALU.mult, op1=ALU.mult),
                     "latents")

            def axial(x, heads, dim, name, tt, last):
                nf = dim // 4
                cosv, sinv = (const(k + name)[:, dim * tt:dim * tt + dim] for k in ("cos", "sin"))
                tmp = scr[:, 0:heads * dim].rearrange("p (h e) -> p h e", h=heads)
                for s in range(2):
                    for ax in range(2):
                        o, i = 2 * nf * ax + nf * s, 2 * nf * ax + nf * (1 - s)
                        step(nc.vector.tensor_tensor(tmp[:, :, o:o + nf], x[:, :, i:i + nf],
                                                     bc(sinv[:, o:o + nf], [P, heads, nf], 1), ALU.mult))
                step(nc.vector.tensor_tensor(x, x, bc(cosv, [P, heads, dim], 1), ALU.mult))
                step(nc.vector.tensor_tensor(x, x, tmp, ALU.add), last)

            for tt in range(TT):
                axial(px[:, tt, O_RQ:O_RV].rearrange("p (h e) -> p h e", h=2 * RH), 2 * RH, RDK, "R", tt, "roped_r")
            dve.wait_ge(sem("ld_decay"), 16)
            for h in range(RH):
                dve.wait_ge(sem("dext_exp"), 2 * h + 2)
                own, back = dext[:, h, 2:4, :].rearrange("p k q -> p (k q)"), dtmp[:, 512:1024]
                step(nc.vector.tensor_tensor(own, own, decay[:, 2048:2560], ALU.mult))
                step(nc.vector.tensor_tensor(back, back, decay[:, 2560:3072], ALU.mult))
                d = dext[:, h].rearrange("p k q -> p (k q)")
                step(nc.vector.tensor_tensor(d, d, dtmp, ALU.add), "dext_done")
            for j in range(2 * RH):
                h, half = j // 2, j % 2
                d = dext[:, h, 2 * half:2 * half + 2, :].rearrange("p k q -> p (k q)")
                emptied(nc.vector.tensor_tensor(sd[:, h, 2 * half:2 * half + 2, :].rearrange("p k q -> p (k q)"),
                                                take("rs", j), d, ALU.mult), "rs", j)
            step(nc.vector.memset(ssum[:, 32:33], 0.0), "dext_used")
            for tt in range(TT):
                emptied(nc.vector.tensor_copy(ro[:, tt, :], take("ro", tt)), "ro", tt)
            step(nc.vector.memset(ssum[:, 32:33], 0.0), "ro_taken")
            o4 = ro.rearrange("p t (h e) -> p t h e", h=RH)
            for tt in range(TT):
                mean_sq(o4[:, tt], RDV, RH * tt, RH)
            inverse_root(RH * TT)
            for tt in range(TT):
                step(nc.vector.tensor_tensor(o4[:, tt], o4[:, tt], bc(rstd[:, RH * tt:RH * tt + RH], [P, RH, RDV], 2),
                                             ALU.mult))
                step(nc.vector.tensor_tensor(ro[:, tt, :], ro[:, tt, :], g_ro, ALU.mult))
                step(nc.vector.tensor_tensor(ro[:, tt, :], ro[:, tt, :], px[:, tt, O_RG:PIN], ALU.mult), "ro_ready")
            dve.wait_ge(sem("freed_act"), outs.emptied("qu", "act"))
            for j in range(4):
                pe = pc[:, j, KVL:KVL + PE_W] if j < 2 else px[:, j - 2, O_PE:O_RQ]
                step(nc.vector.tensor_copy(K2[:, j, :, NOPE:QK], bc(pe, [P, MH, PE_W], 1)))
            for j in range(6):
                mean_sq(K2[:, j] if j < 4 else Q2[:, j - 4], QK, MH * j, MH)
            inverse_root(6 * MH)
            for j in range(6):
                x = K2[:, j] if j < 4 else Q2[:, j - 4]
                g = g_kh if j < 4 else g_qh
                step(nc.vector.tensor_tensor(x, x, bc(rstd[:, MH * j:MH * j + MH], [P, MH, QK], 2), ALU.mult))
                step(nc.vector.tensor_tensor(x, x, bc(g, [P, MH, QK], 1), ALU.mult))
                if j >= 2:
                    axial(x[:, :, NOPE:QK], MH, PE_W, "M", j % 2, "dve_step")
            step(nc.vector.memset(ssum[:, 32:33], 0.0), "kq_ready")

            def weights(s):
                dve.wait_ge(sem("freed_act"), outs.nth[outs.at["s2"][s]])
                step(nc.vector.reciprocal(rstd[:, s:s + 1], mx[:, s:s + 1]))
                step(nc.vector.tensor_scalar(E2[:, s, :], E2[:, s, :], rstd[:, s:s + 1], None, ALU.mult), "E2_ready")

            def turned(h):
                for qt in range(TT):
                    if h >= 4 and qt == 0:
                        dve.wait_ge(sem("oT2_head"), h - 3)
                    emptied(nc.vector.tensor_copy(ET2[:, h % 4, :, P * qt:P * qt + P],
                                                  take("eT", 2 * h + qt).rearrange("p (k q) -> p k q", k=4)),
                            "eT", 2 * h + qt)

            for h in range(MH + 1):
                if h < MH:
                    for s in (2 * h, 2 * h + 1):
                        src = take("s2", s)
                        step(nc.vector.tensor_reduce(ssum[:, s:s + 1], src, AX, ALU.max))
                        step(nc.vector.tensor_scalar(mneg[:, s:s + 1], ssum[:, s:s + 1], -QK ** -0.5, None, ALU.mult), "s2_max")
                    for s in (2 * h, 2 * h + 1):
                        weights(s)
                if h:
                    turned(h - 1)
            dve.wait_ge(sem("freed_act"), outs.emptied("mb2", "act"))
            for j in range(4):
                tt, h = j // 2, j % 2
                cut = slice(512 * h, 512 * h + 512)
                gated = wfront[:, 512 * j:512 * j + 512]
                emptied(nc.vector.tensor_tensor(gated, take("wo2", j), mb2[:, cut], ALU.mult), "wo2", j)
                step(nc.vector.tensor_tensor(xs[:, tt, cut], xs[:, tt, cut], gated, ALU.add), "wo2_added")
            step(nc.vector.scalar_tensor_tensor(out=mb34[:, 1, :], in0=mb34[:, 1, :], scalar=1.0, in1=g_ff, op0=ALU.add,
                                                op1=ALU.mult))
            for tt in range(TT):
                mean_sq_row(xs[:, tt, :], tt, wbig[:, 12288:13312])
            inverse_root(TT)
            for tt in range(TT):
                step(nc.vector.scalar_tensor_tensor(out=hf[:, tt, :], in0=xs[:, tt, :], scalar=rstd[:, tt:tt + 1],
                                                    in1=mb34[:, 1, :], op0=ALU.mult, op1=ALU.mult))
                step(nc.vector.tensor_tensor(hf[:, tt, :], hf[:, tt, :], mb34[:, 0, :], ALU.add),
                     "hf_part" if tt == 0 else "hf_ready")
            dve.wait_ge(sem("ld_b"), 96)
            parts = []
            src = braw
            for i in range(3):
                step(nc.vector.tensor_copy(bpart, src))
                r = slice(32 * i, 32 * i + 32)
                step(nc.vector.tensor_copy(b1p[r, :], bpart[r, 0:2 * FF2]))
                step(nc.vector.tensor_copy(b2p[r, :], bpart[r, 2 * FF2:]), "bias_parts")
                if i < 2:
                    step(nc.vector.tensor_tensor(brem, src, bpart, ALU.subtract))
                    src = brem
            route(1)
            mixture(1)
            dve.wait_ge(sem("m2_scattered"), 1)
            dve.wait_ge(sem("mb5_taken"), 2)
            for tt in range(TT):
                prod = act_[:, 1024 + 1024 * tt:2048 + 1024 * tt]
                step(nc.vector.tensor_tensor(prod, ps[:, 2 * tt:2 * tt + 2, :].rearrange("p b c -> p (b c)"),
                                             act_[:, 0:1024], ALU.mult))
                step(nc.vector.tensor_tensor(xs[:, tt, :], xs[:, tt, :], prod, ALU.add))
            step(nc.vector.memset(mneg, 0.0), "y_ready")

        @block.tensor
        def _(pe):
            filled = sem("filled")

            def bank(name, j):
                b = outs.before(name, j)
                if b is not None:
                    pe.wait_ge(sem("freed_" + b[0]), b[1])
                return ps[:, outs.bank(name, j), :]

            def turn(name, j, blocks):
                dst = bank(name, j)
                for i, b in enumerate(blocks):
                    n = b.shape[-1]
                    m = b.shape[0]
                    mm = nc.tensor.transpose(dst[0:n, P * i:P * i + m] if m == P else dst[0:n, 0:m], b, ident[0:m, 0:m])
                mm.then_inc(filled, 1)

            def quarter(ap, h):
                return [ap[:, P * (4 * h + i):P * (4 * h + i) + P] for i in range(4)]

            pe.wait_ge(sem("ld_consts"), 16)
            pe.wait_ge(sem("ld_x"), 16)
            for j in range(4):
                turn("xT", j, quarter(xs[:, j // 2, :], j % 2))
            pe.wait_ge(sem("cc_ready"), 1)
            nc.tensor.transpose(ps[:, 7, 0:16], cc, ident[0:16, 0:16]).then_inc(sem("ccT_mm"), 1)

            def proj(c):
                pe.wait_ge(sem(f"ld_win{c}"), 16)
                for tt in range(TT):
                    dst = bank("proj", 2 * c + tt)
                    if c == 0:
                        pe.wait_ge(freed_act, outs.nth[outs.at["xT"][2 * tt + 1]])
                    for k in range(KT):
                        mm = nc.tensor.matmul(dst, tT[:, k, P * tt:P * tt + P], w_in[:, c, 512 * k:512 * k + 512],
                                              start=(k == 0), stop=(k == KT - 1))
                    mm.then_inc(filled, 1)

            def modulation(r):
                dst = bank("ada", r)
                for v in range(2):
                    pe.wait_ge(sem(f"ld_ada{v}"), 16 * (r + 1))
                if r == 0:
                    pe.wait_ge(sem("ccT_ready"), 1)
                for k in range(KT):
                    for g in range(4):
                        mm = nc.tensor.matmul(dst[32 * g:32 * g + 32, :], ccT[:, k, :],
                                              ada[:, g // 2, k, 512 * (g % 2):512 * (g % 2) + 512],
                                              start=(k == 0), stop=(k == KT - 1))
                mm.then_inc(filled, 1)

            freed_act = sem("freed_act")
            proj(0)
            proj(1)
            modulation(0)
            proj(2)
            proj(3)
            modulation(1)
            proj(4)
            modulation(2)
            pe.wait_ge(sem("ld_wsp"), 16)
            for j in range(2):
                turn("wsT", j, quarter(w_sp, j))
            pe.wait_ge(sem("ld_bsp"), 16)
            turn("bsT", 0, [b_sp])
            pe.wait_ge(sem("roped1"), 1)
            for j in range(4):
                turn("qkT", j, quarter(qk[:, j // 2, :], j % 2))
            pe.wait_ge(freed_act, outs.emptied("qkT", "act"))
            order = [0, 2, 4, 6, 1, 3, 5, 7]
            for j in range(6):
                dst = bank("sc", j)
                qt, hs = (0, order[4 * j:4 * j + 4]) if j < 2 else (1, order[2 * (j - 2):2 * (j - 2) + 2])
                w = P * (qt + 1)
                for i, h in enumerate(hs):
                    r = slice(64 * (h % 2), 64 * (h % 2) + 64)
                    mm = nc.tensor.matmul(dst[:, w * i:w * i + w], tT[r, h // 2, P * qt:P * qt + P],
                                          tT[r, 4 + h // 2, 0:w], start=True, stop=True)
                mm.then_inc(filled, 1)
            pe.wait_ge(sem("vs_ready"), TT)
            for j in range(2):
                dst = bank("z", j)
                for i in range(4):
                    g = 4 * j + i
                    mm = nc.tensor.matmul(dst[:, P * i:P * i + P], wsT[:, g, :], vs1[:, :, 64 * g:64 * g + 64],
                                          start=True, stop=True)
                mm.then_inc(filled, 1)
            pe.wait_ge(sem("E_ready"), 2)
            for j in range(6):
                (qt, kt), h = ((0, 0), (1, 0), (1, 1))[j // 2], j % 2
                e = E0 if qt == 0 else E1
                turn("ET", j, [e[:, 4 * h + i, P * kt:P * kt + P] for i in range(4)])
            pe.wait_ge(freed_act, outs.emptied("ET", "act"))
            for m in range(2):
                for j in (2 * m, 2 * m + 1):
                    for h in (2 * j, 2 * j + 1):
                        pos = order.index(h)
                        dst = ps[64 * (h % 2):64 * (h % 2) + 64, 6 + m, S * (j % 2):S * (j % 2) + S]
                        nc.tensor.matmul(dst, v1[:, 0, 64 * h:64 * h + 64], ET[:, 0, pos, :], start=True, stop=False)
                        mm = nc.tensor.matmul(dst[:, P:S], v1[:, 1, 64 * h:64 * h + 64], ET[:, 1, pos, P:S],
                                              start=False, stop=True)
                mm.then_inc(sem("oT_mm"), 1)
            pe.wait_ge(sem("sgu_ready"), 1)
            for tt in range(TT):
                turn("mT", tt, quarter(u1[:, tt, :], 0))
            pe.wait_ge(sem("oT_taken"), 2)
            pe.wait_ge(freed_act, outs.emptied("mT", "act"))
            pe.wait_ge(sem("ld_wo"), 16)
            for j in range(4):
                tt, h = j // 2, j % 2
                dst = bank("wo", j)
                for k in range(KT):
                    mm = nc.tensor.matmul(dst, mixT[:, k, P * tt:P * tt + P], wo_w[:, k, 512 * h:512 * h + 512],
                                          start=(k == 0), stop=(k == KT - 1))
                mm.then_inc(filled, 1)

            def route(m, xT, w, name):
                pe.wait_ge(freed_act, outs.emptied(name, "act"))
                pe.wait_ge(sem(f"ld_wr{m + 1}"), 16)
                n = w.shape[-1]
                dst = bank(f"lg{m + 1}", 0)
                for tt in range(TT):
                    for k in range(KT):
                        mm = nc.tensor.matmul(dst[:, 64 * tt:64 * tt + n], xT[:, k, P * tt:P * tt + P], w[:, k, :],
                                              start=(k == 0), stop=(k == KT - 1))
                mm.then_inc(filled, 1)
                pe.wait_ge(sem("sel_ready"), m + 1)
                dst = bank(f"rk{m + 1}", 0)
                nc.tensor.matmul(dst[:, 0:NE], const("upper"), sel[:, 0, :], start=True, stop=True)
                nc.tensor.matmul(dst[:, NE:2 * NE], ones, sel[:, 0, :], start=True, stop=False)
                nc.tensor.matmul(dst[:, NE:2 * NE], const("upper"), sel[:, 1, :], start=False, stop=True).then_inc(filled, 1)
                rows = (M1_ROWS, M2_ROWS)[m]
                dst = bank(f"cn{m + 1}", 0)
                for q in range(2 - m):
                    for tt in range(TT):
                        mm = nc.tensor.matmul(dst[0:rows, 2 * q:2 * q + 2], row_sel(q, tt, rows), ones[:, 0:2],
                                              start=(tt == 0), stop=(tt == 1))
                mm.then_inc(filled, 1)
                pe.wait_ge(sem("flags"), m + 1)
                nc.tensor.matmul(bank(f"ps{m + 1}", 0)[0:rows, 0:2], const("upper")[0:rows, 0:rows], flag[0:rows, :],
                                 start=True, stop=True).then_inc(filled, 1)
                pe.wait_ge(sem("ovq_ready"), m + 1)
                dst = bank(f"tb{m + 1}", 0)
                left = [const(f"m{m + 1}_unit"), const(f"m{m + 1}_off"), ones[:, 0:1]]
                for i, c in enumerate(left):
                    mm = nc.tensor.matmul(dst[:, 32 * i:32 * i + 18], c[0:rows].to_broadcast([rows, P]), ovq[0:rows, :],
                                          start=True, stop=True)
                mm.then_inc(filled, 1)

            def unit(m, n, h):
                p = f"m{m + 1}_"
                pe.wait_ge(sem(p + "hot"), n + 1)
                for tt in range(TT):
                    for g in range(2):
                        mm = nc.tensor.matmul(ps[64 * g:64 * g + 64, 6, :], hot[:, tt, :], h[:, tt, HALF * g:HALF * g + HALF],
                                              start=(tt == 0), stop=(tt == TT - 1))
                mm.then_inc(sem(p + "gathered"), 1)
                pe.wait_ge(sem(p + "hotg"), 2 * n + 2)
                for tt in range(TT):
                    mm = nc.tensor.transpose(ps[:, 7, P * tt:P * tt + P], hotg[:, tt].rearrange("p d s -> p (d s)"), ident)
                mm.then_inc(sem(p + "hot_turned"), 1)
                pe.wait_ge(sem(p + "xg"), n + 1)
                for i in range(4):
                    mm = nc.tensor.transpose(ps[:, 6, P * i:P * i + P], xg[:, P * i:P * i + P], ident)
                mm.then_inc(sem(p + "xg_turned"), 1)
                if m == 1:
                    pe.wait_ge(sem("m2_bsel"), n + 1)
                    for b in range(2):
                        for g in range(2):
                            o = FF2 * g + 512 * b
                            nc.tensor.matmul(ps[64 * g:64 * g + 64, 4 + b, :], bsel, b1p[:, o:o + 512],
                                             start=True, stop=False)
                pe.wait_ge(sem(p + "xgT"), n + 1)
                if m == 0:
                    for q in range(2):
                        for k in range(KT):
                            if k % 4 == 0:
                                pe.wait_ge(sem(f"ld_gu{q}{k // 4}"), n * 16 + 16)
                            o = P * (k % 4) + 64 * (k // 4) + 32 * q
                            for g in range(2):
                                r = 64 * g + 32 * q
                                mm = nc.tensor.matmul(ps[r:r + 32, 4, 0:256], xgT[:, o:o + 32], gu_w[:, q, k, :, g, :],
                                                      start=(k == 0), stop=(k == KT - 1))
                        mm.then_inc(sem("m1_up_used"), 1)
                    pe.wait_ge(sem("m1_up_used"), 2 * n + 2)
                    pe.sem_inc(sem(p + "up_mm"), 1)
                else:
                    for k in range(KT):
                        pe.wait_ge(sem(f"ld_w1_{k}"), n * 16 + 16)
                        o = P * (k % 4) + 64 * (k // 4)
                        for b in range(2):
                            for g in range(2):
                                c = FF2 * g + 512 * b
                                mm = nc.tensor.matmul(ps[64 * g:64 * g + 64, 4 + b, :], xgT[:, o:o + 64],
                                                      w1_w[:, k, c:c + 512], start=False, stop=(k == KT - 1))
                        mm.then_inc(sem("m2_w1_used"), 1)
                    pe.wait_ge(sem("m2_w1_used"), n * KT + KT)
                    pe.sem_inc(sem(p + "up_mm"), 1)
                pe.wait_ge(sem(p + "act"), n + 1)
                for i in range(1 if m == 0 else 4):
                    mm = nc.tensor.transpose(ps[:, 4, P * i:P * i + P], m_a[:, P * i:P * i + P], ident)
                mm.then_inc(sem(p + "a_turned"), 1)
                pe.wait_ge(sem(p + "pgT"), 2 * n + 2)
                if m == 1:
                    for g in range(2):
                        nc.tensor.matmul(ps[64 * g:64 * g + 64, 7, :], bsel, b2p[:, HALF * g:HALF * g + HALF],
                                         start=True, stop=False)
                pe.wait_ge(sem(p + "aT"), n + 1)
                if m == 0:
                    for q in range(2):
                        pe.wait_ge(sem(f"ld_dn{q}"), n * 16 + 16)
                    for k in range(FF1 // P):
                        for q in range(2):
                            for g in range(2):
                                r, o = 64 * g + 32 * q, 64 * k + 32 * q
                                mm = nc.tensor.matmul(ps[r:r + 32, 7, :], m_aT[:, o:o + 32],
                                                      dn_w[:, q, k, HALF * g:HALF * g + HALF],
                                                      start=(k == 0), stop=(k == FF1 // P - 1))
                    mm.then_inc(sem(p + "dn_mm"), 1)
                else:
                    for k in range(FF2 // P):
                        pe.wait_ge(sem(f"ld_w2_{k}"), n * 16 + 16)
                        o = P * (k % 4) + 64 * (k // 4)
                        for g in range(2):
                            mm = nc.tensor.matmul(ps[64 * g:64 * g + 64, 7, :], m_aT[:, o:o + 64],
                                                  w2_w[:, k, HALF * g:HALF * g + HALF], start=False, stop=(k == FF2 // P - 1))
                        mm.then_inc(sem("m2_w2_used"), 1)
                    pe.wait_ge(sem("m2_w2_used"), n * KT + KT)
                    pe.sem_inc(sem(p + "dn_mm"), 1)
                    pe.sem_inc(sem("m2_bsel_free"), 1)
                pe.wait_ge(sem(p + "y"), n + 1)
                for g in range(2):
                    for tt in range(TT):
                        nc.tensor.matmul(ps[:, 2 * tt + g, :], pgT[g][:, P * tt:P * tt + P], m_y, start=False, stop=False,
                                         skip_group_check=True)

            def mixture(m, h):
                units = (M1_UNITS, M2_UNITS)[m]
                pe.wait_ge(sem("table_ready"), m + 1)
                if m == 1:
                    pe.wait_ge(sem("bias_parts"), 3)
                    pe.sem_inc(sem("m2_bsel_free"), 1)
                for b in range(4):
                    nc.tensor.matmul(ps[:, b, :], pgT[0][:, 0:P], h[:, 0, 0:512], start=True, stop=False,
                                     skip_group_check=True)
                with pe.Fori(0, units) as u:
                    unit(m, u, h)
                n_over = pe.value_load(table_i[m][0:1, 16:17], min_val=0, max_val=OVER)
                with pe.If(n_over > 0):
                    with pe.Fori(0, n_over) as i:
                        unit(m, i + units, h)
                nc.tensor.transpose(ps[:, 6, 0:P], ident, ident).then_inc(sem(f"m{m + 1}_scattered"), 1)

            pe.wait_ge(sem("h1_ready"), TT)
            for j in range(4):
                turn("hT", j, quarter(xs[:, j // 2, :], j % 2))
            route(0, tT, wr1, "hT")
            pe.wait_ge(sem("freed_dve"), outs.emptied("tb1", "dve"))
            mixture(0, xs)

            pe.wait_ge(sem("x1_ready"), 1)

            def spread(name, j, v, h, ctx_row):
                c = 2 * v + h
                r = 32 * (c % 4) + ctx_row
                nc.tensor.matmul(bank(name, j), ident[:, r:r + 1].to_broadcast([P, P]), modrow[:, c // 4, :],
                                 start=True, stop=True).then_inc(filled, 1)

            for j in range(8):
                spread("mb", j, (j // 2) % 2, j % 2, j // 4)
            for j in range(8):
                if j % 2 == 0:
                    pe.wait_ge(sem("hn_ready"), j // 2 + 1)
                turn("hT4", j, quarter(hn[:, j // 2, :], j % 2))
            pe.wait_ge(freed_act, outs.emptied("hT4", "act"))
            pe.wait_ge(sem("ld_win2"), 16)
            for j in range(8):
                c, tt = j // 2, j % 2
                w = min(512, PIN - 512 * c)
                dst = bank("px", j)
                for k in range(KT):
                    mm = nc.tensor.matmul(dst[:, 0:w], hT4[:, k, S + P * tt:S + P * tt + P], w_in2[:, k, 512 * c:512 * c + w],
                                          start=(k == 0), stop=(k == KT - 1))
                mm.then_inc(filled, 1)
            for j in range(6):
                c, tt = j // 2, j % 2
                o, w = ((O_KV, 160), (O_RK, 512), (O_RK + 512, 256))[c]
                dst = bank("pc", j)
                for k in range(KT):
                    mm = nc.tensor.matmul(dst[:, 0:w], hT4[:, k, P * tt:P * tt + P], w_in2[:, k, o:o + w],
                                          start=(k == 0), stop=(k == KT - 1))
                mm.then_inc(filled, 1)
            pe.wait_ge(sem("latents"), TT)
            for j in range(2):
                turn("cT", j, quarter(cn_, j))
            pe.wait_ge(freed_act, outs.emptied("cT", "act"))
            pe.wait_ge(sem("ld_wkvu"), 16)
            for j in range(8):
                nc.tensor.matmul(bank("kv", j), cT[:, j // 2, :], wkvu[:, 512 * (j % 2):512 * (j % 2) + 512],
                                 start=True, stop=True).then_inc(filled, 1)
            pe.wait_ge(sem("ld_wqu"), 16)
            for j in range(4):
                tt, h = j // 2, j % 2
                dst = bank("qu", j)
                for k in range(2):
                    mm = nc.tensor.matmul(dst[:, 0:4 * QK], cT[:, 4 + 2 * tt + k, :], wqu[:, k, 4 * QK * h:4 * QK * (h + 1)],
                                          start=(k == 0), stop=(k == 1))
                mm.then_inc(filled, 1)
            pe.wait_ge(sem("roped_r"), TT)
            for tt in range(TT):
                turn("rT", tt, [px[:, tt, O_RQ + P * i:O_RQ + P * i + P] for i in range(4)])
            turn("rT", 2, [pc[:, i % 2, 160 + P * (i // 2):160 + P * (i // 2) + P] for i in range(4)])
            pe.wait_ge(freed_act, outs.emptied("rT", "act"))
            for j in range(2 * RH):
                h, half = j // 2, j % 2
                r = slice(64 * (h % 2), 64 * (h % 2) + 64)
                dst = bank("rs", j)
                for i in range(2):
                    k = 2 * half + i
                    mm = nc.tensor.matmul(dst[:, S * i:S * i + S], rkT[r, h // 2, P * k:P * k + P], rqT[r, h // 2, :],
                                          start=True, stop=True)
                mm.then_inc(filled, 1)
            pe.wait_ge(sem("freed_dve"), outs.emptied("rs", "dve"))
            vals = [pc[:, 0, 416:928], pc[:, 1, 416:928], px[:, 0, O_RV:O_RG], px[:, 1, O_RV:O_RG]]
            for tt in range(TT):
                dst = bank("ro", tt)
                for h in range(RH):
                    for k in range(4):
                        mm = nc.tensor.matmul(dst[:, P * h:P * h + P], sd[:, h, k, P * tt:P * tt + P],
                                              vals[k][:, RDV * h:RDV * h + RDV], start=(k == 0), stop=(k == 3))
                mm.then_inc(filled, 1)
            pe.wait_ge(sem("kq_ready"), 1)
            for j in range(12):
                tile, h = j // 2, j % 2
                x = K2[:, tile] if tile < 4 else Q2[:, tile - 4]
                turn("kqT", j, [x[:, 4 * h + i, :] for i in range(4)])
            pe.wait_ge(sem("ro_ready"), TT)
            for tt in range(TT):
                turn("rmT", tt, quarter(ro[:, tt, :], 0))
            pe.wait_ge(freed_act, outs.emptied("rmT", "act"))

            def scores(h):
                for qt in range(TT):
                    nc.tensor.matmul(bank("s2", 2 * h + qt), qT2[:, h, P * qt:P * qt + P], kT2[:, h, :],
                                     start=True, stop=True).then_inc(filled, 1)

            def turn_weights(h):
                for qt in range(TT):
                    s = 2 * h + qt
                    pe.wait_ge(sem("E2_ready"), s + 1)
                    turn("eT", s, quarter(E2[:, s, :], 0))

            def head_out(h):
                pe.wait_ge(sem("freed_dve"), outs.nth[outs.at["eT"][2 * h + 1]])
                m, j = h // 4, h // 2
                dst = ps[64 * (h % 2):64 * (h % 2) + 64, 6 + m, S * (j % 2):S * (j % 2) + S]
                for k in range(4):
                    mm = nc.tensor.matmul(dst, V2[:, k, 64 * h:64 * h + 64], ET2[:, h % 4, k, :], start=(k == 0), stop=(k == 3))
                mm.then_inc(sem("oT2_head"), 1)
                if h % 4 == 3:
                    pe.wait_ge(sem("oT2_head"), h + 1)
                    pe.sem_inc(sem("oT2_mm"), 1)

            for h in range(MH + 1):
                if h < MH:
                    scores(h)
                if h:
                    turn_weights(h - 1)
                    head_out(h - 1)
            for j in range(6):
                spread("mb2", j, 2 + j // 2, j % 2, 0)
            pe.wait_ge(sem("oT2_taken"), 2)
            pe.wait_ge(sem("ld_wo2"), 16)
            for j in range(4):
                tt, h = j // 2, j % 2
                dst = bank("wo2", j)
                for k in range(KT):
                    mm = nc.tensor.matmul(dst, mixT2[:, k, P * tt:P * tt + P], wo2_w[:, k, 512 * h:512 * h + 512],
                                          start=(k == 0), stop=(k == KT - 1))
                mm.then_inc(filled, 1)
            pe.wait_ge(sem("hf_part"), 1)
            for j in range(4):
                if j == 2:
                    pe.wait_ge(sem("hf_ready"), 1)
                turn("hfT", j, quarter(hf[:, j // 2, :], j % 2))
            route(1, hfT, wr2, "hfT")
            pe.wait_ge(sem("freed_dve"), outs.emptied("tb2", "dve"))
            mixture(1, hf)
            for h in range(2):
                c = 2 * 5 + h
                nc.tensor.matmul(ps[:, 6 + h, :], ident[:, 32 * (c % 4):32 * (c % 4) + 1].to_broadcast([P, P]),
                                 modrow[:, c // 4, :], start=True, stop=True).then_inc(sem("mb5_mm"), 1)


def kernel(**inputs):
    import concourse.bacc as _bacc
    from concourse.bass_utils import run_bass_kernel_spmd as _run

    a = {k: np.asarray(v) for k, v in inputs.items()}
    const_at, (consts, early, masks), decay = host_constants()
    arrays = {
        "consts": consts, "early": early, "masks": masks, "decay": decay,
        "x": a["x"][0], "pos": a["positions"][0].reshape(TT, P).T,
        "w_in": a["w_in"][0],
        "vec1": np.concatenate([a["sgu_ln_g"][0], a["sgu_ln_b"][0], a["ln1_g"][0], a["ln1_b"][0], a["ln2_g"][0],
                                a["ln2_b"][0]]),
        "w_spatial": a["w_spatial"][0], "b_spatial": a["b_spatial"][0], "w_out": a["w_out"][0],
        "wr1": np.concatenate([a["w_group"][0], a["w_expert"][0].transpose(1, 0, 2).reshape(D, NE)], 1),
        "rb1": np.concatenate([a["b_group"][0], a["b_expert"][0].reshape(NE)]),
        "w_gate_up": a["w_gate_up"][0].reshape(NE, D, 2 * FF1), "w_down": a["w_down"][0].reshape(NE, FF1, D),
        "cc": np.concatenate([a["c_2"][0].reshape(KT, P), a["c_ctx_2"].reshape(KT, P)], 0),
        "ctx": a["ctx_2"][0], "w_ada_2": a["w_ada_2"][0], "b_ada": a["b_ada_2"][0].reshape(3, 4, 512),
        "w_in_2": a["w_in_2"][0],
        "vec2": np.concatenate([a["g_attn_2"][0], a["g_ffn_2"][0], a["g_q_lora_2"][0], a["g_kv_lora_2"][0],
                                a["g_q_head_2"][0], a["g_k_head_2"][0], a["g_ret_out_2"][0]]),
        "w_q_up_2": a["w_q_up_2"][0], "w_kv_up_2": a["w_kv_up_2"][0],
        "decay_logit": a["ret_decay_logit_2"][0].reshape(2 * RH), "w_out_2": a["w_out_2"][0],
        "wr2": a["w_router_2"][0], "rb2": a["b_router_2"][0],
        "w_mlp1_2": a["w_mlp1_2"][0], "b_mlp1_2": a["b_mlp1_2"][0], "w_mlp2_2": a["w_mlp2_2"][0],
        "b_mlp2_2": a["b_mlp2_2"][0],
    }
    arrays = {f"in_{k}": np.ascontiguousarray(v) for k, v in arrays.items()}
    nc = _bacc.Bacc("TRN2", target_bir_lowering=False, num_devices=1)
    t = {k[3:]: nc.dram_tensor(k, v.shape, mybir.dt.from_np(v.dtype), kind="ExternalInput").ap() for k, v in arrays.items()}
    out = nc.dram_tensor("out_x", (S, D), F32, kind="ExternalOutput").ap()
    build(nc, t, out, const_at)
    r = _run(nc, [arrays], core_ids=[0])
    return r.results[0]["out_x"].reshape(1, S, D)
```

```python
from contextlib import ExitStack

import numpy as np

import concourse.bass as bass
from concourse import mybir

ALU = mybir.AluOpType
ACT = mybir.ActivationFunctionType
AX = mybir.AxisListType.X
F32, BF16, I32, U32 = mybir.dt.float32, mybir.dt.bfloat16, mybir.dt.int32, mybir.dt.uint32

P = 128
S, D = 256, 1024
TT, KT = S // P, D // P
HALF = D // 2
H1, DH1, AW = 8, 64, 512
SG, SGW = 8, 512
ROT1 = 8
NE = 32
FF1 = 256
NGRP, EPG = 4, 8
ALPHA = 2.0 ** 0.25
LN_EPS, RMS_EPS = 1e-5, 1e-6
NEG = -1e30
MH, NOPE, PE_W, MV = 8, 64, 32, 64
QK = NOPE + PE_W
QL, KVL = 256, 128
RH, RDK, RDV = 4, 64, 128
O_KV, O_PE, O_RQ = QL, QL + KVL, QL + KVL + PE_W
O_RK = O_RQ + RH * RDK
O_RV = O_RK + RH * RDK
O_RG = O_RV + RH * RDV
PIN = O_RG + RH * RDV
PIECES = (O_RG - O_RK) // P
CHUNKS = (0, 1, 2, 4, 3)
PX = ((0, O_RQ), (O_RQ, O_RV - O_RQ), (O_RV, RH * RDV), (O_RG, RH * RDV))
CW = O_RQ - O_KV + O_RG - O_RK
FF2 = 1024
LIMIT, SWA = 7.0, 1.702
SLOTS = 64
GROUPS, CAP = (NE // 2, NE), (32, 64)
BLOCKS = tuple(S // c for c in CAP)
TABLE = 52
SMALL = 560
BANKS = 6


def host_constants():
    f = np.float32
    p = np.arange(P)
    c = {}
    c["ident"] = np.eye(P)
    c["upper"] = p[:, None] < p[None, :]
    c["ones"] = np.ones((P, P))
    c["tri"] = p[:, None] <= p[None, :]
    for t in range(TT):
        dist = (t * P + p)[:, None] - np.arange((t + 1) * P)[None, :]
        causal = dist >= 0
        count = causal * ((dist <= 128) * 1 + (dist % 4 == 0) + (dist % 16 == 0))
        c[f"cnt{t}"] = count
        c[f"neg{t}"] = np.where(count > 0, 0.0, NEG)
    c["iota32"] = np.tile(np.arange(32), (P, 1))
    c["iota64"] = np.tile(np.arange(64), (P, 1))
    for m in range(2):
        block = p % BLOCKS[m]
        c[f"off{m}"] = (CAP[m] * block)[:, None]
        c[f"more{m}"] = np.where(block > 0, CAP[m] * block, -1)[:, None]
        c[f"group{m}"] = (p // BLOCKS[m])[:, None]
        c[f"first{m}"] = p[:, None] == BLOCKS[m] * np.arange(NE)[None, :]
    c["eye3"] = (p[:, None] % 32 == np.arange(32)[None, :]) & (p[:, None] < 96)
    c["inv8"] = np.tile(500000.0 ** (-np.arange(8) / 8.0), (P, 1))
    pos = np.arange(S)
    grid = np.stack([pos // 64, pos % 64], -1).astype(f)
    for name, dim in (("M", PE_W), ("R", RDK)):
        nf = dim // 4
        inv = (10000.0 ** (-np.arange(nf) / nf)).astype(f)
        ang = (grid[:, :, None] * inv).astype(f)
        ang = np.broadcast_to(ang[:, :, None, :], (S, 2, 2, nf)).astype(np.float64)
        sign = np.array([-1.0, 1.0])[None, None, :, None]
        c["cos" + name] = np.cos(ang).reshape(TT, P, dim).transpose(1, 0, 2).reshape(P, -1)
        c["sin" + name] = (np.sin(ang) * sign).reshape(TT, P, dim).transpose(1, 0, 2).reshape(P, -1)
    early = ["tri", "cosM", "sinM", "cosR", "sinR"]
    masks = ["cnt0", "neg0", "cnt1", "neg1"]
    groups = [[k for k in c if k not in early + masks], early, masks]
    at, arrays = {}, []
    for i, names in enumerate(groups):
        w = 0
        for k in names:
            at[k] = (i, w, c[k].shape[1])
            w += c[k].shape[1]
        arrays.append(np.ascontiguousarray(np.concatenate([np.asarray(c[k], f) for k in names], 1)))
    kt, i = np.arange(4)[None, :, None], pos[None, None, :]
    j = kt * P + p[:, None, None] - S
    ahead = np.where(j < 0, i - j, np.maximum(i - j, 0))
    behind = np.where(j < 0, 2 * S + j - i, np.maximum(j - i, 0))
    seen_f, seen_b = (i >= j) * 1.0, (j >= i) * 1.0
    decay = np.concatenate([ahead.reshape(P, -1), behind.reshape(P, -1),
                            seen_f[:, 2:].reshape(P, -1), seen_b[:, 2:].reshape(P, -1)], 1).astype(f)
    return at, arrays, decay


class Outputs:

    def __init__(self, plan):
        self.at, self.by, self.nth = {}, [], []
        done = {"act": 0, "dve": 0}
        for name, count, engine in plan:
            first = len(self.by)
            for _ in range(count):
                done[engine] += 1
                self.by.append(engine)
                self.nth.append(done[engine])
            self.at.setdefault(name, []).extend(range(first, first + count))

    def bank(self, name, j):
        return self.at[name][j] % BANKS

    def filled(self, name, j):
        return self.at[name][j] + 1

    def before(self, name, j):
        n = self.at[name][j] - BANKS
        return (self.by[n], self.nth[n]) if n >= 0 else None

    def emptied(self, name, engine):
        last = self.at[name][-1]
        return max([self.nth[n] for n in range(last + 1) if self.by[n] == engine], default=0)


PLAN = (
    [("xT", 4, "act")]
    + [("proj", 5, "act"), ("qkT", 4, "act"), ("proj", 1, "act"), ("ada", 1, "dve"), ("sc", 6, "dve"),
       ("wsT", 2, "dve"), ("bsT", 1, "dve"), ("proj", 2, "act"), ("ada", 1, "dve"), ("proj", 2, "act"),
       ("ada", 1, "dve")]
    + [("ET", 6, "act"), ("mbc", 4, "act"), ("z", 2, "dve"), ("mT", 2, "act"), ("wo", 4, "dve"), ("hTc", 4, "act"),
       ("hT", 4, "act")]
    + [("lg1", 1, "dve"), ("rk1", 1, "dve"), ("cn1", 1, "dve"), ("ps1", 1, "dve"), ("tb1", 1, "dve")]
    + [("mb", 4, "act"), ("pc", 2, "act"), ("hT4", 4, "act"), ("px", 2, "act"), ("cT", 1, "act"), ("px", 1, "act"),
       ("cT", 2, "act"), ("kv", 8, "act"), ("qu", 4, "act"), ("px", 3, "act"), ("rT", 3, "act"), ("px", 2, "act")]
    + [("rs", 8, "dve"), ("kqT", 12, "act"), ("ro", 2, "act")]
    + [("s2", 2, "act"), ("mb2", 6, "act"), ("s2", 2, "act")] + [("s2", 2, "act"), ("eT", 2, "dve")] * (MH - 2)
    + [("eT", 2, "dve"), ("rmT", 2, "act"), ("eT", 2, "dve")]
    + [("wo2", 4, "dve"), ("hfT", 4, "act")]
    + [("lg2", 1, "dve"), ("rk2", 1, "dve"), ("cn2", 1, "dve"), ("ps2", 1, "dve"), ("tb2", 1, "dve")]
)


def build(nc, t, out, const_at):
    ctx = ExitStack()
    with ctx:
        def sb(name, shape, dt=F32):
            return ctx.enter_context(nc.sbuf_tensor(name, shape, dt))

        sems = {}

        def sem(name):
            if name not in sems:
                sems[name] = ctx.enter_context(nc.semaphore(name))
            return sems[name]

        outs = Outputs(PLAN)
        ps = ctx.enter_context(nc.psum_tensor("ps", [P, 8, 512], F32))

        wbig = sb("wbig", [P, 24576])
        wfront = sb("wfront", [P, 16384])
        xs = sb("xs", [P, TT, D])
        tT = sb("tT", [P, KT, S])
        act_ = sb("act_", [P, 5120])
        consts = sb("consts", [P, t["consts"].shape[1]])
        modrow = sb("modrow", [P, 3, 512])
        small = sb("small", [P, SMALL])
        pos_i = sb("pos_i", [P, TT], I32)
        idx_u = sb("idx_u", [P, TT, 8], U32)
        table = sb("table", [P, TABLE + 1 + NE], I32)

        def const(name):
            i, o, w = const_at[name]
            return (consts[:, :], wbig[:, 23744:24256], wbig[:, 3072:3840])[i][:, o:o + w]

        ident = const("ident")
        ones = const("ones")

        free_small = [0]

        def cols(w):
            o = free_small[0]
            free_small[0] += w
            assert free_small[0] <= SMALL, free_small
            return small[:, o:o + w]

        def three(ap, n):
            return ap.rearrange("p (t c) -> p t c", t=n)

        w_in = three(wbig[:, 0:5 * 4096], 5)
        sgu_v = wbig[:, 20480:21504]
        w_sp = wbig[:, 21504:22528]
        b_sp = wbig[0:SG, 22528:22656]
        ln1_v = wbig[:, 4096:6144]
        ln2_v = wbig[:, 14336:16384]
        cx = three(wbig[:, 16384:18432], TT)
        mbc = wbig[:, 18432:20480].rearrange("p (v c) -> p v c", v=2)
        g_at1 = wbig[:, 7168:8192]
        hTc = wbig[:, 12288:14336].rearrange("p (k q) -> p k q", k=KT)
        ada = wfront[:, :].rearrange("p (k c) -> p k c", k=KT)
        wo_w = wfront[:, 0:8192].rearrange("p (k c) -> p k c", k=KT)
        qkT = wbig[:, 0:2048].rearrange("p (k q) -> p k q", k=KT)
        E0 = wbig[:, 2048:3072].rearrange("p (h k) -> p h k", h=H1)
        E1 = wbig[:, 4096:6144].rearrange("p (h k) -> p h k", h=H1)
        ET = wbig[:, 8192:12288].rearrange("p (k h q) -> p k h q", k=TT, h=H1)
        qk = three(act_[:, 0:2048], TT)
        mixT = act_[:, 0:2048].rearrange("p (k q) -> p k q", k=KT)
        v1 = three(act_[:, 2048:3072], TT)
        u1 = three(act_[:, 3072:4096], TT)
        vs1 = three(act_[:, 4096:5120], TT)
        wsT = wbig[:, 6144:7168].rearrange("p (g t) -> p g t", g=SG)
        wr1 = wbig[:, 22656:22944].rearrange("p (k c) -> p k c", k=KT)
        wr2 = wbig[:, 23104:23360].rearrange("p (k c) -> p k c", k=KT)
        ccT = wbig[:, 23360:23616].rearrange("p (k c) -> p k c", k=KT)
        cc = wbig[0:16, 23616:23744]
        rb1 = cols(NGRP + NE)
        rb2 = cols(NE)

        gu_w = wbig[:, 0:8192].rearrange("p (q k h c f) -> p q k h c f", q=2, k=KT, h=2, c=2)
        dn_w = wbig[:, 8192:12288].rearrange("p (q k f) -> p q k f", q=2, k=FF1 // P)
        w1_w = wbig[:, 0:16384].rearrange("p (k f) -> p k f", k=KT)
        w2_w = wbig[:, 16384:24576].rearrange("p (k f) -> p k f", k=FF2 // P)
        m_at = [0]

        def mbuf(w):
            o = m_at[0]
            m_at[0] += w
            assert m_at[0] <= 5120
            return act_[:, o:o + w]

        xg, xgT, m_t, m_l, m_s, m_a, m_aT, m_y = (mbuf(512) for _ in range(8))
        pgT = [mbuf(256), mbuf(256)]
        hot = mbuf(TT * SLOTS).rearrange("p (t s) -> p t s", t=TT)
        hotg = mbuf(TT * 2 * SLOTS).rearrange("p (t d s) -> p t d s", t=TT, d=2)
        keyc, gatec = mbuf(4), mbuf(4)

        def row_sel(q, tt):
            return act_[:, 256 * q + P * tt:256 * q + P * tt + P]

        bsel = [wfront[0:96, 1536 + 32 * i:1568 + 32 * i].bitcast(BF16) for i in range(2)]
        b1p = wfront[0:96, 0:FF2].bitcast(BF16)
        b2p = wfront[0:96, FF2:FF2 + HALF].bitcast(BF16)
        braw = wfront[0:96, 1600:1600 + 3072]
        bpart = wfront[0:96, 4672:4672 + 1536].bitcast(BF16)
        gated = wfront[:, 6208:8192]

        mb = act_[:, 2048:4096].rearrange("p (v c) -> p v c", v=2)
        hn = three(act_[:, 0:2048], TT)
        sq = act_[:, 4096:5120]
        px = three(wbig[:, 0:TT * PIN], TT)
        pc = three(tT[:, :, :].rearrange("p k q -> p (k q)")[:, 0:TT * CW], TT)
        K2 = wbig[:, 3904:3904 + 4 * MH * QK].rearrange("p (t h e) -> p t h e", t=4, h=MH)
        kT2 = wbig[0:QK, 12288:16384].rearrange("p (h k) -> p h k", h=MH)
        qT2 = wbig[0:QK, 10240:12288].rearrange("p (h q) -> p h q", h=MH)
        Q2 = act_[:, 0:TT * MH * QK].rearrange("p (t h e) -> p t h e", t=TT, h=MH)
        V2 = act_[:, 1536:3584].rearrange("p (t c) -> p t c", t=4)
        cn_ = act_[:, 3584:4608]
        cT = wbig[:, 16384:17408].rearrange("p (b q) -> p b q", b=8)
        vec2_at = 16384
        g_at = wbig[:, vec2_at:vec2_at + 1024]
        g_ff = wbig[:, vec2_at + 1024:vec2_at + 2048]
        g_ql = wbig[:, vec2_at + 2048:vec2_at + 2304]
        g_kvl = wbig[:, vec2_at + 2304:vec2_at + 2432]
        g_qh = wbig[:, vec2_at + 2432:vec2_at + 2528]
        g_kh = wbig[:, vec2_at + 2528:vec2_at + 2624]
        g_ro = wbig[:, vec2_at + 2624:vec2_at + 3136]
        VEC2 = 3136
        wqu = wbig[:, 19520:21056].rearrange("p (k c) -> p k c", k=2)
        wkvu = wbig[:, 21056:22080]
        mb2 = wbig[:, 22080:23104]
        mb3, mb4 = act_[:, 0:1024], act_[:, 3584:4608]
        w_in2 = wfront[:, 0:KT * PIN].rearrange("p (k c) -> p k c", k=KT)
        dext = [wbig[:, 10240 + 1024 * h + (h // 2) * 2048:][:, 0:1024].rearrange("p (k q) -> p k q", k=4) for h in range(RH)]
        decay = wbig[:, 6976:10048]
        dtmp = wbig[:, 0:4096].rearrange("p (h q) -> p h q", h=RH)
        E2 = wfront[:, 0:8192].rearrange("p (s k) -> p s k", s=2 * MH)
        wo2_w = wfront[:, 8192:16384].rearrange("p (k c) -> p k c", k=KT)
        ET2 = wbig[:, 0:4096].rearrange("p (s k q) -> p s k q", s=4, k=4)
        sd = wfront[:, 0:4096].rearrange("p (h k q) -> p h k q", h=RH, k=4)
        rT = act_[:, 3584:5120]
        rqT = rT[:, 0:512].rearrange("p (b q) -> p b q", b=2)
        rkT = rT[:, 512:1536].rearrange("p (b k) -> p b k", b=2)
        ro = wbig[:, 6976:8000].rearrange("p (t c) -> p t c", t=TT)
        mixT2 = wbig[:, 8000:10048].rearrange("p (k q) -> p k q", k=KT)
        scr = wbig[:, 6976:10048]
        scr_l = wfront[:, 15616:16384]
        hf = tT[:, :, :].rearrange("p k q -> p (k q)").rearrange("p (t c) -> p t c", t=TT)
        hfT = act_[:, 1536:3584].rearrange("p (k q) -> p k q", k=KT)
        lgam = cols(2 * RH)
        lgt = cols(4 * 2 * RH)
        rg = wbig[:, 9024:10048].rearrange("p (t c) -> p t c", t=TT)
        rsq = lgt[:, 8:8 + TT * RH]
        scr_p = scr[:, 1536:2560]

        stats, mv = cols(12), cols(2 * TT)
        rstd = cols(64)
        ssum = cols(64)
        cs1 = cols(TT * 2 * ROT1).rearrange("p (f t e) -> p f t e", f=2, t=TT)
        rot = cols(5 * TT * ROT1)
        mx, mneg = cols(16), cols(16)
        lg = cols(TT * 36).rearrange("p (t c) -> p t c", t=TT)
        g8 = cols(TT * 8).rearrange("p (t c) -> p t c", t=TT)
        top8 = cols(TT * 8).rearrange("p (t c) -> p t c", t=TT)
        idxf = cols(TT * 8).rearrange("p (t c) -> p t c", t=TT)
        topw = cols(TT * 4).rearrange("p (t c) -> p t c", t=TT)
        psel = cols(TT)
        goh = cols(TT * NGRP).rearrange("p (t c) -> p t c", t=TT)
        spare = wfront[:, 15616:16384]
        sel, gate, key, oh = (spare[:, 64 * i:64 * i + 64].rearrange("p (t c) -> p t c", t=TT) for i in range(4))
        place_of = spare[:, 256:256 + TABLE + 2]
        off = spare[:, 320:320 + TABLE]
        flag = cols(2)
        pos_f = cols(TT)

        d_win = t["w_in"].rearrange("(k p) (c f) -> c p k f", p=P, f=512)
        d_ada = t["w_ada_2"].rearrange("(k p) (r f) -> r p k f", p=P, f=4 * 512)
        d_gu = t["w_gate_up"].rearrange("e (k p) f -> e p k f", p=P)
        d_dn = t["w_down"].rearrange("e (k p) f -> e p k f", p=P)
        d_w1 = t["w_mlp1_2"].rearrange("e (k p) f -> e k p f", p=P)
        d_w2 = t["w_mlp2_2"].rearrange("e (k p) f -> e k p f", p=P)

        def row(ap, n=P):
            return ap.partition_broadcast(n)

        block = ctx.enter_context(nc.Block())

        @block.sync
        def _(sp):
            def load(dst, src, name):
                sp.dma_start(dst, src).then_inc(sem(name), 16)

            load(consts[:, :], t["consts"], "ld_consts")
            load(wbig[:, 23744:24256], t["early"], "ld_early")
            load(xs[:, :, :], t["x"].rearrange("(t p) d -> p t d", p=P), "ld_x")
            load(cc, t["cc"], "ld_cc")

            def load_w_in(c):
                load(w_in[:, c, :].rearrange("p (k f) -> p k f", k=KT), d_win[c], f"ld_win{c}")

            def load_ada(i):
                k = KT // 2 * (i % 2)
                load(ada[:, k:k + KT // 2, :], d_ada[i // 2, :, k:k + KT // 2], f"ld_ada{i % 2}")

            for c in CHUNKS[:2]:
                load_w_in(c)
            load(pos_i[:, :], t["pos"], "ld_pos")
            for c in CHUNKS[2:]:
                load_w_in(c)
            sp.wait_ge(sem("filled"), outs.filled("proj", 1))
            load(wbig[:, 3072:3840], t["masks"], "ld_masks")
            load_ada(0)
            load_ada(1)
            load(w_sp.rearrange("p (g s) -> p g s", g=SG), t["w_spatial"].rearrange("g t s -> t g s"), "ld_spatial")
            load(b_sp, t["b_spatial"], "ld_spatial")
            sp.wait_ge(sem("modrow_zeroed"), 1)
            for g in range(4):
                load(modrow[32 * g:32 * g + 2, :, :], row(t["b_ada"][:, g, :], 2), "ld_bada")
            sp.wait_ge(sem("ada_used"), 1)
            load_ada(2)
            load(sgu_v, row(t["vec1"][0:1024]), "ld_small")
            load(rb1, row(t["rb1"]), "ld_small")
            load(rb2, row(t["rb2"]), "ld_small")
            load(wr1, t["wr1"].rearrange("(k p) c -> p k c", p=P), "ld_small")
            load(wr2, t["wr2"].rearrange("(k p) c -> p k c", p=P), "ld_small")
            load(lgt[:, 0:8], row(t["decay_logit"]), "ld_small")
            sp.wait_ge(sem("filled"), outs.filled("ada", 0))
            load_ada(3)
            sp.wait_ge(sem("ada_used"), 2)
            load_ada(4)
            sp.wait_ge(sem("filled"), outs.filled("ada", 1))
            load_ada(5)
            sp.wait_ge(sem("filled"), outs.filled("proj", 7))
            load(cx, t["ctx"].rearrange("(t p) d -> p t d", p=P), "ld_ctx")
            load(g_at1, row(t["vec2"][0:D]), "ld_gat1")
            sp.wait_ge(sem("ada_used"), 3)
            load(wo_w, t["w_out"].rearrange("(k p) c -> p k c", p=P), "ld_wo")
            sp.wait_ge(sem("filled"), outs.filled("proj", 9))
            load(ln2_v, row(t["vec1"][3072:5120]), "ld_ln2")
            sp.wait_ge(sem("filled"), outs.filled("ET", 5))
            load(ln1_v, row(t["vec1"][1024:3072]), "ld_ln1")

            def load_pair(u):
                for q in range(2):
                    e = u * 2 + q
                    for h in range(2):
                        yield (gu_w[:, q, 4 * h:4 * h + 4].rearrange("p k h c f -> p k (h c f)"),
                               d_gu[bass.ds(e, 1), :, 4 * h:4 * h + 4].rearrange("a p k f -> (a p) k f"),
                               f"ld_gu{q}{h}")
                for q in range(2):
                    e = u * 2 + q
                    yield (dn_w[:, q], d_dn[bass.ds(e, 1)].rearrange("a p k f -> (a p) k f"), f"ld_dn{q}")

            first = list(load_pair(0))
            for dst, src, name in first[0:2]:
                load(dst, src, name)
            sp.wait_ge(sem("oT_mm"), 2)
            for dst, src, name in first[4:6]:
                load(dst, src, name)
            sp.wait_ge(sem("filled"), outs.filled("wo", 3))
            load(w_in2, t["w_in_2"].rearrange("(k p) c -> p k c", p=P), "ld_w_in_2")
            sp.wait_ge(sem("h1_ready"), TT)
            for dst, src, name in first[2:4]:
                load(dst, src, name)
            sp.wait_ge(sem("filled"), outs.filled("hTc", 3))
            load(wbig[:, vec2_at:vec2_at + VEC2], row(t["vec2"]), "ld_latent")
            load(wqu, t["w_q_up_2"].rearrange("(k p) c -> p k c", p=P), "ld_latent")
            load(wkvu, t["w_kv_up_2"], "ld_latent")

            def unit_before(g):
                return sp.value_load(table[0:1, bass.ds(g + TABLE + 1, 1)], min_val=0, max_val=TABLE - 4)

            sp.wait_ge(sem("table_ready"), 1)
            with sp.Fori(1, GROUPS[0]) as g:
                n = unit_before(g)
                for i, (dst, src, name) in enumerate(load_pair(g)):
                    if i == 0:
                        sp.wait_ge(sem("m1_up_used"), n * 2 + 1)
                    elif i == 2:
                        sp.wait_ge(sem("m1_up_used"), n * 2 + 2)
                    elif i == 4:
                        sp.wait_ge(sem("m1_dn_mm"), n + 1)
                    load(dst, src, name)
            sp.wait_ge(sem("m1_scattered"), 1)
            load(decay, t["decay"], "ld_decay")
            sp.wait_ge(sem("filled"), outs.filled("px", 7))
            load(wo2_w, t["w_out_2"].rearrange("(k p) c -> p k c", p=P), "ld_wo2")

            def load_expert(e):
                for k in range(KT):
                    yield (w1_w[:, k, :], d_w1[bass.ds(e, 1), k].rearrange("a p f -> (a p) f"), f"ld_w1_{k}")
                for k in range(FF2 // P):
                    yield (w2_w[:, k, :], d_w2[bass.ds(e, 1), k].rearrange("a p f -> (a p) f"), f"ld_w2_{k}")

            chunks = list(load_expert(0))

            def load_first(*which):
                for i in which:
                    dst, src, name = chunks[i]
                    load(dst, src, name)

            sp.wait_ge(sem("filled"), outs.filled("kqT", 11))
            load_first(2, 8, 12, 15)
            sp.wait_ge(sem("ro_ready"), TT)
            load_first(10, 11)
            sp.wait_ge(sem("filled"), outs.filled("s2", 2 * MH - 1))
            load_first(5, 6, 7)
            sp.wait_ge(sem("filled"), outs.filled("eT", 2 * MH - 1))
            for i in range(3):
                load(braw[32 * i:32 * i + 32, 0:2 * FF2], t["b_mlp1_2"], "ld_b")
                load(braw[32 * i:32 * i + 32, 2 * FF2:], t["b_mlp2_2"], "ld_b")
            sp.wait_ge(sem("oT2_mm"), 2)
            load_first(0, 1)
            sp.wait_ge(sem("filled"), outs.filled("wo2", 3))
            load_first(3, 4)
            sp.wait_ge(sem("wo2_added"), 4)
            load_first(13)
            sp.wait_ge(sem("hf_ready"), 1)
            load_first(9)
            sp.wait_ge(sem("filled"), outs.filled("lg2", 0))
            load_first(14)

            sp.wait_ge(sem("table_ready"), 2)
            with sp.Fori(1, GROUPS[1]) as e:
                n = unit_before(e)
                for i, (dst, src, name) in enumerate(load_expert(e)):
                    sp.wait_ge(sem("m2_w1_used" if i < KT else "m2_w2_used"), n * KT + (i % KT + 1))
                    load(dst, src, name)
            sp.wait_ge(sem("y_ready"), 1)
            sp.dma_start(out.rearrange("(t p) d -> p t d", p=P), xs[:, :, :]).then_inc(sem("stored"), 16)
            sp.wait_ge(sem("stored"), 16)

        @block.scalar
        def _(act):
            freed = sem("freed_act")
            emptied = [0]
            steps = [0]

            def step(ins):
                steps[0] += 1
                ins.then_inc(sem("act_step"), 1)
                act.wait_ge(sem("act_step"), steps[0])

            def empty(name, j, dst, view, func=ACT.Copy, **kw):
                act.wait_ge(sem("filled"), outs.filled(name, j))
                src = view(ps[:, outs.bank(name, j), :])
                emptied[0] += 1
                assert emptied[0] == outs.nth[outs.at[name][j]]
                return nc.scalar.activation(dst, src, func, **kw).then_inc(freed, 1)

            roots = [0]

            def root(n):
                roots[0] += 1
                act.wait_ge(sem("var_ready"), roots[0])
                nc.scalar.activation(rstd[:, 0:n], rstd[:, 0:n], ACT.Sqrt).then_inc(sem("root_ready"), 1)

            def four(ap):
                return ap.rearrange("p (b q) -> p b q", b=4)

            def same(ap):
                return ap

            act.wait_ge(sem("ld_cc"), 16)
            nc.scalar.activation(cc, cc, ACT.Silu).then_inc(sem("cc_ready"), 1)
            for j in range(4):
                tt, h = j // 2, j % 2
                empty("xT", j, tT[:, 4 * h:4 * h + 4, P * tt:P * tt + P], four)
            act.wait_ge(sem("angles"), 1)
            nc.scalar.activation(cs1[:, :, :, :].rearrange("p f t e -> p (f t e)"), rot[:, 0:2 * TT * ROT1],
                                 ACT.Sin).then_inc(sem("sincos"), 1)

            def proj_in(j):
                c, tt = CHUNKS[j // 2], j % 2
                if c < 2:
                    dst, f = qk[:, tt, 512 * c:512 * c + 512], ACT.Copy
                elif c == 2:
                    dst, f = v1[:, tt, :], ACT.Copy
                else:
                    dst, f = (u1 if c == 3 else vs1)[:, tt, :], ACT.Gelu
                empty("proj", j, dst, same, f)

            for j in range(5):
                proj_in(j)
            for j in range(4):
                tt, h = j // 2, j % 2
                empty("qkT", j, qkT[:, 4 * h:4 * h + 4, P * tt:P * tt + P], four)
            proj_in(5)
            proj_in(6)
            act.wait_ge(sem("sc_shift"), 2)
            nc.scalar.activation(E0, E0, ACT.Exp).then_inc(sem("sc_exp"), 1)
            nc.scalar.activation(E1, E1, ACT.Exp).then_inc(sem("sc_exp"), 1)
            proj_in(7)
            root(TT)
            proj_in(8)
            proj_in(9)
            for j in range(6):
                (qt, kt), h = ((0, 0), (1, 0), (1, 1))[j // 2], j % 2
                empty("ET", j, ET[:, kt, 4 * h:4 * h + 4, P * qt:P * qt + P], four)
            for j in range(4):
                empty("mbc", j, mbc[:, j // 2, 512 * (j % 2):512 * (j % 2) + 512], same)
            for m in range(2):
                act.wait_ge(sem("oT_mm"), m + 1)
                nc.scalar.activation(mixT[:, 2 * m:2 * m + 2, :], ps[:, 6 + m, :].rearrange("p (b q) -> p b q", b=2),
                                     ACT.Copy).then_inc(sem("oT_taken"), 1)
            for tt in range(TT):
                empty("mT", tt, mixT[:, 4:8, P * tt:P * tt + P], four)
            root(TT)
            act.wait_ge(sem("lg_neg"), 1)
            nc.scalar.activation(lgt[:, 8:16], lgt[:, 8:16], ACT.Exp).then_inc(sem("lg_exp"), 1)
            act.wait_ge(sem("lg_neg"), 2)
            nc.scalar.activation(lgt[:, 24:32], lgt[:, 16:24], ACT.Ln).then_inc(sem("lg_ln"), 1)
            for j in range(4):
                tt, h = j // 2, j % 2
                empty("hTc", j, hTc[:, 4 * h:4 * h + 4, P * tt:P * tt + P], four)
            root(TT)
            for j in range(4):
                tt, h = j // 2, j % 2
                empty("hT", j, tT[:, 4 * h:4 * h + 4, P * tt:P * tt + P], four)

            def route_exps(m):
                if m == 0:
                    act.wait_ge(sem("grp_shift"), 1)
                    nc.scalar.activation(g8[:, :, 0:NGRP], g8[:, :, 0:NGRP], ACT.Exp).then_inc(sem("grp_exp"), 1)
                k = 2 if m == 0 else 4
                act.wait_ge(sem("top_shift"), m + 1)
                nc.scalar.activation(topw[:, :, 0:k], topw[:, :, 0:k], ACT.Exp).then_inc(sem("top_exp"), 1)

            def mixture(m):
                p = f"m{m + 1}_"

                def tokens_in(n):
                    act.wait_ge(sem(p + "gathered"), n + 1)
                    nc.scalar.activation(xg, ps[:, 6, :], ACT.Copy).then_inc(sem(p + "xg"), 1)

                def turned_in(n):
                    act.wait_ge(sem(p + "xg_turned"), n + 1)
                    nc.scalar.activation(xgT, ps[:, 6, :], ACT.Copy).then_inc(sem(p + "xgT"), 1)

                act.wait_ge(sem("table_ready"), m + 1)
                units = act.value_load(table[0:1, TABLE:TABLE + 1], min_val=GROUPS[m], max_val=TABLE - 4)
                tokens_in(0)
                turned_in(0)

                def unit(n):
                    if m == 0:
                        act.wait_ge(sem(p + "up_mm"), n + 1)
                        nc.scalar.activation(m_s[:, 0:P], ps[:, 4, 0:P], ACT.Silu).then_inc(sem(p + "sig"), 1)
                    else:
                        act.wait_ge(sem(p + "glu"), n + 1)
                        nc.scalar.activation(m_s, m_t, ACT.Sigmoid, scale=SWA).then_inc(sem(p + "sig"), 1)
                    tokens_in(n + 1)
                    w = P if m == 0 else 512
                    act.wait_ge(sem(p + "a_turned"), n + 1)
                    nc.scalar.activation(m_aT[:, 0:w], ps[:, 4, 0:w], ACT.Copy).then_inc(sem(p + "aT"), 1)
                    turned_in(n + 1)
                    act.wait_ge(sem(p + "dn_mm"), n + 1)
                    nc.scalar.activation(m_y, ps[:, 7, :], ACT.Copy).then_inc(sem(p + "y"), 1)

                if m == 0:
                    for tt in range(TT):
                        with act.Fori(PIECES * tt, PIECES * tt + PIECES) as n:
                            unit(n)
                            act.wait_ge(sem("pc_mm"), n + 1)
                            nc.scalar.activation(pc[:, tt, bass.ds((n - PIECES * tt) * P + 160, P)], ps[:, 4, 0:P], ACT.Copy)\
                                .then_inc(sem("pc_taken"), 1)
                with act.Fori(0 if m else TT * PIECES, units) as n:
                    unit(n)

            route_exps(0)
            mixture(0)

            for j in range(4):
                empty("mb", j, mb[:, j // 2, 512 * (j % 2):512 * (j % 2) + 512], same)
            root(TT)

            def decay_exps(h):
                nc.scalar.activation(dext[h].rearrange("p k q -> p (k q)"), decay[:, 0:1024], ACT.Exp,
                                     scale=lgam[:, h:h + 1]).then_inc(sem("dext_exp"), 1)
                nc.scalar.activation(dtmp[:, h, :], decay[:, 1024:2048], ACT.Exp,
                                     scale=lgam[:, RH + h:RH + h + 1]).then_inc(sem("dext_exp"), 1)

            act.wait_ge(sem("ld_decay"), 16)
            decay_exps(0)
            decay_exps(1)
            for tt in range(TT):
                empty("pc", tt, pc[:, tt, 0:160], lambda a: a[:, 0:160])
            root(TT)
            act.wait_ge(sem("x1_ready"), 1)
            decay_exps(2)
            decay_exps(3)
            for j in range(4):
                tt, h = j // 2, j % 2
                empty("hT4", j, hTc[:, 4 * h:4 * h + 4, P * tt:P * tt + P], four)

            def px_in(j):
                (o, w), tt = PX[j // 2], j % 2
                if o == O_RG:
                    empty("px", j, rg[:, tt, :], lambda a: a[:, 0:w], ACT.Silu)
                else:
                    empty("px", j, px[:, tt, o:o + w], lambda a: a[:, 0:w])

            def latents_in(j):
                a, b = ((0, 2), (2, 4), (4, 8))[j]
                empty("cT", j, cT[:, a:b, :], lambda p: four(p)[:, 0:b - a, :])

            def kv_in(j):
                tile, h = j // 2, j % 2
                act.wait_ge(sem("filled"), outs.filled("kv", j))
                src = ps[:, outs.bank("kv", j), :].rearrange("p (h e) -> p h e", h=4)
                step(nc.scalar.activation(K2[:, tile, 4 * h:4 * h + 4, 0:NOPE], src[:, :, 0:NOPE], ACT.Copy))
                empty("kv", j, V2[:, tile, 256 * h:256 * h + 256].rearrange("p (h e) -> p h e", h=4),
                      lambda a: a.rearrange("p (h e) -> p h e", h=4)[:, :, NOPE:])

            root(TT)
            act.wait_ge(sem("dext_done"), RH)
            px_in(0)
            px_in(1)
            latents_in(0)
            root(2 * TT)
            px_in(2)
            latents_in(1)
            latents_in(2)
            for j in range(8):
                kv_in(j)
            for j in range(4):
                tt, h = j // 2, j % 2
                empty("qu", j, Q2[:, tt, 4 * h:4 * h + 4, :],
                      lambda a: a[:, 0:4 * QK].rearrange("p (h e) -> p h e", h=4))
            px_in(3)
            root(6 * MH)
            px_in(4)
            px_in(5)
            for tt in range(TT):
                act.wait_ge(sem("filled"), outs.filled("rT", tt))
                b = four(ps[:, outs.bank("rT", tt), :])
                step(nc.scalar.activation(rqT[:, :, P * tt:P * tt + P], b[:, 0:2, :], ACT.Copy))
                empty("rT", tt, rkT[:, :, S + P * tt:S + P * tt + P], lambda a: four(a)[:, 2:4, :], ACT.Copy,
                      scale=RDK ** -0.5)
            empty("rT", 2, rkT[:, :, 0:S], lambda a: a.rearrange("p (b k) -> p b k", b=2), ACT.Copy,
                  scale=RDK ** -0.5)
            px_in(6)
            px_in(7)
            act.wait_ge(sem("dext_used"), 1)
            for j in range(12):
                tile, h = j // 2, j % 2
                dst = (kT2[:, 4 * h:4 * h + 4, P * tile:P * tile + P] if tile < 4 else
                       qT2[:, 4 * h:4 * h + 4, P * (tile - 4):P * (tile - 4) + P])
                empty("kqT", j, dst, lambda a: four(a)[0:QK])
            for tt in range(TT):
                act.wait_ge(sem("filled"), outs.filled("ro", tt))
                for h in range(RH):
                    cut = slice(RDV * h, RDV * h + RDV)
                    ins = nc.scalar.activation(ro[:, tt, cut], ps[:, outs.bank("ro", tt), cut], ACT.Square,
                                               accum_out=rsq[:, RH * tt + h:RH * tt + h + 1])
                step(ins)
                empty("ro", tt, ro[:, tt, :], same)
            for s in range(2 * MH):
                if s == 6:
                    act.wait_ge(sem("ret_var"), 1)
                    nc.scalar.activation(rsq, rsq, ACT.Sqrt).then_inc(sem("ret_root"), 1)
                act.wait_ge(sem("s2_max"), s + 1)
                empty("s2", s, E2[:, s, :], same, ACT.Exp, bias=mneg[:, s:s + 1], scale=QK ** -0.5,
                      accum_out=mx[:, s:s + 1])
                if s == 1:
                    for j in range(6):
                        empty("mb2", j, (mb2, mb3, mb4)[j // 2][:, 512 * (j % 2):512 * (j % 2) + 512], same)
            for m in range(2):
                if m:
                    for tt in range(TT):
                        empty("rmT", tt, mixT2[:, 4:8, P * tt:P * tt + P], four)
                act.wait_ge(sem("oT2_mm"), m + 1)
                nc.scalar.activation(mixT2[:, 2 * m:2 * m + 2, :], ps[:, 6 + m, :].rearrange("p (b q) -> p b q", b=2),
                                     ACT.Copy).then_inc(sem("oT2_taken"), 1)
            root(TT)
            for j in range(4):
                tt, h = j // 2, j % 2
                empty("hfT", j, hfT[:, 4 * h:4 * h + 4, P * tt:P * tt + P], four)
            route_exps(1)
            mixture(1)
            for h in range(2):
                act.wait_ge(sem("mb5_mm"), h + 1)
                nc.scalar.activation(act_[:, 512 * h:512 * h + 512], ps[:, 6 + h, :], ACT.Copy)\
                    .then_inc(sem("mb5_taken"), 1)

        @block.vector
        def _(dve):
            freed = sem("freed_dve")
            count = {}

            def step(ins, name="dve_step"):
                count[name] = count.get(name, 0) + 1
                ins.then_inc(sem(name), 1)
                dve.wait_ge(sem(name), count[name])

            def take(name, j, w=512):
                dve.wait_ge(sem("filled"), outs.filled(name, j))
                return ps[:, outs.bank(name, j), 0:w]

            def emptied(ins, name, j):
                step(ins, "freed_dve")
                assert count["freed_dve"] == outs.nth[outs.at[name][j]]

            def bc(ap, shape, axis):
                return ap.unsqueeze(axis).to_broadcast(shape)

            def inverse_root(n):
                step(nc.vector.memset(ssum[:, 63:64], 0.0), "var_ready")
                dve.wait_ge(sem("root_ready"), count["var_ready"])
                step(nc.vector.reciprocal(rstd[:, 0:n], rstd[:, 0:n]))

            def layer_norms(x, g, b, last, before=lambda tt: None):
                halves = x.shape[-1] // 512
                for tt in range(TT):
                    before(tt)
                    for h in range(halves):
                        step(nc.vector.bn_stats(stats[:, 6 * h:6 * h + 6], x[:, tt, 512 * h:512 * h + 512]))
                    step(nc.vector.bn_aggr(mv[:, 2 * tt:2 * tt + 2], stats[:, 0:6 * halves]))
                    step(nc.vector.tensor_scalar(rstd[:, tt:tt + 1], mv[:, 2 * tt + 1:2 * tt + 2], LN_EPS, None, ALU.add))
                inverse_root(TT)
                for tt in range(TT):
                    y = x[:, tt, :]
                    step(nc.vector.tensor_scalar(y, y, mv[:, 2 * tt:2 * tt + 1], rstd[:, tt:tt + 1], ALU.subtract, ALU.mult))
                    step(nc.vector.tensor_tensor(y, y, g, ALU.mult))
                    step(nc.vector.tensor_tensor(y, y, b, ALU.add), last)

            def mean_sq(x, width, at, lead, scratch):
                dst = rstd[:, at:at + lead]
                sqv = scratch[:, 0:lead * width].rearrange("p (a b) -> p a b", a=lead)
                step(nc.vector.tensor_tensor(sqv, x, x, ALU.mult))
                step(nc.vector.tensor_reduce(dst, sqv, AX, ALU.add))
                step(nc.vector.tensor_scalar(dst, dst, 1.0 / width, RMS_EPS, ALU.mult, ALU.add))

            def mean_sq_row(x, at, scratch):
                dst = rstd[:, at:at + 1]
                step(nc.vector.tensor_tensor_reduce(out=scratch, in0=x, in1=x, scale=1.0 / x.shape[-1], scalar=RMS_EPS,
                                                    op0=ALU.mult, op1=ALU.add, accum_out=dst))

            def modulated(dst, xs_, shift, scale, g, scratch, last):
                step(nc.vector.scalar_tensor_tensor(out=scale, in0=scale, scalar=1.0, in1=g, op0=ALU.add, op1=ALU.mult))
                for tt in range(TT):
                    mean_sq_row(xs_[:, tt, :], tt, scratch)
                inverse_root(TT)
                for tt in range(TT):
                    step(nc.vector.scalar_tensor_tensor(out=dst[:, tt, :], in0=xs_[:, tt, :], scalar=rstd[:, tt:tt + 1],
                                                        in1=scale, op0=ALU.mult, op1=ALU.mult))
                    step(nc.vector.tensor_tensor(dst[:, tt, :], dst[:, tt, :], shift, ALU.add), last)

            def context_norm():
                dve.wait_ge(sem("freed_act"), outs.emptied("mbc", "act"))
                dve.wait_ge(sem("ld_gat1"), 16)
                dve.wait_ge(sem("ld_ctx"), 16)
                modulated(cx, cx, mbc[:, 0, :], mbc[:, 1, :], g_at1, g_at1, "hc_ready")

            def log_decays():
                dve.wait_ge(sem("ld_small"), 96)
                x, e, one, ln = (lgt[:, 8 * i:8 * i + 8] for i in range(4))
                fix = lgam
                step(nc.vector.tensor_scalar(fix, x, -1.0, None, ALU.mult))
                step(nc.vector.tensor_tensor(fix, fix, x, ALU.max))
                step(nc.vector.tensor_scalar(e, fix, -1.0, None, ALU.mult), "lg_neg")
                dve.wait_ge(sem("lg_exp"), 1)
                step(nc.vector.tensor_scalar(one, e, 1.0, None, ALU.add), "lg_neg")
                dve.wait_ge(sem("lg_ln"), 1)
                step(nc.vector.tensor_scalar(fix, one, 1.0, None, ALU.is_equal))
                step(nc.vector.tensor_tensor(ln, ln, fix, ALU.add))
                step(nc.vector.scalar_tensor_tensor(out=one, in0=one, scalar=-1.0, in1=fix, op0=ALU.add, op1=ALU.add))
                step(nc.vector.reciprocal(one, one))
                step(nc.vector.tensor_tensor(ln, ln, e, ALU.mult))
                step(nc.vector.tensor_tensor(ln, ln, one, ALU.mult))
                step(nc.vector.tensor_scalar(fix, x, 0.0, None, ALU.min))
                step(nc.vector.tensor_tensor(lgam, fix, ln, ALU.subtract), "lg_ready")
            step(nc.vector.memset(modrow[:, :, :], 0.0), "modrow_zeroed")
            step(nc.vector.memset(ccT, 0.0))
            dve.wait_ge(sem("ccT_mm"), 1)
            step(nc.vector.tensor_copy(ccT[:, :, 0:2], ps[:, 7, 0:16].rearrange("p (r k) -> p k r", r=2)), "ccT_ready")
            dve.wait_ge(sem("ld_pos"), 16)
            dve.wait_ge(sem("ld_consts"), 16)
            n = TT * ROT1
            two_pi = 2 * np.pi
            p1 = 6.28125
            p2 = float(np.floor((two_pi - p1) * 2 ** 21) / 2 ** 21)
            p3 = two_pi - p1 - p2
            magic = 1.5 * 2 ** 23
            ang, turns, cosang = rot[:, 0:n], rot[:, 2 * n:3 * n], rot[:, n:2 * n]
            step(nc.vector.tensor_copy(pos_f, pos_i[:, :]))
            step(nc.vector.tensor_tensor(three(ang, TT), bc(pos_f, [P, TT, ROT1], 2), bc(const("inv8"), [P, TT, ROT1], 1),
                                         ALU.mult))
            step(nc.vector.tensor_scalar(turns, ang, 1.0 / two_pi, None, ALU.mult))
            step(nc.vector.tensor_scalar(turns, turns, magic, None, ALU.add))
            step(nc.vector.tensor_scalar(turns, turns, -magic, None, ALU.add))
            for part in (p1, p2, p3):
                step(nc.vector.scalar_tensor_tensor(out=ang, in0=turns, scalar=-part, in1=ang, op0=ALU.mult, op1=ALU.add))
            step(nc.vector.tensor_scalar(cosang, ang, np.pi / 2, None, ALU.add))
            step(nc.vector.tensor_scalar(turns, cosang, np.pi, -two_pi, ALU.is_gt, ALU.mult))
            step(nc.vector.tensor_tensor(cosang, cosang, turns, ALU.add))
            lim = float(np.nextafter(np.float32(np.pi), np.float32(0)))
            step(nc.vector.tensor_scalar(rot[:, 0:2 * n], rot[:, 0:2 * n], lim, -lim, ALU.min, ALU.max), "angles")
            dve.wait_ge(sem("sincos"), 1)
            dve.wait_ge(sem("freed_act"), outs.nth[outs.at["proj"][3]])
            heads = qk.rearrange("p t (h e) -> p t h e", e=DH1)
            r1, r2 = heads[:, :, :, 0:ROT1], heads[:, :, :, ROT1:2 * ROT1]
            shape = [P, TT, 16, ROT1]
            sin_b, cos_b = (bc(cs1[:, f], shape, 2) for f in range(2))
            a, b, c2, d = (E0.rearrange("p h k -> p (h k)")[:, 256 * i:256 * (i + 1)]
                           .rearrange("p (t h e) -> p t h e", t=TT, h=16) for i in range(4))
            for dst, x, y in ((a, r1, cos_b), (b, r2, sin_b), (c2, r2, cos_b), (d, r1, sin_b)):
                step(nc.vector.tensor_tensor(dst, x, y, ALU.mult))
            step(nc.vector.tensor_tensor(r1, a, b, ALU.subtract))
            step(nc.vector.tensor_tensor(r2, c2, d, ALU.add), "roped1")

            def modulation_row(r):
                if r == 0:
                    dve.wait_ge(sem("ld_bada"), 64)
                emptied(nc.vector.tensor_tensor(modrow[:, r, :], take("ada", r), modrow[:, r, :], ALU.add), "ada", r)

            modulation_row(0)
            dve.wait_ge(sem("ld_masks"), 16)
            for j in range(6):
                if j < 2:
                    dst, m, hs, w = E0[:, 4 * j:4 * j + 4, :], const("neg0"), 4, P
                else:
                    dst, m, hs, w = E1[:, 2 * (j - 2):2 * (j - 2) + 2, :], const("neg1"), 2, S
                emptied(nc.vector.scalar_tensor_tensor(
                    out=dst, in0=take("sc", j).rearrange("p (h k) -> p h k", h=hs), scalar=DH1 ** -0.5,
                    in1=bc(m, [P, hs, w], 1), op0=ALU.mult, op1=ALU.add), "sc", j)
            dve.wait_ge(sem("ld_early"), 16)
            for j in range(2):
                emptied(nc.vector.tensor_tensor(wsT[:, 4 * j:4 * j + 4, :], take("wsT", j).rearrange("p (g t) -> p g t", g=4),
                                                bc(const("tri"), [P, 4, P], 1), ALU.mult), "wsT", j)
            bsT = ssum[:, 0:SG]
            emptied(nc.vector.tensor_copy(bsT, take("bsT", 0, SG)), "bsT", 0)
            for i, (e, w) in enumerate(((E0, P), (E1, S))):
                m8 = mx[:, 8 * i:8 * i + 8]
                step(nc.vector.tensor_reduce(m8, e, AX, ALU.max))
                step(nc.vector.tensor_tensor(e, e, bc(m8, [P, H1, w], 2), ALU.subtract), "sc_shift")
            for i, (e, w) in enumerate(((E0, P), (E1, S))):
                m8, r8 = mx[:, 8 * i:8 * i + 8], rstd[:, 8 * i:8 * i + 8]
                dve.wait_ge(sem("sc_exp"), i + 1)
                step(nc.vector.tensor_tensor(e, e, bc(const(f"cnt{i}"), [P, H1, w], 1), ALU.mult))
                step(nc.vector.tensor_reduce(m8, e, AX, ALU.add))
                step(nc.vector.reciprocal(r8, m8))
                step(nc.vector.tensor_tensor(e, e, bc(r8, [P, H1, w], 2), ALU.mult), "E_ready")
            modulation_row(1)
            dve.wait_ge(sem("ld_small"), 96)
            dve.wait_ge(sem("freed_act"), outs.nth[outs.at["proj"][7]])
            layer_norms(vs1, sgu_v[:, 0:SGW], sgu_v[:, SGW:], "vs_ready")
            modulation_row(2)
            for j in range(2):
                z = take("z", j).rearrange("p (g c e) -> p c g e", g=4, c=TT)
                for tt in range(TT):
                    dst = vs1[:, tt, 256 * j:256 * j + 256].rearrange("p (g e) -> p g e", g=4)
                    ins = nc.vector.tensor_tensor(dst, z[:, tt], bc(bsT[:, 4 * j:4 * j + 4], [P, 4, 64], 2), ALU.add)
                    if tt == 0:
                        step(ins)
                    else:
                        emptied(ins, "z", j)
            dve.wait_ge(sem("freed_act"), outs.nth[outs.at["proj"][9]])
            step(nc.vector.tensor_tensor(u1, u1, vs1, ALU.mult), "sgu_ready")
            context_norm()
            log_decays()
            dve.wait_ge(sem("ld_x"), 16)

            def residual(tt):
                for j in (2 * tt, 2 * tt + 1):
                    x = xs[:, tt, 512 * (j % 2):512 * (j % 2) + 512]
                    emptied(nc.vector.scalar_tensor_tensor(out=x, in0=x, scalar=ALPHA, in1=take("wo", j), op0=ALU.mult,
                                                           op1=ALU.add), "wo", j)

            dve.wait_ge(sem("ld_ln1"), 16)
            layer_norms(xs, ln1_v[:, 0:D], ln1_v[:, D:], "h1_ready", residual)

            def route(m):
                k = 2 if m == 0 else 4
                w = NGRP + NE if m == 0 else NE
                dve.wait_ge(sem("ld_small"), 96)
                src = take(f"lg{m + 1}", 0, 2 * 64).rearrange("p (t c) -> p t c", t=TT)[:, :, 0:w]
                emptied(nc.vector.tensor_tensor(lg[:, :, 0:w], src, bc((rb1, rb2)[m], [P, TT, w], 1), ALU.add),
                        f"lg{m + 1}", 0)

                def best(vals):
                    for tt in range(TT):
                        step(nc.vector.max(top8[:, tt, :], vals[:, tt, :]))
                        step(nc.vector.max_index(idx_u[:, tt, :], top8[:, tt, :], vals[:, tt, :]))
                    step(nc.vector.tensor_copy(idxf, idx_u[:, :, :]))

                if m == 0:
                    step(nc.vector.memset(g8, -3e38))
                    step(nc.vector.tensor_copy(g8[:, :, 0:NGRP], lg[:, :, 0:NGRP]))
                    best(g8)
                    step(nc.vector.tensor_tensor(g8[:, :, 0:NGRP], lg[:, :, 0:NGRP],
                                                 top8[:, :, 0:1].to_broadcast([P, TT, NGRP]), ALU.subtract), "grp_shift")
                    step(nc.vector.tensor_tensor(goh, bc(const("iota32")[:, 0:NGRP], [P, TT, NGRP], 1),
                                                 idxf[:, :, 0:1].to_broadcast([P, TT, NGRP]), ALU.is_equal))
                    step(nc.vector.tensor_scalar(goh, goh, -1.0, -NEG, ALU.add, ALU.mult))
                    e4 = lg[:, :, NGRP:].rearrange("p t (g e) -> p t g e", g=NGRP)
                    step(nc.vector.tensor_tensor(e4, e4, bc(goh, [P, TT, NGRP, EPG], 3), ALU.add))
                    dve.wait_ge(sem("grp_exp"), 1)
                    step(nc.vector.tensor_reduce(psel, g8[:, :, 0:NGRP], AX, ALU.add))
                    step(nc.vector.reciprocal(psel, psel))
                    logits = lg[:, :, NGRP:]
                else:
                    logits = lg[:, :, 0:NE]
                best(logits)
                tw = topw[:, :, 0:k]
                step(nc.vector.tensor_tensor(tw, top8[:, :, 0:k], top8[:, :, 0:1].to_broadcast([P, TT, k]), ALU.subtract),
                     "top_shift")
                dve.wait_ge(sem("top_exp"), m + 1)
                den = ssum[:, 0:TT]
                step(nc.vector.tensor_reduce(den, tw, AX, ALU.add))
                step(nc.vector.reciprocal(den, den))
                if m == 0:
                    step(nc.vector.tensor_tensor(den, den, psel, ALU.mult))
                step(nc.vector.tensor_tensor(tw, tw, bc(den, [P, TT, k], 2), ALU.mult))
                step(nc.vector.memset(sel, 0.0))
                step(nc.vector.memset(gate, 0.0))
                for i in range(k):
                    shape = [P, TT, NE]
                    step(nc.vector.tensor_tensor(oh, bc(const("iota32"), shape, 1), idxf[:, :, i:i + 1].to_broadcast(shape),
                                                 ALU.is_equal))
                    step(nc.vector.tensor_tensor(sel, sel, oh, ALU.add))
                    step(nc.vector.tensor_tensor(oh, oh, topw[:, :, i:i + 1].to_broadcast(shape), ALU.mult))
                    step(nc.vector.tensor_tensor(gate, gate, oh, ALU.add))
                for q in range(2 - m):
                    for tt in range(TT):
                        s = sel[:, tt, :].rearrange("p (u q) -> p q u", q=2 - m)[:, q, :]
                        step(nc.vector.tensor_copy(row_sel(q, tt).rearrange("p (u b) -> p u b", b=BLOCKS[m]),
                                                   bc(s, [P, GROUPS[m], BLOCKS[m]], 2)))
                step(nc.vector.memset(place_of, 0.0), "sel_ready")
                rank = take(f"rk{m + 1}", 0, TT * NE).rearrange("p (t c) -> p t c", t=TT)
                emptied(nc.vector.scalar_tensor_tensor(out=key, in0=rank, scalar=1.0, in1=sel, op0=ALU.add, op1=ALU.mult),
                        f"rk{m + 1}", 0)
                step(nc.vector.tensor_scalar(key, key, -1.0, None, ALU.add))
                cn = take(f"cn{m + 1}", 0, 4)
                f0 = flag[:, 0:1]
                if m == 0:
                    step(nc.vector.tensor_copy(f0, cn[:, 2:3]))
                    emptied(nc.vector.tensor_tensor(f0, cn[:, 0:1], f0, ALU.max), "cn1", 0)
                else:
                    emptied(nc.vector.tensor_copy(f0, cn[:, 0:1]), "cn2", 0)
                step(nc.vector.tensor_tensor(f0, f0, const(f"more{m}"), ALU.is_gt))
                step(nc.vector.tensor_copy(flag[:, 1:2], f0), "flags")
                place = rstd[:, 0:1]
                emptied(nc.vector.tensor_copy(place, take(f"ps{m + 1}", 0, 1)), f"ps{m + 1}", 0)
                step(nc.vector.tensor_scalar(place_of[:, 0:TABLE], const("iota64")[:, 0:TABLE], place, f0, ALU.is_equal,
                                             ALU.mult))
                step(nc.vector.tensor_copy(place_of[:, TABLE:TABLE + 1], f0), "places_ready")
                tb = take(f"tb{m + 1}", 0)
                step(nc.vector.tensor_copy(off, tb[:, 64:64 + TABLE]))
                step(nc.vector.tensor_copy(table[:, 0:TABLE], tb[:, 0:TABLE]))
                step(nc.vector.tensor_copy(table[:, TABLE:TABLE + 1], tb[:, 128 + TABLE:129 + TABLE]))
                emptied(nc.vector.tensor_scalar(table[:, TABLE + 1:], tb[:, 192:192 + NE], -1.0, None, ALU.add), f"tb{m + 1}", 0)
                step(nc.vector.memset(m_y, 0.0))
                step(nc.vector.memset(pgT[0], 0.0))
                step(nc.vector.memset(pgT[1], 0.0), "table_ready")

            def mixture(m):
                p = f"m{m + 1}_"
                w = 2 if m == 0 else 1
                cap = CAP[m]
                FETCH, UNIT = 2, (2, 4)[m]
                kc = keyc[:, 0:TT * w].rearrange("p (t c) -> p t c", t=TT)
                gc = gatec[:, 0:TT * w].rearrange("p (t c) -> p t c", t=TT)
                shape = [P, TT, w, cap]
                h4 = hot.rearrange("p t (c s) -> p t c s", c=w)

                def group_of(n):
                    return dve.value_load(table[0:1, bass.ds(n, 1)], min_val=0, max_val=GROUPS[m] - 1)

                def link(ins, value):
                    ins.then_inc(sem(p + "dve_step"), 1)
                    dve.wait_ge(sem(p + "dve_step"), value)

                def one_hot(n, done):
                    g = group_of(n)
                    link(nc.vector.tensor_scalar(kc, key[:, :, bass.ds(g * w, w)], off[:, bass.ds(n, 1)], None, ALU.subtract),
                         done + 1)
                    link(nc.vector.tensor_copy(gc, gate[:, :, bass.ds(g * w, w)]), done + 2)
                    iota = const("iota64")[:, 0:cap].unsqueeze(1).unsqueeze(1).to_broadcast(shape)
                    nc.vector.tensor_tensor(h4, iota, bc(kc, shape, 3), ALU.is_equal).then_inc(sem(p + "hot"), 1)

                def gates(n):
                    dve.wait_ge(sem(p + "hot"), n + 1)
                    for i in range(2):
                        nc.vector.tensor_tensor(hotg[:, :, i, :].rearrange("p t (c s) -> p t c s", c=w), h4,
                                                bc(gc, shape, 3), ALU.mult).then_inc(sem(p + "hotg"), 1)

                def bias_of(n):
                    nc.vector.tensor_copy(bsel[0], const("eye3")[0:96, bass.ds(group_of(n), 1)].to_broadcast([96, SLOTS]))\
                        .then_inc(sem("m2_bsel1"), 1)

                one_hot(0, 0)
                gates(0)
                if m == 1:
                    bias_of(0)
                dve.wait_ge(sem(p + "gathered"), 1)
                dve.wait_ge(sem(p + "hotg"), 2)
                one_hot(1, FETCH)
                units = dve.value_load(table[0:1, TABLE:TABLE + 1], min_val=GROUPS[m], max_val=TABLE - 4)
                with dve.Fori(0, units) as n:
                    done = n * UNIT + 2 * FETCH
                    dve.wait_ge(sem(p + "up_mm"), n + 1)
                    if m == 0:
                        dve.wait_ge(sem(p + "sig"), n + 1)
                        nc.vector.tensor_tensor(m_a[:, 0:P], m_s[:, 0:P], ps[:, 4, P:2 * P], ALU.mult)\
                            .then_inc(sem(p + "act"), 1)
                    else:
                        uu = ps[:, 4:6, :].rearrange("p b (f g) -> p (b f) g", g=2)
                        nc.vector.tensor_scalar(m_t, uu[:, :, 0], LIMIT, None, ALU.min).then_inc(sem(p + "glu"), 1)
                        link(nc.vector.tensor_scalar(m_l, uu[:, :, 1], LIMIT, -LIMIT, ALU.min, ALU.max), done + 1)
                        dve.wait_ge(sem(p + "glu"), n + 1)
                        link(nc.vector.scalar_tensor_tensor(out=m_l, in0=m_l, scalar=1.0, in1=m_t, op0=ALU.add, op1=ALU.mult),
                             done + 2)
                        dve.wait_ge(sem(p + "sig"), n + 1)
                        nc.vector.tensor_tensor(m_a, m_l, m_s, ALU.mult).then_inc(sem(p + "act"), 1)
                        dve.wait_ge(sem("m2_bsel1"), n + 1)
                        nc.vector.tensor_copy(bsel[1], bsel[0]).then_inc(sem("m2_bsel2"), 1)
                        dve.wait_ge(sem("m2_bsel2"), n + 1)
                    dve.wait_ge(sem(p + "hot_turned"), n + 1)
                    for i in range(2):
                        h = slice(64 * i, 64 * i + 64)
                        nc.vector.tensor_copy(pgT[i][h, :], ps[h, 5, 0:2 * P]).then_inc(sem(p + "pgT"), 1)
                    gates(n + 1)
                    if m == 1:
                        bias_of(n + 1)
                    dve.wait_ge(sem(p + "gathered"), n + 2)
                    dve.wait_ge(sem(p + "hotg"), n * 2 + 4)
                    one_hot(n + 2, done + (UNIT - FETCH))

            route(0)
            mixture(0)
            dve.wait_ge(sem("m1_scattered"), 1)
            for tt in range(TT):
                x = xs[:, tt, :]
                step(nc.vector.scalar_tensor_tensor(out=x, in0=x, scalar=ALPHA,
                                                    in1=ps[:, 2 * tt:2 * tt + 2, :].rearrange("p b c -> p (b c)"),
                                                    op0=ALU.mult, op1=ALU.add), "m1_sums_read")
            dve.wait_ge(sem("ld_ln2"), 16)
            layer_norms(xs, ln2_v[:, 0:D], ln2_v[:, D:], "dve_step")
            step(nc.vector.memset(mneg, 0.0), "x1_ready")

            dve.wait_ge(sem("ld_latent"), 48)
            dve.wait_ge(sem("freed_act"), outs.emptied("mb", "act"))
            modulated(hn, xs, mb[:, 0, :], mb[:, 1, :], g_at, sq, "hn_ready")

            def normed(x, at, g, o):
                w = x.shape[-1]
                step(nc.vector.scalar_tensor_tensor(out=cn_[:, o:o + w], in0=x, scalar=rstd[:, at:at + 1], in1=g,
                                                    op0=ALU.mult, op1=ALU.mult), "latents")

            dve.wait_ge(sem("freed_act"), outs.emptied("pc", "act"))
            for tt in range(TT):
                mean_sq_row(pc[:, tt, 0:KVL], tt, scr_l[:, 0:KVL])
            inverse_root(TT)
            for tt in range(TT):
                normed(pc[:, tt, 0:KVL], tt, g_kvl, KVL * tt)
            dve.wait_ge(sem("freed_act"), outs.nth[outs.at["px"][1]])
            for tt in range(TT):
                mean_sq_row(px[:, tt, O_KV:O_PE], tt, scr_l[:, 0:KVL])
                mean_sq_row(px[:, tt, 0:QL], TT + tt, scr_l[:, 0:QL])
            inverse_root(2 * TT)
            for tt in range(TT):
                normed(px[:, tt, O_KV:O_PE], tt, g_kvl, KVL * (TT + tt))
            for tt in range(TT):
                normed(px[:, tt, 0:QL], TT + tt, g_ql, 512 + QL * tt)
            def axial(x, heads, dim, name, last):
                nf = dim // 4
                cosv, sinv = (three(const(k + name), TT) for k in ("cos", "sin"))
                tmp = scr[:, 0:TT * heads * dim].rearrange("p (t h e) -> p t h e", t=TT, h=heads)
                for s in range(2):
                    for ax in range(2):
                        o, i = 2 * nf * ax + nf * s, 2 * nf * ax + nf * (1 - s)
                        step(nc.vector.tensor_tensor(tmp[:, :, :, o:o + nf], x[:, :, :, i:i + nf],
                                                     bc(sinv[:, :, o:o + nf], [P, TT, heads, nf], 2), ALU.mult))
                step(nc.vector.tensor_tensor(x, x, bc(cosv, [P, TT, heads, dim], 2), ALU.mult))
                step(nc.vector.tensor_tensor(x, x, tmp, ALU.add), last)

            def heads_of(x):
                return x.rearrange("p t h e -> p (t h) e")

            def head_norm(x, at, g):
                n = TT * MH
                step(nc.vector.tensor_tensor(x, x, bc(rstd[:, at:at + n], [P, n, QK], 2), ALU.mult))
                step(nc.vector.tensor_tensor(x, x, bc(g, [P, n, QK], 1), ALU.mult))

            Kc, Kx, Qx = heads_of(K2[:, 0:2]), heads_of(K2[:, 2:4]), heads_of(Q2)
            dve.wait_ge(sem("dext_done"), RH)
            dve.wait_ge(sem("freed_act"), outs.nth[outs.at["kv"][3]])
            step(nc.vector.tensor_copy(K2[:, 0:2, :, NOPE:QK], bc(pc[:, :, KVL:KVL + PE_W], [P, TT, MH, PE_W], 2)))
            mean_sq(Kc, QK, 0, 2 * MH, scr)
            dve.wait_ge(sem("freed_act"), outs.nth[outs.at["kv"][7]])
            step(nc.vector.tensor_copy(K2[:, 2:4, :, NOPE:QK], bc(px[:, :, O_PE:O_RQ], [P, TT, MH, PE_W], 2)))
            mean_sq(Kx, QK, 2 * MH, 2 * MH, scr)
            dve.wait_ge(sem("freed_act"), outs.emptied("qu", "act"))
            mean_sq(Qx, QK, 4 * MH, 2 * MH, scr)
            inverse_root(6 * MH)
            head_norm(Kc, 0, g_kh)
            head_norm(Kx, 2 * MH, g_kh)
            head_norm(Qx, 4 * MH, g_qh)
            axial(K2[:, 2:4, :, NOPE:QK], MH, PE_W, "M", "dve_step")
            axial(Q2[:, :, :, NOPE:QK], MH, PE_W, "M", "dve_step")
            step(nc.vector.memset(ssum[:, 32:33], 0.0), "kq_ready")
            for j in range(2 * RH):
                h, half = j // 2, j % 2
                d = dext[h][:, 2 * half:2 * half + 2, :].rearrange("p k q -> p (k q)")
                emptied(nc.vector.tensor_tensor(sd[:, h, 2 * half:2 * half + 2, :].rearrange("p k q -> p (k q)"),
                                                take("rs", j), d, ALU.mult), "rs", j)
            step(nc.vector.memset(ssum[:, 32:33], 0.0), "dext_used")
            def weights(s):
                dve.wait_ge(sem("freed_act"), outs.nth[outs.at["s2"][s]])
                step(nc.vector.reciprocal(rstd[:, s:s + 1], mx[:, s:s + 1]))
                step(nc.vector.tensor_scalar(E2[:, s, :], E2[:, s, :], rstd[:, s:s + 1], None, ALU.mult), "E2_ready")

            def turned(h):
                for qt in range(TT):
                    if h >= 4 and qt == 0:
                        dve.wait_ge(sem("oT2_head"), h - 3)
                    emptied(nc.vector.tensor_copy(ET2[:, h % 4, :, P * qt:P * qt + P],
                                                  take("eT", 2 * h + qt).rearrange("p (k q) -> p k q", k=4)),
                            "eT", 2 * h + qt)

            for h in range(MH + 2):
                if h < MH:
                    for s in (2 * h, 2 * h + 1):
                        src = take("s2", s)
                        step(nc.vector.tensor_reduce(ssum[:, s:s + 1], src, AX, ALU.max))
                        step(nc.vector.tensor_scalar(mneg[:, s:s + 1], ssum[:, s:s + 1], -QK ** -0.5, None, ALU.mult), "s2_max")
                if 1 <= h <= MH:
                    for s in (2 * h - 2, 2 * h - 1):
                        weights(s)
                if h == 1:
                    dve.wait_ge(sem("freed_act"), outs.emptied("ro", "act"))
                    step(nc.vector.tensor_scalar(rsq, rsq, 1.0 / RDV, RMS_EPS, ALU.mult, ALU.add), "ret_var")
                if h == 4:
                    dve.wait_ge(sem("ret_root"), 1)
                    step(nc.vector.reciprocal(rsq, rsq), "ret_scale")
                if h >= 2:
                    turned(h - 2)
            dve.wait_ge(sem("ld_b"), 96)
            for i in range(3):
                step(nc.vector.tensor_copy(bpart, braw))
                r = slice(32 * i, 32 * i + 32)
                step(nc.vector.tensor_copy(b1p[r, :], bpart[r, 0:2 * FF2]))
                step(nc.vector.tensor_copy(b2p[r, :], bpart[r, 2 * FF2:]), "bias_parts")
                if i < 2:
                    step(nc.vector.tensor_tensor(braw, braw, bpart, ALU.subtract))
            step(nc.vector.scalar_tensor_tensor(out=mb4, in0=mb4, scalar=1.0, in1=g_ff, op0=ALU.add, op1=ALU.mult))
            for j in range(4):
                tt, h = j // 2, j % 2
                cut = slice(512 * h, 512 * h + 512)
                part = gated[:, 512 * (j % 2):512 * (j % 2) + 512]
                emptied(nc.vector.tensor_tensor(part, take("wo2", j), mb2[:, cut], ALU.mult), "wo2", j)
                step(nc.vector.tensor_tensor(xs[:, tt, cut], xs[:, tt, cut], part, ALU.add), "wo2_added")
            for tt in range(TT):
                mean_sq_row(xs[:, tt, :], tt, gated[:, 0:D])
            inverse_root(TT)
            for tt in range(TT):
                step(nc.vector.scalar_tensor_tensor(out=hf[:, tt, :], in0=xs[:, tt, :], scalar=rstd[:, tt:tt + 1],
                                                    in1=mb4, op0=ALU.mult, op1=ALU.mult))
                step(nc.vector.tensor_tensor(hf[:, tt, :], hf[:, tt, :], mb3, ALU.add),
                     "hf_part" if tt == 0 else "hf_ready")
            route(1)
            mixture(1)
            dve.wait_ge(sem("m2_scattered"), 1)
            dve.wait_ge(sem("mb5_taken"), 2)
            for tt in range(TT):
                prod = act_[:, 1024 + 1024 * tt:2048 + 1024 * tt]
                step(nc.vector.tensor_tensor(prod, ps[:, 2 * tt:2 * tt + 2, :].rearrange("p b c -> p (b c)"),
                                             act_[:, 0:1024], ALU.mult))
                step(nc.vector.tensor_tensor(xs[:, tt, :], xs[:, tt, :], prod, ALU.add))
            step(nc.vector.memset(mneg, 0.0), "y_ready")

        @block.gpsimd
        def _(pool):
            count = {}

            def step(ins, name="pool_step"):
                count[name] = count.get(name, 0) + 1
                ins.then_inc(sem(name), 1)
                pool.wait_ge(sem(name), count[name])

            def decays(h):
                pool.wait_ge(sem("dext_exp"), 2 * h + 2)
                own, back = dext[h][:, 2:4, :].rearrange("p k q -> p (k q)"), dtmp[:, h, 512:1024]
                step(nc.gpsimd.tensor_tensor(own, own, decay[:, 2048:2560], ALU.mult))
                step(nc.gpsimd.tensor_tensor(back, back, decay[:, 2560:3072], ALU.mult))
                d = dext[h].rearrange("p k q -> p (k q)")
                step(nc.gpsimd.tensor_tensor(d, d, dtmp[:, h, :], ALU.add), "dext_done")

            pool.wait_ge(sem("ld_decay"), 16)
            for h in range(RH):
                decays(h)
            pool.wait_ge(sem("freed_act"), outs.nth[outs.at["px"][3]])
            heads, nf = 2 * RH, RDK // 4
            x = px[:, :, O_RQ:O_RV].rearrange("p t (h e) -> p t h e", h=heads)
            cosv, sinv = (three(const(k), TT) for k in ("cosR", "sinR"))
            tmp = scr_p.rearrange("p (t h e) -> p t h e", t=TT, h=heads)
            for s in range(2):
                for ax in range(2):
                    o, i = 2 * nf * ax + nf * s, 2 * nf * ax + nf * (1 - s)
                    step(nc.gpsimd.tensor_tensor(tmp[:, :, :, o:o + nf], x[:, :, :, i:i + nf],
                                                 sinv[:, :, o:o + nf].unsqueeze(2).to_broadcast([P, TT, heads, nf]), ALU.mult))
            step(nc.gpsimd.tensor_tensor(x, x, cosv.unsqueeze(2).to_broadcast([P, TT, heads, RDK]), ALU.mult))
            step(nc.gpsimd.tensor_tensor(x, x, tmp, ALU.add), "roped_r")
            pool.wait_ge(sem("ret_scale"), 1)
            for tt in range(TT):
                o4 = ro[:, tt, :].rearrange("p (h e) -> p h e", h=RH)
                scale = rsq[:, RH * tt:RH * tt + RH].unsqueeze(2).to_broadcast([P, RH, RDV])
                step(nc.gpsimd.tensor_tensor(o4, o4, scale, ALU.mult))
                step(nc.gpsimd.tensor_tensor(ro[:, tt, :], ro[:, tt, :], g_ro, ALU.mult))
                step(nc.gpsimd.tensor_tensor(ro[:, tt, :], ro[:, tt, :], rg[:, tt, :], ALU.mult), "ro_ready")

        @block.tensor
        def _(pe):
            filled = sem("filled")

            def bank(name, j):
                b = outs.before(name, j)
                if b is not None:
                    pe.wait_ge(sem("freed_" + b[0]), b[1])
                return ps[:, outs.bank(name, j), :]

            def turn(name, j, blocks):
                dst = bank(name, j)
                for i, b in enumerate(blocks):
                    n = b.shape[-1]
                    m = b.shape[0]
                    mm = nc.tensor.transpose(dst[0:n, P * i:P * i + m] if m == P else dst[0:n, 0:m], b, ident[0:m, 0:m])
                mm.then_inc(filled, 1)

            def quarter(ap, h):
                return [ap[:, P * (4 * h + i):P * (4 * h + i) + P] for i in range(4)]

            pe.wait_ge(sem("ld_consts"), 16)
            pe.wait_ge(sem("ld_x"), 16)
            for j in range(4):
                turn("xT", j, quarter(xs[:, j // 2, :], j % 2))
            pe.wait_ge(sem("cc_ready"), 1)
            nc.tensor.transpose(ps[:, 7, 0:16], cc, ident[0:16, 0:16]).then_inc(sem("ccT_mm"), 1)

            def proj(j):
                c, tt = CHUNKS[j // 2], j % 2
                pe.wait_ge(sem(f"ld_win{c}"), 16)
                dst = bank("proj", j)
                if j < 2:
                    pe.wait_ge(freed_act, outs.nth[outs.at["xT"][2 * tt + 1]])
                for k in range(KT):
                    mm = nc.tensor.matmul(dst, tT[:, k, P * tt:P * tt + P], w_in[:, c, 512 * k:512 * k + 512],
                                          start=(k == 0), stop=(k == KT - 1))
                mm.then_inc(filled, 1)

            def modulation(i):
                r, half = i // 2, i % 2
                dst = bank("ada", r) if half == 0 else ps[:, outs.bank("ada", r), :]
                pe.wait_ge(sem(f"ld_ada{half}"), 16 * (r + 1))
                if i == 0:
                    pe.wait_ge(sem("ccT_ready"), 1)
                for k in range(KT // 2 * half, KT // 2 * half + KT // 2):
                    for g in range(4):
                        mm = nc.tensor.matmul(dst[32 * g:32 * g + 32, :], ccT[:, k, :], ada[:, k, 512 * g:512 * g + 512],
                                              start=(k == 0), stop=(k == KT - 1))
                mm.then_inc(filled if half else sem("ada_used"), 1)

            def spread(name, j, v, h, ctx_row):
                c = 2 * v + h
                r = 32 * (c % 4) + ctx_row
                nc.tensor.matmul(bank(name, j), ident[:, r:r + 1].to_broadcast([P, P]), modrow[:, c // 4, :],
                                 start=True, stop=True).then_inc(filled, 1)

            freed_act = sem("freed_act")
            for j in range(5):
                proj(j)
            pe.wait_ge(sem("roped1"), 1)
            for j in range(4):
                turn("qkT", j, quarter(qk[:, j // 2, :], j % 2))
            modulation(0)
            proj(5)
            modulation(1)
            pe.wait_ge(freed_act, outs.emptied("qkT", "act"))
            order = [0, 2, 4, 6, 1, 3, 5, 7]
            for j in range(6):
                dst = bank("sc", j)
                qt, hs = (0, order[4 * j:4 * j + 4]) if j < 2 else (1, order[2 * (j - 2):2 * (j - 2) + 2])
                w = P * (qt + 1)
                for i, h in enumerate(hs):
                    r = slice(64 * (h % 2), 64 * (h % 2) + 64)
                    mm = nc.tensor.matmul(dst[:, w * i:w * i + w], qkT[r, h // 2, P * qt:P * qt + P],
                                          qkT[r, 4 + h // 2, 0:w], start=True, stop=True)
                mm.then_inc(filled, 1)
            pe.wait_ge(sem("ld_spatial"), 32)
            for j in range(2):
                turn("wsT", j, quarter(w_sp, j))
            turn("bsT", 0, [b_sp])
            proj(6)
            modulation(2)
            proj(7)
            modulation(3)
            proj(8)
            modulation(4)
            proj(9)
            modulation(5)
            pe.wait_ge(sem("E_ready"), 2)
            for j in range(6):
                (qt, kt), h = ((0, 0), (1, 0), (1, 1))[j // 2], j % 2
                e = E0 if qt == 0 else E1
                turn("ET", j, [e[:, 4 * h + i, P * kt:P * kt + P] for i in range(4)])
            pe.wait_ge(sem("freed_dve"), outs.nth[outs.at["ada"][0]])
            for j in range(4):
                spread("mbc", j, j // 2, j % 2, 1)
            pe.wait_ge(freed_act, outs.emptied("ET", "act"))
            for m in range(2):
                for j in (2 * m, 2 * m + 1):
                    for h in (2 * j, 2 * j + 1):
                        pos = order.index(h)
                        dst = ps[64 * (h % 2):64 * (h % 2) + 64, 6 + m, S * (j % 2):S * (j % 2) + S]
                        nc.tensor.matmul(dst, v1[:, 0, 64 * h:64 * h + 64], ET[:, 0, pos, :], start=True, stop=False)
                        mm = nc.tensor.matmul(dst[:, P:S], v1[:, 1, 64 * h:64 * h + 64], ET[:, 1, pos, P:S],
                                              start=False, stop=True)
                mm.then_inc(sem("oT_mm"), 1)
            pe.wait_ge(sem("vs_ready"), TT)
            for j in range(2):
                dst = bank("z", j)
                for i in range(4):
                    g = 4 * j + i
                    mm = nc.tensor.matmul(dst[:, P * i:P * i + P], wsT[:, g, :], vs1[:, :, 64 * g:64 * g + 64],
                                          start=True, stop=True)
                mm.then_inc(filled, 1)
            pe.wait_ge(sem("sgu_ready"), 1)
            for tt in range(TT):
                turn("mT", tt, quarter(u1[:, tt, :], 0))
            pe.wait_ge(sem("oT_taken"), 2)
            pe.wait_ge(freed_act, outs.emptied("mT", "act"))
            pe.wait_ge(sem("ld_wo"), 16)
            for j in range(4):
                tt, h = j // 2, j % 2
                dst = bank("wo", j)
                for k in range(KT):
                    mm = nc.tensor.matmul(dst, mixT[:, k, P * tt:P * tt + P], wo_w[:, k, 512 * h:512 * h + 512],
                                          start=(k == 0), stop=(k == KT - 1))
                mm.then_inc(filled, 1)

            def route(m, xT, w, name):
                pe.wait_ge(freed_act, outs.emptied(name, "act"))
                pe.wait_ge(sem("ld_small"), 96)
                n = w.shape[-1]
                dst = bank(f"lg{m + 1}", 0)
                for tt in range(TT):
                    for k in range(KT):
                        mm = nc.tensor.matmul(dst[:, 64 * tt:64 * tt + n], xT[:, k, P * tt:P * tt + P], w[:, k, :],
                                              start=(k == 0), stop=(k == KT - 1))
                mm.then_inc(filled, 1)
                pe.wait_ge(sem("sel_ready"), m + 1)
                dst = bank(f"rk{m + 1}", 0)
                nc.tensor.matmul(dst[:, 0:NE], const("upper"), sel[:, 0, :], start=True, stop=True)
                nc.tensor.matmul(dst[:, NE:2 * NE], ones, sel[:, 0, :], start=True, stop=False)
                nc.tensor.matmul(dst[:, NE:2 * NE], const("upper"), sel[:, 1, :], start=False, stop=True).then_inc(filled, 1)
                dst = bank(f"cn{m + 1}", 0)
                for q in range(2 - m):
                    for tt in range(TT):
                        mm = nc.tensor.matmul(dst[:, 2 * q:2 * q + 2], row_sel(q, tt), ones[:, 0:2],
                                              start=(tt == 0), stop=(tt == 1))
                mm.then_inc(filled, 1)
                pe.wait_ge(sem("flags"), m + 1)
                nc.tensor.matmul(bank(f"ps{m + 1}", 0)[:, 0:2], const("upper"), flag, start=True, stop=True).then_inc(filled, 1)
                pe.wait_ge(sem("places_ready"), m + 1)
                dst = bank(f"tb{m + 1}", 0)
                place = rstd[:, 0:1]
                for i, (col, rhs) in enumerate(((const(f"group{m}"), place_of), (const(f"off{m}"), place_of),
                                                (ones[:, 0:1], place_of), (place, const(f"first{m}")))):
                    mm = nc.tensor.matmul(dst[:, 64 * i:64 * i + rhs.shape[-1]], col.to_broadcast([P, P]), rhs,
                                          start=True, stop=True)
                mm.then_inc(filled, 1)

            def mixture(m, h):
                p = f"m{m + 1}_"

                def tokens_in(n):
                    pe.wait_ge(sem(p + "hot"), n + 1)
                    for tt in range(TT):
                        for g in range(2):
                            mm = nc.tensor.matmul(ps[64 * g:64 * g + 64, 6, :], hot[:, tt, :],
                                                  h[:, tt, HALF * g:HALF * g + HALF], start=(tt == 0), stop=(tt == TT - 1))
                    mm.then_inc(sem(p + "gathered"), 1)

                def tokens_turned(n):
                    pe.wait_ge(sem(p + "xg"), n + 1)
                    for i in range(4):
                        mm = nc.tensor.transpose(ps[:, 6, P * i:P * i + P], xg[:, P * i:P * i + P], ident)
                    mm.then_inc(sem(p + "xg_turned"), 1)

                def tokens_out():
                    for g in range(2):
                        for tt in range(TT):
                            nc.tensor.matmul(ps[:, 2 * tt + g, :], pgT[g][:, P * tt:P * tt + P], m_y, start=False,
                                             stop=False, skip_group_check=True)

                def up_pair(loads):
                    for q in range(2):
                        for k in range(KT):
                            if k % 4 == 0:
                                pe.wait_ge(sem(f"ld_gu{q}{k // 4}"), loads)
                            o = P * (k % 4) + 64 * (k // 4) + 32 * q
                            for g in range(2):
                                r = 64 * g + 32 * q
                                mm = nc.tensor.matmul(ps[r:r + 32, 4, 0:256], xgT[:, o:o + 32], gu_w[:, q, k, :, g, :],
                                                      start=(k == 0), stop=(k == KT - 1))
                        mm.then_inc(sem("m1_up_used"), 1)

                def down_pair(loads):
                    for q in range(2):
                        pe.wait_ge(sem(f"ld_dn{q}"), loads)
                    for k in range(FF1 // P):
                        for q in range(2):
                            for g in range(2):
                                r, o = 64 * g + 32 * q, 64 * k + 32 * q
                                mm = nc.tensor.matmul(ps[r:r + 32, 7, :], m_aT[:, o:o + 32],
                                                      dn_w[:, q, k, HALF * g:HALF * g + HALF],
                                                      start=(k == 0), stop=(k == FF1 // P - 1))
                    mm.then_inc(sem(p + "dn_mm"), 1)

                def bias(i, part, bank_, o):
                    for g in range(2):
                        c = o + g * (FF2 if i == 0 else HALF)
                        nc.tensor.matmul(ps[64 * g:64 * g + 64, bank_, :], bsel[i], part[:, c:c + 512],
                                         start=True, stop=False)

                def up_expert(loads):
                    for k in range(KT):
                        pe.wait_ge(sem(f"ld_w1_{k}"), loads)
                        o = P * (k % 4) + 64 * (k // 4)
                        for b in range(2):
                            for g in range(2):
                                c = FF2 * g + 512 * b
                                mm = nc.tensor.matmul(ps[64 * g:64 * g + 64, 4 + b, :], xgT[:, o:o + 64],
                                                      w1_w[:, k, c:c + 512], start=False, stop=(k == KT - 1))
                        mm.then_inc(sem("m2_w1_used"), 1)

                def down_expert(loads):
                    for k in range(FF2 // P):
                        pe.wait_ge(sem(f"ld_w2_{k}"), loads)
                        o = P * (k % 4) + 64 * (k // 4)
                        for g in range(2):
                            mm = nc.tensor.matmul(ps[64 * g:64 * g + 64, 7, :], m_aT[:, o:o + 64],
                                                  w2_w[:, k, HALF * g:HALF * g + HALF], start=False, stop=(k == FF2 // P - 1))
                        mm.then_inc(sem("m2_w2_used"), 1)

                pe.wait_ge(sem("table_ready"), m + 1)
                if m == 1:
                    pe.wait_ge(sem("bias_parts"), 3)
                for b in range(4):
                    nc.tensor.matmul(ps[:, b, :], pgT[0][:, 0:P], h[:, 0, 0:512], start=True, stop=False,
                                     skip_group_check=True)
                pe.sem_inc(sem(p + "y"), 1)
                pe.sem_inc(sem(p + "pgT"), 2)
                tokens_in(0)
                tokens_turned(0)
                units = pe.value_load(table[0:1, TABLE:TABLE + 1], min_val=GROUPS[m], max_val=TABLE - 4)
                def unit(n):
                    loads = pe.value_load(table[0:1, bass.ds(n, 1)], min_val=0, max_val=GROUPS[m] - 1) * 16 + 16
                    pe.wait_ge(sem(p + "pgT"), n * 2 + 2)
                    if m == 0:
                        pe.wait_ge(sem(p + "xgT"), n + 1)
                        up_pair(loads)
                        pe.wait_ge(sem("m1_up_used"), n * 2 + 2)
                    else:
                        pe.wait_ge(sem("m2_bsel1"), n + 1)
                        for b in range(2):
                            bias(0, b1p, 4 + b, 512 * b)
                        pe.wait_ge(sem(p + "xgT"), n + 1)
                        up_expert(loads)
                        pe.wait_ge(sem("m2_w1_used"), n * KT + KT)
                    pe.sem_inc(sem(p + "up_mm"), 1)
                    pe.wait_ge(sem(p + "y"), n + 1)
                    tokens_out()
                    tokens_in(n + 1)
                    pe.wait_ge(sem(p + "act"), n + 1)
                    for i in range(1 if m == 0 else 4):
                        mm = nc.tensor.transpose(ps[:, 4, P * i:P * i + P], m_a[:, P * i:P * i + P], ident)
                    mm.then_inc(sem(p + "a_turned"), 1)
                    pe.wait_ge(sem(p + "hotg"), n * 2 + 2)
                    for tt in range(TT):
                        mm = nc.tensor.transpose(ps[:, 5, P * tt:P * tt + P], hotg[:, tt].rearrange("p d s -> p (d s)"), ident)
                    mm.then_inc(sem(p + "hot_turned"), 1)
                    tokens_turned(n + 1)
                    if m == 0:
                        pe.wait_ge(sem(p + "aT"), n + 1)
                        down_pair(loads)
                    else:
                        pe.wait_ge(sem("m2_bsel2"), n + 1)
                        bias(1, b2p, 7, 0)
                        pe.wait_ge(sem(p + "aT"), n + 1)
                        down_expert(loads)
                        pe.wait_ge(sem("m2_w2_used"), n * KT + KT)
                        pe.sem_inc(sem(p + "dn_mm"), 1)

                if m == 0:
                    for tt in range(TT):
                        with pe.Fori(PIECES * tt, PIECES * tt + PIECES) as n:
                            unit(n)
                            o = (n - PIECES * tt) * P + O_RK
                            pe.wait_ge(sem("ld_w_in_2"), 16)
                            for k in range(KT):
                                mm = nc.tensor.matmul(ps[:, 4, 0:P], hTc[:, k, P * tt:P * tt + P], w_in2[:, k, bass.ds(o, P)],
                                                      start=(k == 0), stop=(k == KT - 1))
                            mm.then_inc(sem("pc_mm"), 1)
                            pe.wait_ge(sem("pc_taken"), n + 1)
                with pe.Fori(0 if m else TT * PIECES, units) as n:
                    unit(n)
                pe.wait_ge(sem(p + "y"), units + 1)
                pe.wait_ge(sem(p + "pgT"), units * 2 + 2)
                tokens_out()
                nc.tensor.transpose(ps[:, 6, 0:P], ident, ident).then_inc(sem(f"m{m + 1}_scattered"), 1)

            pe.wait_ge(sem("hc_ready"), TT)
            for j in range(4):
                turn("hTc", j, quarter(cx[:, j // 2, :], j % 2))
            pe.wait_ge(sem("h1_ready"), TT)
            for j in range(4):
                turn("hT", j, quarter(xs[:, j // 2, :], j % 2))
            route(0, tT, wr1, "hT")
            pe.wait_ge(sem("freed_dve"), outs.emptied("tb1", "dve"))
            mixture(0, xs)

            pe.wait_ge(sem("m1_sums_read"), TT)
            for j in range(4):
                spread("mb", j, j // 2, j % 2, 0)
            for tt in range(TT):
                dst = bank("pc", tt)
                for k in range(KT):
                    mm = nc.tensor.matmul(dst[:, 0:160], hTc[:, k, P * tt:P * tt + P], w_in2[:, k, O_KV:O_RQ],
                                          start=(k == 0), stop=(k == KT - 1))
                mm.then_inc(filled, 1)
            for j in range(4):
                if j % 2 == 0:
                    pe.wait_ge(sem("hn_ready"), j // 2 + 1)
                turn("hT4", j, quarter(hn[:, j // 2, :], j % 2))
            pe.wait_ge(freed_act, outs.emptied("hT4", "act"))

            def project(j):
                (o, w), tt = PX[j // 2], j % 2
                dst = bank("px", j)
                for k in range(KT):
                    mm = nc.tensor.matmul(dst[:, 0:w], hTc[:, k, P * tt:P * tt + P], w_in2[:, k, o:o + w],
                                          start=(k == 0), stop=(k == KT - 1))
                mm.then_inc(filled, 1)

            def keys_values(j):
                nc.tensor.matmul(bank("kv", j), cT[:, j // 2, :], wkvu[:, 512 * (j % 2):512 * (j % 2) + 512],
                                 start=True, stop=True).then_inc(filled, 1)

            project(0)
            project(1)
            pe.wait_ge(sem("latents"), TT)
            turn("cT", 0, [cn_[:, 0:P], cn_[:, P:2 * P]])
            project(2)
            pe.wait_ge(sem("latents"), 3 * TT)
            turn("cT", 1, [cn_[:, 2 * P:3 * P], cn_[:, 3 * P:4 * P]])
            turn("cT", 2, quarter(cn_, 1))
            pe.wait_ge(freed_act, outs.nth[outs.at["cT"][0]])
            pe.wait_ge(sem("ld_latent"), 48)
            for j in range(8):
                if j == 4:
                    pe.wait_ge(freed_act, outs.emptied("cT", "act"))
                keys_values(j)
            pe.wait_ge(sem("ld_latent"), 48)
            for j in range(4):
                tt, h = j // 2, j % 2
                dst = bank("qu", j)
                for k in range(2):
                    mm = nc.tensor.matmul(dst[:, 0:4 * QK], cT[:, 4 + 2 * tt + k, :], wqu[:, k, 4 * QK * h:4 * QK * (h + 1)],
                                          start=(k == 0), stop=(k == 1))
                mm.then_inc(filled, 1)
            project(3)
            project(4)
            project(5)
            pe.wait_ge(sem("roped_r"), 1)
            for tt in range(TT):
                turn("rT", tt, [px[:, tt, O_RQ + P * i:O_RQ + P * i + P] for i in range(4)])
            turn("rT", 2, [pc[:, i % 2, 160 + P * (i // 2):160 + P * (i // 2) + P] for i in range(4)])
            project(6)
            project(7)
            pe.wait_ge(freed_act, outs.emptied("rT", "act"))
            for j in range(2 * RH):
                h, half = j // 2, j % 2
                r = slice(64 * (h % 2), 64 * (h % 2) + 64)
                dst = bank("rs", j)
                for i in range(2):
                    k = 2 * half + i
                    mm = nc.tensor.matmul(dst[:, S * i:S * i + S], rkT[r, h // 2, P * k:P * k + P], rqT[r, h // 2, :],
                                          start=True, stop=True)
                mm.then_inc(filled, 1)
            pe.wait_ge(sem("kq_ready"), 1)
            for j in range(12):
                tile, h = j // 2, j % 2
                x = K2[:, tile] if tile < 4 else Q2[:, tile - 4]
                turn("kqT", j, [x[:, 4 * h + i, :] for i in range(4)])
            pe.wait_ge(sem("freed_dve"), outs.emptied("rs", "dve"))
            pe.wait_ge(freed_act, outs.emptied("px", "act"))
            vals = [pc[:, 0, 416:928], pc[:, 1, 416:928], px[:, 0, O_RV:O_RG], px[:, 1, O_RV:O_RG]]
            for tt in range(TT):
                dst = bank("ro", tt)
                for h in range(RH):
                    for k in range(4):
                        mm = nc.tensor.matmul(dst[:, P * h:P * h + P], sd[:, h, k, P * tt:P * tt + P],
                                              vals[k][:, RDV * h:RDV * h + RDV], start=(k == 0), stop=(k == 3))
                mm.then_inc(filled, 1)
            pe.wait_ge(freed_act, outs.emptied("kqT", "act"))

            def scores(h):
                for qt in range(TT):
                    nc.tensor.matmul(bank("s2", 2 * h + qt), qT2[:, h, P * qt:P * qt + P], kT2[:, h, :],
                                     start=True, stop=True).then_inc(filled, 1)

            def turn_weights(h):
                for qt in range(TT):
                    s = 2 * h + qt
                    pe.wait_ge(sem("E2_ready"), s + 1)
                    turn("eT", s, quarter(E2[:, s, :], 0))

            def head_out(h):
                pe.wait_ge(sem("freed_dve"), outs.nth[outs.at["eT"][2 * h + 1]])
                m, j = h // 4, h // 2
                dst = ps[64 * (h % 2):64 * (h % 2) + 64, 6 + m, S * (j % 2):S * (j % 2) + S]
                for k in range(4):
                    mm = nc.tensor.matmul(dst, V2[:, k, 64 * h:64 * h + 64], ET2[:, h % 4, k, :], start=(k == 0), stop=(k == 3))
                mm.then_inc(sem("oT2_head"), 1)
                if h % 4 == 3:
                    pe.wait_ge(sem("oT2_head"), h + 1)
                    pe.sem_inc(sem("oT2_mm"), 1)

            for h in range(MH + 3):
                if h < MH:
                    scores(h)
                if h == 0:
                    for j in range(6):
                        spread("mb2", j, 2 + j // 2, j % 2, 0)
                if h == MH + 1:
                    pe.wait_ge(sem("ro_ready"), TT)
                    for tt in range(TT):
                        turn("rmT", tt, quarter(ro[:, tt, :], 0))
                if 2 <= h < MH + 2:
                    turn_weights(h - 2)
                if h >= 3:
                    head_out(h - 3)
            pe.wait_ge(freed_act, outs.emptied("rmT", "act"))
            pe.wait_ge(sem("oT2_taken"), 2)
            pe.wait_ge(sem("ld_wo2"), 16)
            for j in range(4):
                tt, h = j // 2, j % 2
                dst = bank("wo2", j)
                for k in range(KT):
                    mm = nc.tensor.matmul(dst, mixT2[:, k, P * tt:P * tt + P], wo2_w[:, k, 512 * h:512 * h + 512],
                                          start=(k == 0), stop=(k == KT - 1))
                mm.then_inc(filled, 1)
            pe.wait_ge(sem("hf_part"), 1)
            for j in range(4):
                if j == 2:
                    pe.wait_ge(sem("hf_ready"), 1)
                turn("hfT", j, quarter(hf[:, j // 2, :], j % 2))
            route(1, hfT, wr2, "hfT")
            pe.wait_ge(sem("freed_dve"), outs.emptied("tb2", "dve"))
            mixture(1, hf)
            for h in range(2):
                c = 2 * 5 + h
                nc.tensor.matmul(ps[:, 6 + h, :], ident[:, 32 * (c % 4):32 * (c % 4) + 1].to_broadcast([P, P]),
                                 modrow[:, c // 4, :], start=True, stop=True).then_inc(sem("mb5_mm"), 1)


def kernel(**inputs):
    import concourse.bacc as _bacc
    from concourse.bass_utils import run_bass_kernel_spmd as _run

    a = {k: np.asarray(v) for k, v in inputs.items()}
    const_at, (consts, early, masks), decay = host_constants()
    arrays = {
        "consts": consts, "early": early, "masks": masks, "decay": decay,
        "x": a["x"][0], "pos": a["positions"][0].reshape(TT, P).T,
        "w_in": a["w_in"][0],
        "vec1": np.concatenate([a["sgu_ln_g"][0], a["sgu_ln_b"][0], a["ln1_g"][0], a["ln1_b"][0], a["ln2_g"][0],
                                a["ln2_b"][0]]),
        "w_spatial": a["w_spatial"][0], "b_spatial": a["b_spatial"][0], "w_out": a["w_out"][0],
        "wr1": np.concatenate([a["w_group"][0], a["w_expert"][0].transpose(1, 0, 2).reshape(D, NE)], 1),
        "rb1": np.concatenate([a["b_group"][0], a["b_expert"][0].reshape(NE)]),
        "w_gate_up": a["w_gate_up"][0].reshape(NE, D, 2 * FF1), "w_down": a["w_down"][0].reshape(NE, FF1, D),
        "cc": np.concatenate([a["c_2"][0].reshape(KT, P), a["c_ctx_2"].reshape(KT, P)], 0),
        "ctx": a["ctx_2"][0], "w_ada_2": a["w_ada_2"][0], "b_ada": a["b_ada_2"][0].reshape(3, 4, 512),
        "w_in_2": a["w_in_2"][0],
        "vec2": np.concatenate([a["g_attn_2"][0], a["g_ffn_2"][0], a["g_q_lora_2"][0], a["g_kv_lora_2"][0],
                                a["g_q_head_2"][0], a["g_k_head_2"][0], a["g_ret_out_2"][0]]),
        "w_q_up_2": a["w_q_up_2"][0], "w_kv_up_2": a["w_kv_up_2"][0],
        "decay_logit": a["ret_decay_logit_2"][0].reshape(2 * RH), "w_out_2": a["w_out_2"][0],
        "wr2": a["w_router_2"][0], "rb2": a["b_router_2"][0],
        "w_mlp1_2": a["w_mlp1_2"][0], "b_mlp1_2": a["b_mlp1_2"][0], "w_mlp2_2": a["w_mlp2_2"][0],
        "b_mlp2_2": a["b_mlp2_2"][0],
    }
    arrays = {f"in_{k}": np.ascontiguousarray(v) for k, v in arrays.items()}
    nc = _bacc.Bacc("TRN2", target_bir_lowering=False, num_devices=1)
    t = {k[3:]: nc.dram_tensor(k, v.shape, mybir.dt.from_np(v.dtype), kind="ExternalInput").ap() for k, v in arrays.items()}
    out = nc.dram_tensor("out_x", (S, D), F32, kind="ExternalOutput").ap()
    build(nc, t, out, const_at)
    r = _run(nc, [arrays], core_ids=[0])
    return r.results[0]["out_x"].reshape(1, S, D)
```

```python
from contextlib import ExitStack

import numpy as np

import concourse.bass as bass
from concourse import mybir

ALU = mybir.AluOpType
ACT = mybir.ActivationFunctionType
AX = mybir.AxisListType.X
F32, BF16, I32, U32 = mybir.dt.float32, mybir.dt.bfloat16, mybir.dt.int32, mybir.dt.uint32

P = 128
S, D = 256, 1024
TT, KT = S // P, D // P
HALF = D // 2
H1, DH1, AW = 8, 64, 512
SG, SGW = 8, 512
ROT1 = 8
NE = 32
FF1 = 256
NGRP, EPG = 4, 8
ALPHA = 2.0 ** 0.25
LN_EPS, RMS_EPS = 1e-5, 1e-6
NEG = -1e30
MH, NOPE, PE_W, MV = 8, 64, 32, 64
QK = NOPE + PE_W
QL, KVL = 256, 128
RH, RDK, RDV = 4, 64, 128
O_KV, O_PE, O_RQ = QL, QL + KVL, QL + KVL + PE_W
O_RK = O_RQ + RH * RDK
O_RV = O_RK + RH * RDK
O_RG = O_RV + RH * RDV
PIN = O_RG + RH * RDV
PIECES = (O_RG - O_RK) // P
CHUNKS = (0, 1, 2, 4, 3)
PX = ((0, O_RQ), (O_RQ, O_RV - O_RQ), (O_RV, RH * RDV), (O_RG, RH * RDV))
CW = O_RQ - O_KV + O_RG - O_RK
FF2 = 1024
LIMIT, SWA = 7.0, 1.702
SLOTS = 64
GROUPS, CAP = (NE // 2, NE), (32, 64)
BLOCKS = tuple(S // c for c in CAP)
TABLE = 52
WARM = 24
SMALL = 560
BANKS = 6


def host_constants():
    f = np.float32
    p = np.arange(P)
    c = {}
    c["ident"] = np.eye(P)
    c["upper"] = p[:, None] < p[None, :]
    c["ones"] = np.ones((P, P))
    c["tri"] = p[:, None] <= p[None, :]
    for t in range(TT):
        dist = (t * P + p)[:, None] - np.arange((t + 1) * P)[None, :]
        causal = dist >= 0
        count = causal * ((dist <= 128) * 1 + (dist % 4 == 0) + (dist % 16 == 0))
        c[f"cnt{t}"] = count
        c[f"neg{t}"] = np.where(count > 0, 0.0, NEG)
    c["iota32"] = np.tile(np.arange(32), (P, 1))
    c["iota64"] = np.tile(np.arange(64), (P, 1))
    for m in range(2):
        block = p % BLOCKS[m]
        c[f"off{m}"] = (CAP[m] * block)[:, None]
        c[f"more{m}"] = np.where(block > 0, CAP[m] * block, -1)[:, None]
        c[f"group{m}"] = (p // BLOCKS[m])[:, None]
        c[f"first{m}"] = p[:, None] == BLOCKS[m] * np.arange(NE)[None, :]
    c["eye3"] = (p[:, None] % 32 == np.arange(32)[None, :]) & (p[:, None] < 96)
    c["pair"] = p[:, None] % 64 == np.arange(NGRP + NE)[None, :]
    c["inv8"] = np.tile(500000.0 ** (-np.arange(8) / 8.0), (P, 1))
    pos = np.arange(S)
    grid = np.stack([pos // 64, pos % 64], -1).astype(f)
    for name, dim in (("M", PE_W), ("R", RDK)):
        nf = dim // 4
        inv = (10000.0 ** (-np.arange(nf) / nf)).astype(f)
        ang = (grid[:, :, None] * inv).astype(f)
        ang = np.broadcast_to(ang[:, :, None, :], (S, 2, 2, nf)).astype(np.float64)
        sign = np.array([-1.0, 1.0])[None, None, :, None]
        c["cos" + name] = np.cos(ang).reshape(TT, P, dim).transpose(1, 0, 2).reshape(P, -1)
        c["sin" + name] = (np.sin(ang) * sign).reshape(TT, P, dim).transpose(1, 0, 2).reshape(P, -1)
    early = ["tri", "cosM", "sinM", "cosR", "sinR"]
    masks = ["cnt0", "neg0", "cnt1", "neg1"]
    groups = [[k for k in c if k not in early + masks], early, masks]
    at, arrays = {}, []
    for i, names in enumerate(groups):
        w = 0
        for k in names:
            at[k] = (i, w, c[k].shape[1])
            w += c[k].shape[1]
        arrays.append(np.ascontiguousarray(np.concatenate([np.asarray(c[k], f) for k in names], 1)))
    kt, i = np.arange(4)[None, :, None], pos[None, None, :]
    j = kt * P + p[:, None, None] - S
    ahead = np.where(j < 0, i - j, np.maximum(i - j, 0))
    behind = np.where(j < 0, 2 * S + j - i, np.maximum(j - i, 0))
    seen_f, seen_b = (i >= j) * 1.0, (j >= i) * 1.0
    decay = np.concatenate([ahead.reshape(P, -1), behind.reshape(P, -1),
                            seen_f[:, 2:].reshape(P, -1), seen_b[:, 2:].reshape(P, -1)], 1).astype(f)
    return at, arrays, decay


class Outputs:

    def __init__(self, plan):
        self.at, self.by, self.nth = {}, [], []
        done = {"act": 0, "dve": 0}
        for name, count, engine in plan:
            first = len(self.by)
            for _ in range(count):
                done[engine] += 1
                self.by.append(engine)
                self.nth.append(done[engine])
            self.at.setdefault(name, []).extend(range(first, first + count))

    def bank(self, name, j):
        return self.at[name][j] % BANKS

    def filled(self, name, j):
        return self.at[name][j] + 1

    def before(self, name, j):
        n = self.at[name][j] - BANKS
        return (self.by[n], self.nth[n]) if n >= 0 else None

    def emptied(self, name, engine):
        last = self.at[name][-1]
        return max([self.nth[n] for n in range(last + 1) if self.by[n] == engine], default=0)


PLAN = (
    [("xT", 4, "act")]
    + [("proj", 5, "act"), ("qkT", 4, "act"), ("proj", 1, "act"), ("ada", 1, "dve"), ("sc", 6, "dve"),
       ("wsT", 2, "dve"), ("bsT", 1, "dve"), ("proj", 2, "act"), ("ada", 1, "dve"), ("proj", 2, "act"),
       ("ada", 1, "dve")]
    + [("z", 2, "dve"), ("ET", 6, "act"), ("mT", 2, "act"), ("mbc", 4, "act"), ("wo", 4, "dve"), ("hTc", 4, "act"),
       ("hT", 4, "act")]
    + [("lp1", 1, "dve"), ("lg1", 1, "dve"), ("cn1", 1, "dve"), ("ps1", 1, "dve"), ("rk1", 1, "dve"), ("tb1", 1, "dve")]
    + [("mb", 4, "act"), ("pc", 2, "act"), ("hT4", 4, "act"), ("px", 2, "act"), ("cT", 1, "act"), ("px", 1, "act"),
       ("cT", 2, "act"), ("kv", 8, "act"), ("qu", 4, "act"), ("px", 3, "act"), ("rT", 3, "act"), ("px", 2, "act")]
    + [("rs", 8, "dve")] + [("kqT", 1, "act"), ("kqT", 1, "dve")] * 6 + [("ro", 2, "dve")]
    + [("s2", 4, "act")] + [("s2", 2, "act"), ("eT", 1, "dve"), ("eT", 1, "act")] * (MH - 2)
    + [("eT", 1, "dve"), ("eT", 1, "act"), ("rmT", 2, "act"), ("eT", 1, "dve"), ("eT", 1, "act")]
    + [("mb2", 2, "act"), ("wo2", 4, "dve"), ("mb2", 4, "dve"), ("hfT", 4, "act"), ("mb5", 2, "act")]
    + [("lp2", 1, "dve"), ("lg2", 1, "dve"), ("cn2", 1, "dve"), ("ps2", 1, "dve"), ("rk2", 1, "dve"), ("tb2", 1, "dve")]
)


def build(nc, t, out, const_at):
    ctx = ExitStack()
    with ctx:
        def sb(name, shape, dt=F32):
            return ctx.enter_context(nc.sbuf_tensor(name, shape, dt))

        sems = {}

        def sem(name):
            if name not in sems:
                sems[name] = ctx.enter_context(nc.semaphore(name))
            return sems[name]

        outs = Outputs(PLAN)
        ps = ctx.enter_context(nc.psum_tensor("ps", [P, 8, 512], F32))

        wbig = sb("wbig", [P, 24576])
        wfront = sb("wfront", [P, 16384])
        xs = sb("xs", [P, TT, D])
        tT = sb("tT", [P, KT, S])
        act_ = sb("act_", [P, 5120])
        consts = sb("consts", [P, t["consts"].shape[1]])
        modrow = sb("modrow", [P, 3, 512])
        small = sb("small", [P, SMALL])
        pos_i = sb("pos_i", [P, TT], I32)
        idx_u = sb("idx_u", [P, TT, 8], U32)
        table = sb("table", [P, TABLE + 1 + NE], I32)

        def const(name):
            i, o, w = const_at[name]
            return (consts[:, :], wbig[:, 23744:24256], wbig[:, 3072:3840])[i][:, o:o + w]

        ident = const("ident")
        ones = const("ones")

        free_small = [0]

        def cols(w):
            o = free_small[0]
            free_small[0] += w
            assert free_small[0] <= SMALL, free_small
            return small[:, o:o + w]

        def three(ap, n):
            return ap.rearrange("p (t c) -> p t c", t=n)

        w_in = three(wbig[:, 0:5 * 4096], 5)
        sgu_v = wbig[:, 20480:21504]
        w_sp = wbig[:, 21504:22528]
        b_sp = wbig[0:SG, 22528:22656]
        ln1_v = wbig[:, 4096:6144]
        ln2_v = wbig[:, 14336:16384]
        cx = three(wbig[:, 16384:18432], TT)
        mbc = wbig[:, 18432:20480].rearrange("p (v c) -> p v c", v=2)
        g_at1 = wbig[:, 7168:8192]
        hTc = wbig[:, 12288:14336].rearrange("p (k q) -> p k q", k=KT)
        ada = wfront[:, :].rearrange("p (k c) -> p k c", k=KT)
        wo_w = wfront[:, 0:8192].rearrange("p (k c) -> p k c", k=KT)
        qkT = wbig[:, 0:2048].rearrange("p (k q) -> p k q", k=KT)
        E0 = wbig[:, 2048:3072].rearrange("p (h k) -> p h k", h=H1)
        E1 = wbig[:, 4096:6144].rearrange("p (h k) -> p h k", h=H1)
        ET = wbig[:, 8192:12288].rearrange("p (k h q) -> p k h q", k=TT, h=H1)
        qk = three(act_[:, 0:2048], TT)
        mixT = act_[:, 0:2048].rearrange("p (k q) -> p k q", k=KT)
        v1 = three(act_[:, 2048:3072], TT)
        u1 = three(act_[:, 3072:4096], TT)
        vs1 = three(act_[:, 4096:5120], TT)
        wsT = wbig[:, 6144:7168].rearrange("p (g t) -> p g t", g=SG)
        wr1 = wbig[:, 22656:22944].rearrange("p (k c) -> p k c", k=KT)
        wr2 = wbig[:, 23104:23360].rearrange("p (k c) -> p k c", k=KT)
        ccT = wbig[:, 23360:23616].rearrange("p (k c) -> p k c", k=KT)
        cc = wbig[0:16, 23616:23744]
        rb1 = cols(NGRP + NE)
        rb2 = cols(NE)

        gu_w = wbig[:, 0:8192].rearrange("p (q k h c f) -> p q k h c f", q=2, k=KT, h=2, c=2)
        dn_w = wbig[:, 8192:12288].rearrange("p (q k f) -> p q k f", q=2, k=FF1 // P)
        w1_w = wbig[:, 0:16384].rearrange("p (k f) -> p k f", k=KT)
        w2_w = wbig[:, 16384:24576].rearrange("p (k f) -> p k f", k=FF2 // P)
        m_at = [0]

        def mbuf(w):
            o = m_at[0]
            m_at[0] += w
            assert m_at[0] <= 5120
            return act_[:, o:o + w]

        xg, xgT, m_t, m_l, m_s, m_a, m_aT, m_y = (mbuf(512) for _ in range(8))
        pgT = [mbuf(256), mbuf(256)]
        hot = mbuf(TT * SLOTS).rearrange("p (t s) -> p t s", t=TT)
        hotg = mbuf(TT * 2 * SLOTS).rearrange("p (t d s) -> p t d s", t=TT, d=2)
        keyc, gatec = mbuf(4), mbuf(4)

        logit_parts = act_[:, 512:512 + S]

        def row_sel(q, tt):
            return act_[:, 256 * q + P * tt:256 * q + P * tt + P]

        bsel = [wfront[0:96, 1536 + 32 * i:1568 + 32 * i].bitcast(BF16) for i in range(2)]
        b1p = wfront[0:96, 0:FF2].bitcast(BF16)
        b2p = wfront[0:96, FF2:FF2 + HALF].bitcast(BF16)
        braw = wfront[0:96, 1600:1600 + 3072]
        bpart = wfront[0:96, 4672:4672 + 1536].bitcast(BF16)
        gated = wfront[:, 6208:8192]

        mb = act_[:, 2048:4096].rearrange("p (v c) -> p v c", v=2)
        hn = three(act_[:, 0:2048], TT)
        sq = act_[:, 4096:5120]
        px = three(wbig[:, 0:TT * PIN], TT)
        pc = three(tT[:, :, :].rearrange("p k q -> p (k q)")[:, 0:TT * CW], TT)
        K2 = wbig[:, 3904:3904 + 4 * MH * QK].rearrange("p (t h e) -> p t h e", t=4, h=MH)
        kT2 = wbig[0:QK, 12288:16384].rearrange("p (h k) -> p h k", h=MH)
        qT2 = wbig[0:QK, 10240:12288].rearrange("p (h q) -> p h q", h=MH)
        Q2 = act_[:, 0:TT * MH * QK].rearrange("p (t h e) -> p t h e", t=TT, h=MH)
        V2 = act_[:, 1536:3584].rearrange("p (t c) -> p t c", t=4)
        cn_ = act_[:, 3584:4608]
        cT = wbig[:, 16384:17408].rearrange("p (b q) -> p b q", b=8)
        vec2_at = 16384
        g_at = wbig[:, vec2_at:vec2_at + 1024]
        g_ff = wbig[:, vec2_at + 1024:vec2_at + 2048]
        g_ql = wbig[:, vec2_at + 2048:vec2_at + 2304]
        g_kvl = wbig[:, vec2_at + 2304:vec2_at + 2432]
        g_qh = wbig[:, vec2_at + 2432:vec2_at + 2528]
        g_kh = wbig[:, vec2_at + 2528:vec2_at + 2624]
        g_ro = wbig[:, vec2_at + 2624:vec2_at + 3136]
        VEC2 = 3136
        wqu = wbig[:, 19520:21056].rearrange("p (k c) -> p k c", k=2)
        wkvu = wbig[:, 21056:22080]
        mb2 = wbig[:, 22080:23104]
        mb4 = act_[:, 3584:4608]
        w_in2 = wfront[:, 0:KT * PIN].rearrange("p (k c) -> p k c", k=KT)
        dext = [wbig[:, 10240 + 1024 * h + (h // 2) * 2048:][:, 0:1024].rearrange("p (k q) -> p k q", k=4) for h in range(RH)]
        decay = wbig[:, 6976:10048]
        dtmp = wbig[:, 0:4096].rearrange("p (h q) -> p h q", h=RH)
        E2 = wfront[:, 0:8192].rearrange("p (s k) -> p s k", s=2 * MH)
        wo2_w = wfront[:, 8192:16384].rearrange("p (k c) -> p k c", k=KT)
        ET2 = wbig[:, 0:4096].rearrange("p (s k q) -> p s k q", s=4, k=4)
        sd = wfront[:, 0:4096].rearrange("p (h k q) -> p h k q", h=RH, k=4)
        rT = act_[:, 3584:5120]
        rqT = rT[:, 0:512].rearrange("p (b q) -> p b q", b=2)
        rkT = rT[:, 512:1536].rearrange("p (b k) -> p b k", b=2)
        ro = wbig[:, 6976:8000].rearrange("p (t c) -> p t c", t=TT)
        mixT2 = wbig[:, 8000:10048].rearrange("p (k q) -> p k q", k=KT)
        scr = wbig[:, 6976:10048]
        scr_l = wfront[:, 15616:16384]
        hf = tT[:, :, :].rearrange("p k q -> p (k q)").rearrange("p (t c) -> p t c", t=TT)
        def turned_heads(j):
            tile, h = j // 2, j % 2
            x, at = (kT2, P * tile) if tile < 4 else (qT2, P * (tile - 4))
            return x[:, 4 * h:4 * h + 4, at:at + P]

        mb5 = wfront[:, 8192:9216]
        hfT = act_[:, 1536:3584].rearrange("p (k q) -> p k q", k=KT)
        lgam = cols(2 * RH)
        lgt = cols(4 * 2 * RH)
        rg = wbig[:, 9024:10048].rearrange("p (t c) -> p t c", t=TT)
        rsq = lgt[:, 8:8 + TT * RH]
        ro_sq = scr[:, 1024:2048]
        scr_p = scr[:, 1536:2560]

        stats, mv = cols(12), cols(2 * TT)
        rstd = cols(64)
        ssum = cols(64)
        hn_rstd, eps = rstd[:, 32:34], rstd[:, 34:35]
        cs1 = cols(TT * 2 * ROT1).rearrange("p (f t e) -> p f t e", f=2, t=TT)
        rot = cols(5 * TT * ROT1)
        mx, mneg = cols(16), cols(16)
        lg = cols(TT * 36).rearrange("p (t c) -> p t c", t=TT)
        g8 = cols(TT * 8).rearrange("p (t c) -> p t c", t=TT)
        top8 = cols(TT * 8).rearrange("p (t c) -> p t c", t=TT)
        idxf = cols(TT * 8).rearrange("p (t c) -> p t c", t=TT)
        topw = cols(TT * 4).rearrange("p (t c) -> p t c", t=TT)
        psel = cols(TT)
        goh = cols(TT * NGRP).rearrange("p (t c) -> p t c", t=TT)
        spare = wfront[:, 15616:16384]
        sel, gate, key, oh = (spare[:, 64 * i:64 * i + 64].rearrange("p (t c) -> p t c", t=TT) for i in range(4))
        place_of = spare[:, 256:256 + TABLE + 2]
        off = spare[:, 320:320 + TABLE]
        flag = cols(2)
        pos_f = cols(TT)

        d_win = t["w_in"].rearrange("(k p) (c f) -> c p k f", p=P, f=512)
        d_ada = t["w_ada_2"].rearrange("(k p) (r f) -> r p k f", p=P, f=4 * 512)
        d_win2 = t["w_in_2"].rearrange("(k p) c -> p k c", p=P)
        W_IN_SPLIT = -(-KT * D // PIN)
        d_gu = t["w_gate_up"].rearrange("e (k p) f -> e p k f", p=P)
        d_dn = t["w_down"].rearrange("e (k p) f -> e p k f", p=P)
        d_w1 = t["w_mlp1_2"].rearrange("e (k p) f -> e k p f", p=P)
        d_w2 = t["w_mlp2_2"].rearrange("e (k p) f -> e k p f", p=P)

        def row(ap, n=P):
            return ap.partition_broadcast(n)

        block = ctx.enter_context(nc.Block())

        @block.sync
        def _(sp):
            def load(dst, src, name):
                sp.dma_start(dst, src).then_inc(sem(name), 16)

            load(consts[:, :], t["consts"], "ld_consts")
            load(wbig[:, 23744:24256], t["early"], "ld_early")
            load(xs[:, :, :], t["x"].rearrange("(t p) d -> p t d", p=P), "ld_x")
            load(cc, t["cc"], "ld_cc")

            def load_w_in(c):
                load(w_in[:, c, :].rearrange("p (k f) -> p k f", k=KT), d_win[c], f"ld_win{c}")

            def load_ada(i):
                k = KT // 2 * (i % 2)
                load(ada[:, k:k + KT // 2, :], d_ada[i // 2, :, k:k + KT // 2], f"ld_ada{i % 2}")

            for c in CHUNKS[:2]:
                load_w_in(c)
            load(pos_i[:, :], t["pos"], "ld_pos")
            for c in CHUNKS[2:]:
                load_w_in(c)
            sp.wait_ge(sem("filled"), outs.filled("proj", 1))
            load(wbig[:, 3072:3840], t["masks"], "ld_masks")
            load_ada(0)
            load_ada(1)
            load(w_sp.rearrange("p (g s) -> p g s", g=SG), t["w_spatial"].rearrange("g t s -> t g s"), "ld_spatial")
            load(b_sp, t["b_spatial"], "ld_spatial")
            sp.wait_ge(sem("modrow_zeroed"), 1)
            for g in range(4):
                load(modrow[32 * g:32 * g + 2, :, :], row(t["b_ada"][:, g, :], 2), "ld_bada")
            sp.wait_ge(sem("ada_used"), 1)
            load_ada(2)
            load(sgu_v, row(t["vec1"][0:1024]), "ld_small")
            load(rb1, row(t["rb1"]), "ld_small")
            load(rb2, row(t["rb2"]), "ld_small")
            load(wr1, t["wr1"].rearrange("(k p) c -> p k c", p=P), "ld_small")
            load(wr2, t["wr2"].rearrange("(k p) c -> p k c", p=P), "ld_small")
            load(lgt[:, 0:8], row(t["decay_logit"]), "ld_small")
            sp.wait_ge(sem("filled"), outs.filled("ada", 0))
            load_ada(3)
            sp.wait_ge(sem("ada_used"), 2)
            load_ada(4)
            sp.wait_ge(sem("filled"), outs.filled("ada", 1))
            load_ada(5)
            sp.wait_ge(sem("filled"), outs.filled("proj", 7))
            load(cx, t["ctx"].rearrange("(t p) d -> p t d", p=P), "ld_ctx")
            load(g_at1, row(t["vec2"][0:D]), "ld_gat1")
            sp.wait_ge(sem("ada_used"), 3)
            load(wo_w, t["w_out"].rearrange("(k p) c -> p k c", p=P), "ld_wo")
            sp.wait_ge(sem("filled"), outs.filled("proj", 9))
            load(ln2_v, row(t["vec1"][3072:5120]), "ld_ln2")
            sp.wait_ge(sem("filled"), outs.filled("ET", 5))
            load(ln1_v, row(t["vec1"][1024:3072]), "ld_ln1")

            def load_pair(u):
                for q in range(2):
                    e = u * 2 + q
                    for h in range(2):
                        yield (gu_w[:, q, 4 * h:4 * h + 4].rearrange("p k h c f -> p k (h c f)"),
                               d_gu[bass.ds(e, 1), :, 4 * h:4 * h + 4].rearrange("a p k f -> (a p) k f"),
                               f"ld_gu{q}{h}")
                for q in range(2):
                    e = u * 2 + q
                    yield (dn_w[:, q], d_dn[bass.ds(e, 1)].rearrange("a p k f -> (a p) k f"), f"ld_dn{q}")

            first = list(load_pair(0))
            for dst, src, name in first[0:2]:
                load(dst, src, name)
            sp.wait_ge(sem("oT_mm"), 2)
            for dst, src, name in first[4:6]:
                load(dst, src, name)
            sp.wait_ge(sem("filled"), outs.filled("ada", 2))
            load(w_in2[:, W_IN_SPLIT:, :], d_win2[:, W_IN_SPLIT:, :], "ld_w_in_2")
            sp.wait_ge(sem("filled"), outs.filled("wo", 3))
            load(w_in2[:, 0:W_IN_SPLIT, :], d_win2[:, 0:W_IN_SPLIT, :], "ld_w_in_2")
            sp.wait_ge(sem("h1_ready"), TT)
            for dst, src, name in first[2:4]:
                load(dst, src, name)
            sp.wait_ge(sem("filled"), outs.filled("hTc", 3))
            load(wbig[:, vec2_at:vec2_at + VEC2], row(t["vec2"]), "ld_latent")
            load(wqu, t["w_q_up_2"].rearrange("(k p) c -> p k c", p=P), "ld_latent")
            load(wkvu, t["w_kv_up_2"], "ld_latent")

            def unit_before(g):
                return sp.value_load(table[0:1, bass.ds(g + TABLE + 1, 1)], min_val=0, max_val=TABLE - 4)

            sp.wait_ge(sem("table_ready"), 1)
            with sp.Fori(1, GROUPS[0]) as g:
                n = unit_before(g)
                for i, (dst, src, name) in enumerate(load_pair(g)):
                    if i == 0:
                        sp.wait_ge(sem("m1_up_used"), n * 2 + 1)
                    elif i == 2:
                        sp.wait_ge(sem("m1_up_used"), n * 2 + 2)
                    elif i == 4:
                        sp.wait_ge(sem("m1_dn_mm"), n + 1)
                    load(dst, src, name)
            sp.wait_ge(sem("m1_scattered"), TT)
            load(decay, t["decay"], "ld_decay")
            sp.wait_ge(sem("filled"), outs.filled("px", 7))
            load(wo2_w, t["w_out_2"].rearrange("(k p) c -> p k c", p=P), "ld_wo2")

            def load_expert(e):
                for k in range(KT):
                    yield (w1_w[:, k, :], d_w1[bass.ds(e, 1), k].rearrange("a p f -> (a p) f"), f"ld_w1_{k}")
                for k in range(FF2 // P):
                    yield (w2_w[:, k, :], d_w2[bass.ds(e, 1), k].rearrange("a p f -> (a p) f"), f"ld_w2_{k}")

            chunks = list(load_expert(0))

            def load_first(*which):
                for i in which:
                    dst, src, name = chunks[i]
                    load(dst, src, name)

            sp.wait_ge(sem("filled"), outs.filled("kqT", 11))
            load_first(2, 8, 12, 15)
            sp.wait_ge(sem("ro_ready"), TT)
            load_first(10, 11)
            sp.wait_ge(sem("filled"), outs.filled("s2", 2 * MH - 1))
            load_first(5, 6, 7)
            sp.wait_ge(sem("filled"), outs.filled("eT", 2 * MH - 1))
            for i in range(3):
                load(braw[32 * i:32 * i + 32, 0:2 * FF2], t["b_mlp1_2"], "ld_b")
                load(braw[32 * i:32 * i + 32, 2 * FF2:], t["b_mlp2_2"], "ld_b")
            sp.wait_ge(sem("oT2_mm"), 2)
            load_first(0, 1)
            sp.wait_ge(sem("filled"), outs.filled("wo2", 3))
            load_first(3, 4)
            sp.wait_ge(sem("wo2_added"), 4)
            load_first(13)
            sp.wait_ge(sem("hf_ready"), TT)
            load_first(9)
            sp.wait_ge(sem("filled"), outs.filled("lp2", 0))
            load_first(14)

            sp.wait_ge(sem("table_ready"), 2)
            with sp.Fori(1, GROUPS[1]) as e:
                n = unit_before(e)
                for i, (dst, src, name) in enumerate(load_expert(e)):
                    sp.wait_ge(sem("m2_w1_used" if i < KT else "m2_w2_used"), n * KT + (i % KT + 1))
                    load(dst, src, name)
            for tt in range(TT):
                sp.wait_ge(sem("y_ready"), tt + 1)
                sp.dma_start(out[P * tt:P * tt + P, :], xs[:, tt, :]).then_inc(sem("stored"), 16)
            sp.wait_ge(sem("stored"), 16 * TT)

        @block.scalar
        def _(act):
            freed = sem("freed_act")
            emptied = [0]
            steps = [0]

            def step(ins):
                steps[0] += 1
                ins.then_inc(sem("act_step"), 1)
                act.wait_ge(sem("act_step"), steps[0])

            def empty(name, j, dst, view, func=ACT.Copy, **kw):
                act.wait_ge(sem("filled"), outs.filled(name, j))
                src = view(ps[:, outs.bank(name, j), :])
                emptied[0] += 1
                assert emptied[0] == outs.nth[outs.at[name][j]]
                return nc.scalar.activation(dst, src, func, **kw).then_inc(freed, 1)

            roots = [0]

            def root(n):
                roots[0] += 1
                act.wait_ge(sem("var_ready"), roots[0])
                nc.scalar.activation(rstd[:, 0:n], rstd[:, 0:n], ACT.Sqrt).then_inc(sem("root_ready"), 1)

            def four(ap):
                return ap.rearrange("p (b q) -> p b q", b=4)

            def same(ap):
                return ap

            act.wait_ge(sem("ld_cc"), 16)
            nc.scalar.activation(cc, cc, ACT.Silu).then_inc(sem("cc_ready"), 1)
            for j in range(4):
                tt, h = j // 2, j % 2
                empty("xT", j, tT[:, 4 * h:4 * h + 4, P * tt:P * tt + P], four)
            act.wait_ge(sem("angles"), 1)
            nc.scalar.activation(cs1[:, :, :, :].rearrange("p f t e -> p (f t e)"), rot[:, 0:2 * TT * ROT1],
                                 ACT.Sin).then_inc(sem("sincos"), 1)

            def proj_in(j):
                c, tt = CHUNKS[j // 2], j % 2
                if c < 2:
                    dst, f = qk[:, tt, 512 * c:512 * c + 512], ACT.Copy
                elif c == 2:
                    dst, f = v1[:, tt, :], ACT.Copy
                else:
                    dst, f = (u1 if c == 3 else vs1)[:, tt, :], ACT.Gelu
                empty("proj", j, dst, same, f)

            for j in range(5):
                proj_in(j)
            for j in range(4):
                tt, h = j // 2, j % 2
                empty("qkT", j, qkT[:, 4 * h:4 * h + 4, P * tt:P * tt + P], four)
            proj_in(5)
            proj_in(6)
            act.wait_ge(sem("sc_shift"), 2)
            nc.scalar.activation(E0, E0, ACT.Exp).then_inc(sem("sc_exp"), 1)
            nc.scalar.activation(E1, E1, ACT.Exp).then_inc(sem("sc_exp"), 1)
            proj_in(7)
            root(TT)
            proj_in(8)
            proj_in(9)
            for j in range(6):
                (qt, kt), h = ((0, 0), (1, 0), (1, 1))[j // 2], j % 2
                empty("ET", j, ET[:, kt, 4 * h:4 * h + 4, P * qt:P * qt + P], four)
            for m in range(2):
                act.wait_ge(sem("oT_mm"), m + 1)
                nc.scalar.activation(mixT[:, 2 * m:2 * m + 2, :], ps[:, 6 + m, :].rearrange("p (b q) -> p b q", b=2),
                                     ACT.Copy).then_inc(sem("oT_taken"), 1)
            for tt in range(TT):
                empty("mT", tt, mixT[:, 4:8, P * tt:P * tt + P], four)
            for j in range(4):
                empty("mbc", j, mbc[:, j // 2, 512 * (j % 2):512 * (j % 2) + 512], same)
            root(TT)
            act.wait_ge(sem("lg_neg"), 1)
            nc.scalar.activation(lgt[:, 8:16], lgt[:, 8:16], ACT.Exp).then_inc(sem("lg_exp"), 1)
            act.wait_ge(sem("lg_neg"), 2)
            nc.scalar.activation(lgt[:, 24:32], lgt[:, 16:24], ACT.Ln).then_inc(sem("lg_ln"), 1)
            root(1)
            for j in range(4):
                tt, h = j // 2, j % 2
                empty("hTc", j, hTc[:, 4 * h:4 * h + 4, P * tt:P * tt + P], four)
            root(1)
            for j in range(4):
                tt, h = j // 2, j % 2
                empty("hT", j, tT[:, 4 * h:4 * h + 4, P * tt:P * tt + P], four)

            def route_exps(m):
                if m == 0:
                    act.wait_ge(sem("grp_shift"), 1)
                    nc.scalar.activation(g8[:, :, 0:NGRP], g8[:, :, 0:NGRP], ACT.Exp).then_inc(sem("grp_exp"), 1)
                k = 2 if m == 0 else 4
                act.wait_ge(sem("top_shift"), m + 1)
                nc.scalar.activation(topw[:, :, 0:k], topw[:, :, 0:k], ACT.Exp).then_inc(sem("top_exp"), 1)

            def mixture(m):
                p = f"m{m + 1}_"

                def tokens_in(n):
                    act.wait_ge(sem(p + "gathered"), n + 1)
                    nc.scalar.activation(xg, ps[:, 6, :], ACT.Copy).then_inc(sem(p + "xg"), 1)

                def turned_in(n):
                    act.wait_ge(sem(p + "xg_turned"), n + 1)
                    nc.scalar.activation(xgT, ps[:, 6, :], ACT.Copy).then_inc(sem(p + "xgT"), 1)

                act.wait_ge(sem("table_ready"), m + 1)
                last = act.value_load(table[0:1, TABLE:TABLE + 1], min_val=GROUPS[m] - 1, max_val=TABLE - 5)
                tokens_in(0)
                turned_in(0)

                def unit(n, more=True):
                    if m == 0:
                        act.wait_ge(sem(p + "up_mm"), n + 1)
                        nc.scalar.activation(m_s[:, 0:P], ps[:, 4, 0:P], ACT.Silu).then_inc(sem(p + "sig"), 1)
                    else:
                        act.wait_ge(sem(p + "glu"), n + 1)
                        nc.scalar.activation(m_s, m_t, ACT.Sigmoid, scale=SWA).then_inc(sem(p + "sig"), 1)
                    w = P if m == 0 else 512
                    act.wait_ge(sem(p + "a_turned"), n + 1)
                    nc.scalar.activation(m_aT[:, 0:w], ps[:, 4, 0:w], ACT.Copy).then_inc(sem(p + "aT"), 1)
                    act.wait_ge(sem(p + "dn_mm"), n + 1)
                    nc.scalar.activation(m_y, ps[:, 7, :], ACT.Copy).then_inc(sem(p + "y"), 1)
                    if more:
                        tokens_in(n + 1)
                        turned_in(n + 1)

                if m == 0:
                    for tt in range(TT):
                        with act.Fori(PIECES * tt, PIECES * tt + PIECES) as n:
                            unit(n)
                            act.wait_ge(sem("pc_mm"), n + 1)
                            nc.scalar.activation(pc[:, tt, bass.ds((n - PIECES * tt) * P + 160, P)], ps[:, 4, 0:P], ACT.Copy)\
                                .then_inc(sem("pc_taken"), 1)
                with act.Fori(0 if m else TT * PIECES, last) as n:
                    unit(n)
                unit(last, more=False)

            route_exps(0)
            mixture(0)

            for j in range(4):
                empty("mb", j, mb[:, j // 2, 512 * (j % 2):512 * (j % 2) + 512], same)
            root(TT)

            def decay_exps(h):
                nc.scalar.activation(dext[h].rearrange("p k q -> p (k q)"), decay[:, 0:1024], ACT.Exp,
                                     scale=lgam[:, h:h + 1]).then_inc(sem("dext_exp"), 1)
                nc.scalar.activation(dtmp[:, h, :], decay[:, 1024:2048], ACT.Exp,
                                     scale=lgam[:, RH + h:RH + h + 1]).then_inc(sem("dext_exp"), 1)

            act.wait_ge(sem("ld_decay"), 16)
            decay_exps(0)
            decay_exps(1)
            for tt in range(TT):
                empty("pc", tt, pc[:, tt, 0:160], lambda a: a[:, 0:160])
            act.wait_ge(sem("eps_ready"), 1)
            for tt in range(TT):
                act.wait_ge(sem("x1_ready"), tt + 1)
                ins = nc.scalar.activation(hn[:, tt, :], xs[:, tt, :], ACT.Square, accum_out=hn_rstd[:, tt:tt + 1])
            step(ins)
            nc.scalar.activation(hn_rstd, hn_rstd, ACT.Sqrt, scale=1.0 / D, bias=eps).then_inc(sem("hn_root"), 1)
            decay_exps(2)
            decay_exps(3)
            for j in range(4):
                tt, h = j // 2, j % 2
                empty("hT4", j, hTc[:, 4 * h:4 * h + 4, P * tt:P * tt + P], four)

            def px_in(j):
                (o, w), tt = PX[j // 2], j % 2
                if o == O_RG:
                    empty("px", j, rg[:, tt, :], lambda a: a[:, 0:w], ACT.Silu)
                else:
                    empty("px", j, px[:, tt, o:o + w], lambda a: a[:, 0:w])

            def latents_in(j):
                a, b = ((0, 2), (2, 4), (4, 8))[j]
                empty("cT", j, cT[:, a:b, :], lambda p: four(p)[:, 0:b - a, :])

            def kv_in(j):
                tile, h = j // 2, j % 2
                act.wait_ge(sem("filled"), outs.filled("kv", j))
                src = ps[:, outs.bank("kv", j), :].rearrange("p (h e) -> p h e", h=4)
                step(nc.scalar.activation(K2[:, tile, 4 * h:4 * h + 4, 0:NOPE], src[:, :, 0:NOPE], ACT.Copy))
                empty("kv", j, V2[:, tile, 256 * h:256 * h + 256].rearrange("p (h e) -> p h e", h=4),
                      lambda a: a.rearrange("p (h e) -> p h e", h=4)[:, :, NOPE:])

            root(TT)
            act.wait_ge(sem("dext_done"), RH)
            px_in(0)
            px_in(1)
            latents_in(0)
            root(2 * TT)
            px_in(2)
            latents_in(1)
            latents_in(2)
            for j in range(8):
                kv_in(j)
            for j in range(4):
                tt, h = j // 2, j % 2
                empty("qu", j, Q2[:, tt, 4 * h:4 * h + 4, :],
                      lambda a: a[:, 0:4 * QK].rearrange("p (h e) -> p h e", h=4))
            px_in(3)
            root(6 * MH)
            px_in(4)
            px_in(5)
            for tt in range(TT):
                act.wait_ge(sem("filled"), outs.filled("rT", tt))
                b = four(ps[:, outs.bank("rT", tt), :])
                step(nc.scalar.activation(rqT[:, :, P * tt:P * tt + P], b[:, 0:2, :], ACT.Copy))
                empty("rT", tt, rkT[:, :, S + P * tt:S + P * tt + P], lambda a: four(a)[:, 2:4, :], ACT.Copy,
                      scale=RDK ** -0.5)
            empty("rT", 2, rkT[:, :, 0:S], lambda a: a.rearrange("p (b k) -> p b k", b=2), ACT.Copy,
                  scale=RDK ** -0.5)
            px_in(6)
            px_in(7)
            act.wait_ge(sem("dext_used"), 1)
            for j in range(0, 12, 2):
                empty("kqT", j, turned_heads(j), lambda a: four(a)[0:QK])

            def turned_weights(h):
                if h >= 4:
                    act.wait_ge(sem("oT2_pair"), h // 2 - 1)
                empty("eT", 2 * h + 1, ET2[:, h % 4, :, P:2 * P], four)

            def heads_out(m):
                act.wait_ge(sem("oT2_mm"), m + 1)
                nc.scalar.activation(mixT2[:, 2 * m:2 * m + 2, :], ps[:, 6 + m, :].rearrange("p (b q) -> p b q", b=2),
                                     ACT.Copy).then_inc(sem("oT2_taken"), 1)

            for h in range(MH + 2):
                if h < MH:
                    if h == 3:
                        act.wait_ge(sem("ret_var"), 1)
                        nc.scalar.activation(rsq, rsq, ACT.Sqrt).then_inc(sem("ret_root"), 1)
                    for s in (2 * h, 2 * h + 1):
                        act.wait_ge(sem("s2_max"), s + 1)
                        empty("s2", s, E2[:, s, :], same, ACT.Exp, bias=mneg[:, s:s + 1], scale=QK ** -0.5,
                              accum_out=mx[:, s:s + 1])
                if 1 <= h <= MH:
                    s = 2 * h - 1
                    act.wait_ge(sem("E2_scale"), h)
                    nc.scalar.activation(E2[:, s, :], E2[:, s, :], ACT.Copy, scale=rstd[:, s:s + 1])\
                        .then_inc(sem("E2_ready_act"), 1)
                if h == MH + 1:
                    heads_out(0)
                    for tt in range(TT):
                        empty("rmT", tt, mixT2[:, 4:8, P * tt:P * tt + P], four)
                if h >= 2:
                    turned_weights(h - 2)
            for j in range(2):
                empty("mb2", j, mb2[:, 512 * j:512 * j + 512], same)
            heads_out(1)
            root(TT)
            for j in range(4):
                tt, h = j // 2, j % 2
                empty("hfT", j, hfT[:, 4 * h:4 * h + 4, P * tt:P * tt + P], four)
            for j in range(2):
                empty("mb5", j, mb5[:, 512 * j:512 * j + 512], same)
            route_exps(1)
            mixture(1)

        @block.vector
        def _(dve):
            freed = sem("freed_dve")
            count = {}

            def step(ins, name="dve_step"):
                count[name] = count.get(name, 0) + 1
                ins.then_inc(sem(name), 1)
                dve.wait_ge(sem(name), count[name])

            def take(name, j, w=512):
                dve.wait_ge(sem("filled"), outs.filled(name, j))
                return ps[:, outs.bank(name, j), 0:w]

            def emptied(ins, name, j):
                step(ins, "freed_dve")
                assert count["freed_dve"] == outs.nth[outs.at[name][j]]

            def bc(ap, shape, axis):
                return ap.unsqueeze(axis).to_broadcast(shape)

            def inverse_root(n, meanwhile=None):
                step(nc.vector.memset(ssum[:, 63:64], 0.0), "var_ready")
                if meanwhile is not None:
                    meanwhile()
                dve.wait_ge(sem("root_ready"), count["var_ready"])
                step(nc.vector.reciprocal(rstd[:, 0:n], rstd[:, 0:n]))

            def layer_norms(x, g, b, last, before=None):
                halves = x.shape[-1] // 512

                def variance(tt, at):
                    for h in range(halves):
                        step(nc.vector.bn_stats(stats[:, 6 * h:6 * h + 6], x[:, tt, 512 * h:512 * h + 512]))
                    step(nc.vector.bn_aggr(mv[:, 2 * tt:2 * tt + 2], stats[:, 0:6 * halves]))
                    step(nc.vector.tensor_scalar(rstd[:, at:at + 1], mv[:, 2 * tt + 1:2 * tt + 2], LN_EPS, None, ALU.add))

                def normed(tt, at):
                    y = x[:, tt, :]
                    step(nc.vector.tensor_scalar(y, y, mv[:, 2 * tt:2 * tt + 1], rstd[:, at:at + 1], ALU.subtract, ALU.mult))
                    step(nc.vector.tensor_tensor(y, y, g, ALU.mult))
                    step(nc.vector.tensor_tensor(y, y, b, ALU.add), last)

                if before is None:
                    for tt in range(TT):
                        variance(tt, tt)
                    inverse_root(TT)
                    for tt in range(TT):
                        normed(tt, tt)
                else:
                    for tt in range(TT):
                        before(tt)
                        variance(tt, 0)
                        inverse_root(1)
                        normed(tt, 0)

            def mean_sq(x, width, at, lead, scratch):
                dst = rstd[:, at:at + lead]
                sqv = scratch[:, 0:lead * width].rearrange("p (a b) -> p a b", a=lead)
                step(nc.vector.tensor_tensor(sqv, x, x, ALU.mult))
                step(nc.vector.tensor_reduce(dst, sqv, AX, ALU.add))
                step(nc.vector.tensor_scalar(dst, dst, 1.0 / width, RMS_EPS, ALU.mult, ALU.add))

            def mean_sq_row(x, at, scratch):
                dst = rstd[:, at:at + 1]
                step(nc.vector.tensor_tensor_reduce(out=scratch, in0=x, in1=x, scale=1.0 / x.shape[-1], scalar=RMS_EPS,
                                                    op0=ALU.mult, op1=ALU.add, accum_out=dst))

            def modulated(dst, xs_, shift, scale, g, scratch, last):
                step(nc.vector.scalar_tensor_tensor(out=scale, in0=scale, scalar=1.0, in1=g, op0=ALU.add, op1=ALU.mult))
                for tt in range(TT):
                    mean_sq_row(xs_[:, tt, :], tt, scratch)
                inverse_root(TT)
                for tt in range(TT):
                    step(nc.vector.scalar_tensor_tensor(out=dst[:, tt, :], in0=xs_[:, tt, :], scalar=rstd[:, tt:tt + 1],
                                                        in1=scale, op0=ALU.mult, op1=ALU.mult))
                    step(nc.vector.tensor_tensor(dst[:, tt, :], dst[:, tt, :], shift, ALU.add), last)

            def context_norm():
                dve.wait_ge(sem("freed_act"), outs.emptied("mbc", "act"))
                dve.wait_ge(sem("ld_gat1"), 16)
                dve.wait_ge(sem("ld_ctx"), 16)
                modulated(cx, cx, mbc[:, 0, :], mbc[:, 1, :], g_at1, g_at1, "hc_ready")

            def log_decays():
                dve.wait_ge(sem("ld_small"), 96)
                x, e, one, ln = (lgt[:, 8 * i:8 * i + 8] for i in range(4))
                fix = lgam
                step(nc.vector.tensor_scalar(fix, x, -1.0, None, ALU.mult))
                step(nc.vector.tensor_tensor(fix, fix, x, ALU.max))
                step(nc.vector.tensor_scalar(e, fix, -1.0, None, ALU.mult), "lg_neg")
                dve.wait_ge(sem("lg_exp"), 1)
                step(nc.vector.tensor_scalar(one, e, 1.0, None, ALU.add), "lg_neg")
                dve.wait_ge(sem("lg_ln"), 1)
                step(nc.vector.tensor_scalar(fix, one, 1.0, None, ALU.is_equal))
                step(nc.vector.tensor_tensor(ln, ln, fix, ALU.add))
                step(nc.vector.scalar_tensor_tensor(out=one, in0=one, scalar=-1.0, in1=fix, op0=ALU.add, op1=ALU.add))
                step(nc.vector.reciprocal(one, one))
                step(nc.vector.tensor_tensor(ln, ln, e, ALU.mult))
                step(nc.vector.tensor_tensor(ln, ln, one, ALU.mult))
                step(nc.vector.tensor_scalar(fix, x, 0.0, None, ALU.min))
                step(nc.vector.tensor_tensor(lgam, fix, ln, ALU.subtract), "lg_ready")
            step(nc.vector.memset(modrow[:, :, :], 0.0), "modrow_zeroed")
            step(nc.vector.memset(ccT, 0.0))
            dve.wait_ge(sem("ccT_mm"), 1)
            step(nc.vector.tensor_copy(ccT[:, :, 0:2], ps[:, 7, 0:16].rearrange("p (r k) -> p k r", r=2)), "ccT_ready")
            dve.wait_ge(sem("ld_pos"), 16)
            dve.wait_ge(sem("ld_consts"), 16)
            n = TT * ROT1
            two_pi = 2 * np.pi
            p1 = 6.28125
            p2 = float(np.floor((two_pi - p1) * 2 ** 21) / 2 ** 21)
            p3 = two_pi - p1 - p2
            magic = 1.5 * 2 ** 23
            ang, turns, cosang = rot[:, 0:n], rot[:, 2 * n:3 * n], rot[:, n:2 * n]
            step(nc.vector.tensor_copy(pos_f, pos_i[:, :]))
            step(nc.vector.tensor_tensor(three(ang, TT), bc(pos_f, [P, TT, ROT1], 2), bc(const("inv8"), [P, TT, ROT1], 1),
                                         ALU.mult))
            step(nc.vector.tensor_scalar(turns, ang, 1.0 / two_pi, None, ALU.mult))
            step(nc.vector.tensor_scalar(turns, turns, magic, None, ALU.add))
            step(nc.vector.tensor_scalar(turns, turns, -magic, None, ALU.add))
            for part in (p1, p2, p3):
                step(nc.vector.scalar_tensor_tensor(out=ang, in0=turns, scalar=-part, in1=ang, op0=ALU.mult, op1=ALU.add))
            step(nc.vector.tensor_scalar(cosang, ang, np.pi / 2, None, ALU.add))
            step(nc.vector.tensor_scalar(turns, cosang, np.pi, -two_pi, ALU.is_gt, ALU.mult))
            step(nc.vector.tensor_tensor(cosang, cosang, turns, ALU.add))
            lim = float(np.nextafter(np.float32(np.pi), np.float32(0)))
            step(nc.vector.tensor_scalar(rot[:, 0:2 * n], rot[:, 0:2 * n], lim, -lim, ALU.min, ALU.max), "angles")
            dve.wait_ge(sem("sincos"), 1)
            dve.wait_ge(sem("freed_act"), outs.nth[outs.at["proj"][3]])
            heads = qk.rearrange("p t (h e) -> p t h e", e=DH1)
            r1, r2 = heads[:, :, :, 0:ROT1], heads[:, :, :, ROT1:2 * ROT1]
            shape = [P, TT, 16, ROT1]
            sin_b, cos_b = (bc(cs1[:, f], shape, 2) for f in range(2))
            a, b, c2, d = (E0.rearrange("p h k -> p (h k)")[:, 256 * i:256 * (i + 1)]
                           .rearrange("p (t h e) -> p t h e", t=TT, h=16) for i in range(4))
            for dst, x, y in ((a, r1, cos_b), (b, r2, sin_b), (c2, r2, cos_b), (d, r1, sin_b)):
                step(nc.vector.tensor_tensor(dst, x, y, ALU.mult))
            step(nc.vector.tensor_tensor(r1, a, b, ALU.subtract))
            step(nc.vector.tensor_tensor(r2, c2, d, ALU.add), "roped1")

            def modulation_row(r):
                if r == 0:
                    dve.wait_ge(sem("ld_bada"), 64)
                emptied(nc.vector.tensor_tensor(modrow[:, r, :], take("ada", r), modrow[:, r, :], ALU.add), "ada", r)

            modulation_row(0)
            dve.wait_ge(sem("ld_masks"), 16)
            for j in range(6):
                if j < 2:
                    dst, m, hs, w = E0[:, 4 * j:4 * j + 4, :], const("neg0"), 4, P
                else:
                    dst, m, hs, w = E1[:, 2 * (j - 2):2 * (j - 2) + 2, :], const("neg1"), 2, S
                emptied(nc.vector.scalar_tensor_tensor(
                    out=dst, in0=take("sc", j).rearrange("p (h k) -> p h k", h=hs), scalar=DH1 ** -0.5,
                    in1=bc(m, [P, hs, w], 1), op0=ALU.mult, op1=ALU.add), "sc", j)
            dve.wait_ge(sem("ld_early"), 16)
            for j in range(2):
                emptied(nc.vector.tensor_tensor(wsT[:, 4 * j:4 * j + 4, :], take("wsT", j).rearrange("p (g t) -> p g t", g=4),
                                                bc(const("tri"), [P, 4, P], 1), ALU.mult), "wsT", j)
            bsT = ssum[:, 0:SG]
            emptied(nc.vector.tensor_copy(bsT, take("bsT", 0, SG)), "bsT", 0)
            for i, (e, w) in enumerate(((E0, P), (E1, S))):
                m8 = mx[:, 8 * i:8 * i + 8]
                step(nc.vector.tensor_reduce(m8, e, AX, ALU.max))
                step(nc.vector.tensor_tensor(e, e, bc(m8, [P, H1, w], 2), ALU.subtract), "sc_shift")
            for i, (e, w) in enumerate(((E0, P), (E1, S))):
                m8, r8 = mx[:, 8 * i:8 * i + 8], rstd[:, 8 * i:8 * i + 8]
                dve.wait_ge(sem("sc_exp"), i + 1)
                step(nc.vector.tensor_tensor(e, e, bc(const(f"cnt{i}"), [P, H1, w], 1), ALU.mult))
                step(nc.vector.tensor_reduce(m8, e, AX, ALU.add))
                step(nc.vector.reciprocal(r8, m8))
                step(nc.vector.tensor_tensor(e, e, bc(r8, [P, H1, w], 2), ALU.mult), "E_ready")
            modulation_row(1)
            dve.wait_ge(sem("ld_small"), 96)
            dve.wait_ge(sem("freed_act"), outs.nth[outs.at["proj"][7]])
            layer_norms(vs1, sgu_v[:, 0:SGW], sgu_v[:, SGW:], "vs_ready")
            modulation_row(2)
            for j in range(2):
                z = take("z", j).rearrange("p (g c e) -> p c g e", g=4, c=TT)
                for tt in range(TT):
                    dst = vs1[:, tt, 256 * j:256 * j + 256].rearrange("p (g e) -> p g e", g=4)
                    ins = nc.vector.tensor_tensor(dst, z[:, tt], bc(bsT[:, 4 * j:4 * j + 4], [P, 4, 64], 2), ALU.add)
                    if tt == 0:
                        step(ins)
                    else:
                        emptied(ins, "z", j)
            dve.wait_ge(sem("freed_act"), outs.nth[outs.at["proj"][9]])
            step(nc.vector.tensor_tensor(u1, u1, vs1, ALU.mult), "sgu_ready")
            context_norm()
            log_decays()
            dve.wait_ge(sem("ld_x"), 16)

            def residual(tt):
                for j in (2 * tt, 2 * tt + 1):
                    x = xs[:, tt, 512 * (j % 2):512 * (j % 2) + 512]
                    emptied(nc.vector.scalar_tensor_tensor(out=x, in0=x, scalar=ALPHA, in1=take("wo", j), op0=ALU.mult,
                                                           op1=ALU.add), "wo", j)

            dve.wait_ge(sem("ld_ln1"), 16)
            layer_norms(xs, ln1_v[:, 0:D], ln1_v[:, D:], "h1_ready", residual)

            def route(m):
                k = 2 if m == 0 else 4
                w = NGRP + NE if m == 0 else NE
                step(nc.vector.memset(place_of, 0.0))
                step(nc.vector.memset(m_y, 0.0))
                step(nc.vector.memset(pgT[0], 0.0))
                step(nc.vector.memset(pgT[1], 0.0), "zeros_ready")
                step(nc.vector.memset(logit_parts, 0.0))
                src = take(f"lp{m + 1}", 0, S)
                step(nc.vector.tensor_copy(logit_parts[0:w, :], src[0:w, :]))
                emptied(nc.vector.tensor_copy(logit_parts[64:64 + w, :], src[64:64 + w, :]), f"lp{m + 1}", 0)
                dve.wait_ge(sem("ld_small"), 96)
                src = take(f"lg{m + 1}", 0, 2 * 64).rearrange("p (t c) -> p t c", t=TT)[:, :, 0:w]
                emptied(nc.vector.tensor_tensor(lg[:, :, 0:w], src, bc((rb1, rb2)[m], [P, TT, w], 1), ALU.add),
                        f"lg{m + 1}", 0)

                def best(vals):
                    for tt in range(TT):
                        step(nc.vector.max(top8[:, tt, :], vals[:, tt, :]))
                        step(nc.vector.max_index(idx_u[:, tt, :], top8[:, tt, :], vals[:, tt, :]))
                    step(nc.vector.tensor_copy(idxf, idx_u[:, :, :]))

                if m == 0:
                    step(nc.vector.memset(g8, -3e38))
                    step(nc.vector.tensor_copy(g8[:, :, 0:NGRP], lg[:, :, 0:NGRP]))
                    best(g8)
                    step(nc.vector.tensor_tensor(g8[:, :, 0:NGRP], lg[:, :, 0:NGRP],
                                                 top8[:, :, 0:1].to_broadcast([P, TT, NGRP]), ALU.subtract), "grp_shift")
                    step(nc.vector.tensor_tensor(goh, bc(const("iota32")[:, 0:NGRP], [P, TT, NGRP], 1),
                                                 idxf[:, :, 0:1].to_broadcast([P, TT, NGRP]), ALU.is_equal))
                    step(nc.vector.tensor_scalar(goh, goh, -1.0, -NEG, ALU.add, ALU.mult))
                    e4 = lg[:, :, NGRP:].rearrange("p t (g e) -> p t g e", g=NGRP)
                    step(nc.vector.tensor_tensor(e4, e4, bc(goh, [P, TT, NGRP, EPG], 3), ALU.add))
                    logits = lg[:, :, NGRP:]
                else:
                    logits = lg[:, :, 0:NE]
                best(logits)
                shape = [P, TT, k, NE]
                chosen = spare[:, 384:384 + TT * k * NE].rearrange("p (t k c) -> p t k c", t=TT, k=k)
                step(nc.vector.tensor_tensor(chosen, const("iota32").unsqueeze(1).unsqueeze(1).to_broadcast(shape),
                                             bc(idxf[:, :, 0:k], shape, 3), ALU.is_equal))
                step(nc.vector.tensor_reduce(sel, chosen.rearrange("p t k c -> p t c k"), AX, ALU.add))
                for q in range(2 - m):
                    for tt in range(TT):
                        s = sel[:, tt, :].rearrange("p (u q) -> p q u", q=2 - m)[:, q, :]
                        step(nc.vector.tensor_copy(row_sel(q, tt).rearrange("p (u b) -> p u b", b=BLOCKS[m]),
                                                   bc(s, [P, GROUPS[m], BLOCKS[m]], 2)))
                step(nc.vector.memset(flag, 0.0), "sel_ready")
                cn = take(f"cn{m + 1}", 0, 4)
                f0 = flag[:, 0:1]
                if m == 0:
                    step(nc.vector.tensor_copy(f0, cn[:, 2:3]))
                    emptied(nc.vector.tensor_tensor(f0, cn[:, 0:1], f0, ALU.max), "cn1", 0)
                else:
                    emptied(nc.vector.tensor_copy(f0, cn[:, 0:1]), "cn2", 0)
                step(nc.vector.tensor_tensor(f0, f0, const(f"more{m}"), ALU.is_gt))
                step(nc.vector.tensor_copy(flag[:, 1:2], f0), "flags")
                place = rstd[:, 0:1]
                emptied(nc.vector.tensor_copy(place, take(f"ps{m + 1}", 0, 1)), f"ps{m + 1}", 0)
                step(nc.vector.tensor_scalar(place_of[:, 0:TABLE], const("iota64")[:, 0:TABLE], place, f0, ALU.is_equal,
                                             ALU.mult))
                step(nc.vector.tensor_copy(place_of[:, TABLE:TABLE + 1], f0), "places_ready")
                tw = topw[:, :, 0:k]
                step(nc.vector.tensor_tensor(tw, top8[:, :, 0:k], top8[:, :, 0:1].to_broadcast([P, TT, k]), ALU.subtract),
                     "top_shift")
                dve.wait_ge(sem("top_exp"), m + 1)
                if m == 0:
                    dve.wait_ge(sem("grp_exp"), 1)
                    step(nc.vector.tensor_reduce(psel, g8[:, :, 0:NGRP], AX, ALU.add))
                    step(nc.vector.reciprocal(psel, psel))
                den = ssum[:, 0:TT]
                step(nc.vector.tensor_reduce(den, tw, AX, ALU.add))
                step(nc.vector.reciprocal(den, den))
                if m == 0:
                    step(nc.vector.tensor_tensor(den, den, psel, ALU.mult))
                step(nc.vector.tensor_tensor(tw, tw, bc(den, [P, TT, k], 2), ALU.mult))
                step(nc.vector.tensor_tensor(chosen, chosen, bc(tw, shape, 3), ALU.mult))
                step(nc.vector.tensor_reduce(gate, chosen.rearrange("p t k c -> p t c k"), AX, ALU.add))
                rank = take(f"rk{m + 1}", 0, TT * NE).rearrange("p (t c) -> p t c", t=TT)
                emptied(nc.vector.scalar_tensor_tensor(out=key, in0=rank, scalar=1.0, in1=sel, op0=ALU.add, op1=ALU.mult),
                        f"rk{m + 1}", 0)
                step(nc.vector.tensor_scalar(key, key, -1.0, None, ALU.add))
                tb = take(f"tb{m + 1}", 0)
                step(nc.vector.tensor_copy(off, tb[:, 64:64 + TABLE]))
                step(nc.vector.tensor_copy(table[:, 0:TABLE], tb[:, 0:TABLE]))
                step(nc.vector.tensor_scalar(table[:, TABLE:TABLE + 1], tb[:, 128 + TABLE:129 + TABLE], -1.0, None, ALU.add))
                emptied(nc.vector.tensor_scalar(table[:, TABLE + 1:], tb[:, 192:192 + NE], -1.0, None, ALU.add), f"tb{m + 1}", 0)
                step(nc.vector.memset(flag, 0.0), "table_ready")

            def mixture(m):
                p = f"m{m + 1}_"
                w = 2 if m == 0 else 1
                cap = CAP[m]
                FETCH, UNIT = 2, (2, 4)[m]
                kc = keyc[:, 0:TT * w].rearrange("p (t c) -> p t c", t=TT)
                gc = gatec[:, 0:TT * w].rearrange("p (t c) -> p t c", t=TT)
                shape = [P, TT, w, cap]
                h4 = hot.rearrange("p t (c s) -> p t c s", c=w)

                def group_of(n):
                    return dve.value_load(table[0:1, bass.ds(n, 1)], min_val=0, max_val=GROUPS[m] - 1)

                def link(ins, value):
                    ins.then_inc(sem(p + "dve_step"), 1)
                    dve.wait_ge(sem(p + "dve_step"), value)

                def one_hot(n, done):
                    g = group_of(n)
                    link(nc.vector.tensor_scalar(kc, key[:, :, bass.ds(g * w, w)], off[:, bass.ds(n, 1)], None, ALU.subtract),
                         done + 1)
                    link(nc.vector.tensor_copy(gc, gate[:, :, bass.ds(g * w, w)]), done + 2)
                    iota = const("iota64")[:, 0:cap].unsqueeze(1).unsqueeze(1).to_broadcast(shape)
                    nc.vector.tensor_tensor(h4, iota, bc(kc, shape, 3), ALU.is_equal).then_inc(sem(p + "hot"), 1)

                def gates(n):
                    dve.wait_ge(sem(p + "hot"), n + 1)
                    for i in range(2):
                        nc.vector.tensor_tensor(hotg[:, :, i, :].rearrange("p t (c s) -> p t c s", c=w), h4,
                                                bc(gc, shape, 3), ALU.mult).then_inc(sem(p + "hotg"), 1)

                def bias_of(n):
                    nc.vector.tensor_copy(bsel[0], const("eye3")[0:96, bass.ds(group_of(n), 1)].to_broadcast([96, SLOTS]))\
                        .then_inc(sem("m2_bsel1"), 1)

                one_hot(0, 0)
                gates(0)
                if m == 1:
                    bias_of(0)
                dve.wait_ge(sem(p + "gathered"), 1)
                dve.wait_ge(sem(p + "hotg"), 2)
                one_hot(1, FETCH)
                last = dve.value_load(table[0:1, TABLE:TABLE + 1], min_val=GROUPS[m] - 1, max_val=TABLE - 5)

                def unit(n, more=True):
                    done = n * UNIT + 2 * FETCH
                    dve.wait_ge(sem(p + "up_mm"), n + 1)
                    if m == 0:
                        dve.wait_ge(sem(p + "sig"), n + 1)
                        nc.vector.tensor_tensor(m_a[:, 0:P], m_s[:, 0:P], ps[:, 4, P:2 * P], ALU.mult)\
                            .then_inc(sem(p + "act"), 1)
                    else:
                        uu = ps[:, 4:6, :].rearrange("p b (f g) -> p (b f) g", g=2)
                        nc.vector.tensor_scalar(m_t, uu[:, :, 0], LIMIT, None, ALU.min).then_inc(sem(p + "glu"), 1)
                        link(nc.vector.tensor_scalar(m_l, uu[:, :, 1], LIMIT, -LIMIT, ALU.min, ALU.max), done + 1)
                        dve.wait_ge(sem(p + "glu"), n + 1)
                        link(nc.vector.scalar_tensor_tensor(out=m_l, in0=m_l, scalar=1.0, in1=m_t, op0=ALU.add, op1=ALU.mult),
                             done + 2)
                        dve.wait_ge(sem(p + "sig"), n + 1)
                        nc.vector.tensor_tensor(m_a, m_l, m_s, ALU.mult).then_inc(sem(p + "act"), 1)
                        dve.wait_ge(sem("m2_bsel1"), n + 1)
                        nc.vector.tensor_copy(bsel[1], bsel[0]).then_inc(sem("m2_bsel2"), 1)
                        dve.wait_ge(sem("m2_bsel2"), n + 1)
                    dve.wait_ge(sem(p + "hot_turned"), n + 1)
                    for i in range(2):
                        h = slice(64 * i, 64 * i + 64)
                        nc.vector.tensor_copy(pgT[i][h, :], ps[h, 5, 0:2 * P]).then_inc(sem(p + "pgT"), 1)
                    if more:
                        gates(n + 1)
                        if m == 1:
                            bias_of(n + 1)
                        dve.wait_ge(sem(p + "gathered"), n + 2)
                        dve.wait_ge(sem(p + "hotg"), n * 2 + 4)
                        one_hot(n + 2, done + (UNIT - FETCH))

                with dve.Fori(0, last) as n:
                    unit(n)
                unit(last, more=False)

            route(0)
            mixture(0)
            step(nc.vector.memset(eps, RMS_EPS), "eps_ready")
            for tt in range(TT):
                dve.wait_ge(sem("m1_scattered"), tt + 1)
                x = xs[:, tt, :]
                step(nc.vector.scalar_tensor_tensor(out=x, in0=x, scalar=ALPHA,
                                                    in1=ps[:, 2 * tt:2 * tt + 2, :].rearrange("p b c -> p (b c)"),
                                                    op0=ALU.mult, op1=ALU.add), "m1_sums_read")
            dve.wait_ge(sem("ld_ln2"), 16)
            layer_norms(xs, ln2_v[:, 0:D], ln2_v[:, D:], "x1_ready")

            dve.wait_ge(sem("hn_root"), 1)
            step(nc.vector.reciprocal(hn_rstd, hn_rstd))
            dve.wait_ge(sem("mb_ready"), 1)
            for tt in range(TT):
                step(nc.vector.scalar_tensor_tensor(out=hn[:, tt, :], in0=xs[:, tt, :], scalar=hn_rstd[:, tt:tt + 1],
                                                    in1=mb[:, 1, :], op0=ALU.mult, op1=ALU.mult))
                step(nc.vector.tensor_tensor(hn[:, tt, :], hn[:, tt, :], mb[:, 0, :], ALU.add), "hn_ready")
            dve.wait_ge(sem("ld_latent"), 48)

            def normed(x, at, g, o):
                w = x.shape[-1]
                step(nc.vector.scalar_tensor_tensor(out=cn_[:, o:o + w], in0=x, scalar=rstd[:, at:at + 1], in1=g,
                                                    op0=ALU.mult, op1=ALU.mult), "latents")

            dve.wait_ge(sem("freed_act"), outs.emptied("pc", "act"))
            for tt in range(TT):
                mean_sq_row(pc[:, tt, 0:KVL], tt, scr_l[:, 0:KVL])
            inverse_root(TT)
            for tt in range(TT):
                normed(pc[:, tt, 0:KVL], tt, g_kvl, KVL * tt)
            dve.wait_ge(sem("freed_act"), outs.nth[outs.at["px"][1]])
            for tt in range(TT):
                mean_sq_row(px[:, tt, O_KV:O_PE], tt, scr_l[:, 0:KVL])
                mean_sq_row(px[:, tt, 0:QL], TT + tt, scr_l[:, 0:QL])
            inverse_root(2 * TT)
            for tt in range(TT):
                normed(px[:, tt, O_KV:O_PE], tt, g_kvl, KVL * (TT + tt))
            for tt in range(TT):
                normed(px[:, tt, 0:QL], TT + tt, g_ql, 512 + QL * tt)
            def axial(x, heads, dim, name, last):
                nf = dim // 4
                cosv, sinv = (three(const(k + name), TT) for k in ("cos", "sin"))
                tmp = scr[:, 0:TT * heads * dim].rearrange("p (t h e) -> p t h e", t=TT, h=heads)
                for s in range(2):
                    for ax in range(2):
                        o, i = 2 * nf * ax + nf * s, 2 * nf * ax + nf * (1 - s)
                        step(nc.vector.tensor_tensor(tmp[:, :, :, o:o + nf], x[:, :, :, i:i + nf],
                                                     bc(sinv[:, :, o:o + nf], [P, TT, heads, nf], 2), ALU.mult))
                step(nc.vector.tensor_tensor(x, x, bc(cosv, [P, TT, heads, dim], 2), ALU.mult))
                step(nc.vector.tensor_tensor(x, x, tmp, ALU.add), last)

            def heads_of(x):
                return x.rearrange("p t h e -> p (t h) e")

            def head_norm(x, at, g):
                n = TT * MH
                step(nc.vector.tensor_tensor(x, x, bc(rstd[:, at:at + n], [P, n, QK], 2), ALU.mult))
                step(nc.vector.tensor_tensor(x, x, bc(g, [P, n, QK], 1), ALU.mult))

            Kc, Kx, Qx = heads_of(K2[:, 0:2]), heads_of(K2[:, 2:4]), heads_of(Q2)
            dve.wait_ge(sem("dext_done"), RH)
            dve.wait_ge(sem("freed_act"), outs.nth[outs.at["kv"][3]])
            step(nc.vector.tensor_copy(K2[:, 0:2, :, NOPE:QK], bc(pc[:, :, KVL:KVL + PE_W], [P, TT, MH, PE_W], 2)))
            mean_sq(Kc, QK, 0, 2 * MH, scr)
            dve.wait_ge(sem("freed_act"), outs.nth[outs.at["kv"][7]])
            step(nc.vector.tensor_copy(K2[:, 2:4, :, NOPE:QK], bc(px[:, :, O_PE:O_RQ], [P, TT, MH, PE_W], 2)))
            mean_sq(Kx, QK, 2 * MH, 2 * MH, scr)
            dve.wait_ge(sem("freed_act"), outs.emptied("qu", "act"))
            mean_sq(Qx, QK, 4 * MH, 2 * MH, scr)
            inverse_root(6 * MH)
            head_norm(Kc, 0, g_kh)
            head_norm(Kx, 2 * MH, g_kh)
            head_norm(Qx, 4 * MH, g_qh)
            axial(K2[:, 2:4, :, NOPE:QK], MH, PE_W, "M", "dve_step")
            axial(Q2[:, :, :, NOPE:QK], MH, PE_W, "M", "dve_step")
            step(nc.vector.memset(ssum[:, 32:33], 0.0), "kq_ready")
            for j in range(2 * RH):
                h, half = j // 2, j % 2
                d = dext[h][:, 2 * half:2 * half + 2, :].rearrange("p k q -> p (k q)")
                emptied(nc.vector.tensor_tensor(sd[:, h, 2 * half:2 * half + 2, :].rearrange("p k q -> p (k q)"),
                                                take("rs", j), d, ALU.mult), "rs", j)
            step(nc.vector.memset(ssum[:, 32:33], 0.0), "dext_used")
            for j in range(1, 12, 2):
                dve.wait_ge(sem("filled"), outs.filled("kqT", j))
                emptied(nc.vector.tensor_copy(turned_heads(j), ps[0:QK, outs.bank("kqT", j), :].rearrange("p (b q) -> p b q", b=4)),
                        "kqT", j)
            for tt in range(TT):
                emptied(nc.vector.tensor_copy(ro[:, tt, :], take("ro", tt)), "ro", tt)
            def weights(h):
                s = 2 * h
                dve.wait_ge(sem("freed_act"), outs.nth[outs.at["s2"][s + 1]])
                step(nc.vector.reciprocal(rstd[:, s:s + 2], mx[:, s:s + 2]), "E2_scale")
                step(nc.vector.tensor_scalar(E2[:, s, :], E2[:, s, :], rstd[:, s:s + 1], None, ALU.mult), "E2_ready")

            def turned(h):
                if h >= 4:
                    dve.wait_ge(sem("oT2_pair"), h // 2 - 1)
                emptied(nc.vector.tensor_copy(ET2[:, h % 4, :, 0:P], take("eT", 2 * h).rearrange("p (k q) -> p k q", k=4)),
                        "eT", 2 * h)

            for h in range(MH + 2):
                if h < MH:
                    for s in (2 * h, 2 * h + 1):
                        src = take("s2", s)
                        step(nc.vector.tensor_reduce(ssum[:, s:s + 1], src, AX, ALU.max))
                        step(nc.vector.tensor_scalar(mneg[:, s:s + 1], ssum[:, s:s + 1], -QK ** -0.5, None, ALU.mult), "s2_max")
                if 1 <= h <= MH:
                    weights(h - 1)
                if h == 1:
                    dve.wait_ge(sem("ret_sq"), TT)
                    step(nc.vector.tensor_reduce(rsq, ro_sq.rearrange("p (h e) -> p h e", e=RDV), AX, ALU.add))
                    step(nc.vector.tensor_scalar(rsq, rsq, 1.0 / RDV, RMS_EPS, ALU.mult, ALU.add), "ret_var")
                if h == 4:
                    dve.wait_ge(sem("ret_root"), 1)
                    step(nc.vector.reciprocal(rsq, rsq), "ret_scale")
                if h >= 2:
                    turned(h - 2)
            dve.wait_ge(sem("ld_b"), 96)
            for i in range(3):
                step(nc.vector.tensor_copy(bpart, braw))
                r = slice(32 * i, 32 * i + 32)
                step(nc.vector.tensor_copy(b1p[r, :], bpart[r, 0:2 * FF2]))
                step(nc.vector.tensor_copy(b2p[r, :], bpart[r, 2 * FF2:]), "bias_parts")
                if i < 2:
                    step(nc.vector.tensor_tensor(braw, braw, bpart, ALU.subtract))
            dve.wait_ge(sem("freed_act"), outs.nth[outs.at["mb2"][1]])
            for j in range(4):
                tt, h = j // 2, j % 2
                cut = slice(512 * h, 512 * h + 512)
                part = gated[:, 512 * (j % 2):512 * (j % 2) + 512]
                emptied(nc.vector.tensor_tensor(part, take("wo2", j), mb2[:, cut], ALU.mult), "wo2", j)
                step(nc.vector.tensor_tensor(xs[:, tt, cut], xs[:, tt, cut], part, ALU.add), "wo2_added")
                if h:
                    mean_sq_row(xs[:, tt, :], tt, gated[:, 0:D])
            def scale_ff():
                for h in range(2):
                    cut = slice(512 * h, 512 * h + 512)
                    emptied(nc.vector.scalar_tensor_tensor(out=mb4[:, cut], in0=take("mb2", 2 + h), scalar=1.0,
                                                           in1=g_ff[:, cut], op0=ALU.add, op1=ALU.mult), "mb2", 2 + h)

            inverse_root(TT, scale_ff)
            for tt in range(TT):
                step(nc.vector.scalar_tensor_tensor(out=hf[:, tt, :], in0=xs[:, tt, :], scalar=rstd[:, tt:tt + 1],
                                                    in1=mb4, op0=ALU.mult, op1=ALU.mult))
                for h in range(2):
                    cut = slice(512 * h, 512 * h + 512)
                    ins = nc.vector.tensor_tensor(hf[:, tt, cut], hf[:, tt, cut], take("mb2", 4 + h), ALU.add)
                    if tt == 0:
                        step(ins)
                    else:
                        emptied(ins, "mb2", 4 + h)
                step(nc.vector.memset(flag, 0.0), "hf_ready")
            route(1)
            mixture(1)
            dve.wait_ge(sem("freed_act"), outs.emptied("mb5", "act"))
            for tt in range(TT):
                dve.wait_ge(sem("m2_scattered"), tt + 1)
                prod = act_[:, 1024 + 1024 * tt:2048 + 1024 * tt]
                step(nc.vector.tensor_tensor(prod, ps[:, 2 * tt:2 * tt + 2, :].rearrange("p b c -> p (b c)"),
                                             mb5, ALU.mult))
                step(nc.vector.tensor_tensor(xs[:, tt, :], xs[:, tt, :], prod, ALU.add), "y_ready")

        @block.gpsimd
        def _(pool):
            count = {}

            def step(ins, name="pool_step"):
                count[name] = count.get(name, 0) + 1
                ins.then_inc(sem(name), 1)
                pool.wait_ge(sem(name), count[name])

            def decays(h):
                pool.wait_ge(sem("dext_exp"), 2 * h + 2)
                own, back = dext[h][:, 2:4, :].rearrange("p k q -> p (k q)"), dtmp[:, h, 512:1024]
                step(nc.gpsimd.tensor_tensor(own, own, decay[:, 2048:2560], ALU.mult))
                step(nc.gpsimd.tensor_tensor(back, back, decay[:, 2560:3072], ALU.mult))
                d = dext[h].rearrange("p k q -> p (k q)")
                step(nc.gpsimd.tensor_tensor(d, d, dtmp[:, h, :], ALU.add), "dext_done")

            pool.wait_ge(sem("ld_latent"), 48)
            pool.wait_ge(sem("freed_act"), outs.emptied("mb", "act"))
            step(nc.gpsimd.tensor_tensor(mb[:, 1, :], mb[:, 1, :], g_at, ALU.mult))
            step(nc.gpsimd.tensor_tensor(mb[:, 1, :], mb[:, 1, :], g_at, ALU.add), "mb_ready")
            pool.wait_ge(sem("ld_decay"), 16)
            for h in range(RH):
                decays(h)
            pool.wait_ge(sem("freed_act"), outs.nth[outs.at["px"][3]])
            heads, nf = 2 * RH, RDK // 4
            x = px[:, :, O_RQ:O_RV].rearrange("p t (h e) -> p t h e", h=heads)
            cosv, sinv = (three(const(k), TT) for k in ("cosR", "sinR"))
            tmp = scr_p.rearrange("p (t h e) -> p t h e", t=TT, h=heads)
            for s in range(2):
                for ax in range(2):
                    o, i = 2 * nf * ax + nf * s, 2 * nf * ax + nf * (1 - s)
                    step(nc.gpsimd.tensor_tensor(tmp[:, :, :, o:o + nf], x[:, :, :, i:i + nf],
                                                 sinv[:, :, o:o + nf].unsqueeze(2).to_broadcast([P, TT, heads, nf]), ALU.mult))
            step(nc.gpsimd.tensor_tensor(x, x, cosv.unsqueeze(2).to_broadcast([P, TT, heads, RDK]), ALU.mult))
            step(nc.gpsimd.tensor_tensor(x, x, tmp, ALU.add), "roped_r")
            pool.wait_ge(sem("freed_dve"), outs.emptied("ro", "dve"))
            for tt in range(TT):
                step(nc.gpsimd.tensor_tensor(ro_sq[:, 512 * tt:512 * tt + 512], ro[:, tt, :], ro[:, tt, :], ALU.mult), "ret_sq")
            pool.wait_ge(sem("ret_scale"), 1)
            for tt in range(TT):
                o4 = ro[:, tt, :].rearrange("p (h e) -> p h e", h=RH)
                scale = rsq[:, RH * tt:RH * tt + RH].unsqueeze(2).to_broadcast([P, RH, RDV])
                step(nc.gpsimd.tensor_tensor(o4, o4, scale, ALU.mult))
                step(nc.gpsimd.tensor_tensor(ro[:, tt, :], ro[:, tt, :], g_ro, ALU.mult))
                step(nc.gpsimd.tensor_tensor(ro[:, tt, :], ro[:, tt, :], rg[:, tt, :], ALU.mult), "ro_ready")

        @block.tensor
        def _(pe):
            filled = sem("filled")

            def bank(name, j):
                b = outs.before(name, j)
                if b is not None:
                    pe.wait_ge(sem("freed_" + b[0]), b[1])
                return ps[:, outs.bank(name, j), :]

            def turn(name, j, blocks):
                dst = bank(name, j)
                for i, b in enumerate(blocks):
                    n = b.shape[-1]
                    m = b.shape[0]
                    mm = nc.tensor.transpose(dst[0:n, P * i:P * i + m] if m == P else dst[0:n, 0:m], b, ident[0:m, 0:m])
                mm.then_inc(filled, 1)

            def quarter(ap, h):
                return [ap[:, P * (4 * h + i):P * (4 * h + i) + P] for i in range(4)]

            def keep_clock(n):
                with pe.Fori(0, n):
                    nc.tensor.transpose(ps[:, 7, 0:P], ident, ident)

            pe.wait_ge(sem("ld_consts"), 16)
            pe.wait_ge(sem("ld_x"), 16)
            for j in range(4):
                turn("xT", j, quarter(xs[:, j // 2, :], j % 2))
            pe.wait_ge(sem("cc_ready"), 1)
            nc.tensor.transpose(ps[:, 7, 0:16], cc, ident[0:16, 0:16]).then_inc(sem("ccT_mm"), 1)

            def proj(j):
                c, tt = CHUNKS[j // 2], j % 2
                pe.wait_ge(sem(f"ld_win{c}"), 16)
                dst = bank("proj", j)
                if j < 2:
                    pe.wait_ge(freed_act, outs.nth[outs.at["xT"][2 * tt + 1]])
                for k in range(KT):
                    mm = nc.tensor.matmul(dst, tT[:, k, P * tt:P * tt + P], w_in[:, c, 512 * k:512 * k + 512],
                                          start=(k == 0), stop=(k == KT - 1))
                mm.then_inc(filled, 1)

            def modulation(i):
                r, half = i // 2, i % 2
                dst = bank("ada", r) if half == 0 else ps[:, outs.bank("ada", r), :]
                pe.wait_ge(sem(f"ld_ada{half}"), 16 * (r + 1))
                if i == 0:
                    pe.wait_ge(sem("ccT_ready"), 1)
                for k in range(KT // 2 * half, KT // 2 * half + KT // 2):
                    for g in range(4):
                        mm = nc.tensor.matmul(dst[32 * g:32 * g + 32, :], ccT[:, k, :], ada[:, k, 512 * g:512 * g + 512],
                                              start=(k == 0), stop=(k == KT - 1))
                mm.then_inc(filled if half else sem("ada_used"), 1)

            def spread(name, j, v, h, ctx_row):
                c = 2 * v + h
                r = 32 * (c % 4) + ctx_row
                nc.tensor.matmul(bank(name, j), ident[:, r:r + 1].to_broadcast([P, P]), modrow[:, c // 4, :],
                                 start=True, stop=True).then_inc(filled, 1)

            freed_act = sem("freed_act")
            for j in range(5):
                proj(j)
            pe.wait_ge(sem("roped1"), 1)
            for j in range(4):
                turn("qkT", j, quarter(qk[:, j // 2, :], j % 2))
            modulation(0)
            proj(5)
            modulation(1)
            pe.wait_ge(freed_act, outs.emptied("qkT", "act"))
            order = [0, 2, 4, 6, 1, 3, 5, 7]
            for j in range(6):
                dst = bank("sc", j)
                qt, hs = (0, order[4 * j:4 * j + 4]) if j < 2 else (1, order[2 * (j - 2):2 * (j - 2) + 2])
                w = P * (qt + 1)
                for i, h in enumerate(hs):
                    r = slice(64 * (h % 2), 64 * (h % 2) + 64)
                    mm = nc.tensor.matmul(dst[:, w * i:w * i + w], qkT[r, h // 2, P * qt:P * qt + P],
                                          qkT[r, 4 + h // 2, 0:w], start=True, stop=True)
                mm.then_inc(filled, 1)
            pe.wait_ge(sem("ld_spatial"), 32)
            for j in range(2):
                turn("wsT", j, quarter(w_sp, j))
            turn("bsT", 0, [b_sp])
            proj(6)
            modulation(2)
            proj(7)
            modulation(3)
            proj(8)
            modulation(4)
            proj(9)
            modulation(5)
            pe.wait_ge(sem("vs_ready"), TT)
            for j in range(2):
                dst = bank("z", j)
                for i in range(4):
                    g = 4 * j + i
                    mm = nc.tensor.matmul(dst[:, P * i:P * i + P], wsT[:, g, :], vs1[:, :, 64 * g:64 * g + 64],
                                          start=True, stop=True)
                mm.then_inc(filled, 1)
            pe.wait_ge(sem("E_ready"), 2)
            for j in range(6):
                (qt, kt), h = ((0, 0), (1, 0), (1, 1))[j // 2], j % 2
                e = E0 if qt == 0 else E1
                turn("ET", j, [e[:, 4 * h + i, P * kt:P * kt + P] for i in range(4)])
            pe.wait_ge(freed_act, outs.emptied("ET", "act"))
            for m in range(2):
                for j in (2 * m, 2 * m + 1):
                    for h in (2 * j, 2 * j + 1):
                        pos = order.index(h)
                        dst = ps[64 * (h % 2):64 * (h % 2) + 64, 6 + m, S * (j % 2):S * (j % 2) + S]
                        nc.tensor.matmul(dst, v1[:, 0, 64 * h:64 * h + 64], ET[:, 0, pos, :], start=True, stop=False)
                        mm = nc.tensor.matmul(dst[:, P:S], v1[:, 1, 64 * h:64 * h + 64], ET[:, 1, pos, P:S],
                                              start=False, stop=True)
                mm.then_inc(sem("oT_mm"), 1)
            pe.wait_ge(sem("sgu_ready"), 1)
            for tt in range(TT):
                turn("mT", tt, quarter(u1[:, tt, :], 0))
            pe.wait_ge(sem("freed_dve"), outs.nth[outs.at["ada"][0]])
            for j in range(4):
                spread("mbc", j, j // 2, j % 2, 1)
            pe.wait_ge(sem("oT_taken"), 2)
            pe.wait_ge(freed_act, outs.emptied("mT", "act"))
            pe.wait_ge(sem("ld_wo"), 16)
            for j in range(4):
                tt, h = j // 2, j % 2
                dst = bank("wo", j)
                for k in range(KT):
                    mm = nc.tensor.matmul(dst, mixT[:, k, P * tt:P * tt + P], wo_w[:, k, 512 * h:512 * h + 512],
                                          start=(k == 0), stop=(k == KT - 1))
                mm.then_inc(filled, 1)

            def route(m, xT, w, name):
                pe.wait_ge(freed_act, outs.emptied(name, "act"))
                pe.wait_ge(sem("ld_small"), 96)
                n = w.shape[-1]
                dst = bank(f"lp{m + 1}", 0)
                for k in range(KT // 2):
                    for g in range(2):
                        mm = nc.tensor.matmul(dst[64 * g:64 * g + n, 0:S], w[:, KT // 2 * g + k, :], xT[:, KT // 2 * g + k, :],
                                              start=(k == 0), stop=(k == KT // 2 - 1))
                mm.then_inc(filled, 1)
                pe.wait_ge(sem("freed_dve"), outs.emptied(f"lp{m + 1}", "dve"))
                dst = bank(f"lg{m + 1}", 0)
                for tt in range(TT):
                    mm = nc.tensor.matmul(dst[:, 64 * tt:64 * tt + n], logit_parts[:, P * tt:P * tt + P], const("pair")[:, 0:n],
                                          start=True, stop=True)
                mm.then_inc(filled, 1)
                pe.wait_ge(sem("sel_ready"), m + 1)
                dst = bank(f"cn{m + 1}", 0)
                for q in range(2 - m):
                    for tt in range(TT):
                        mm = nc.tensor.matmul(dst[:, 2 * q:2 * q + 2], row_sel(q, tt), ones[:, 0:2],
                                              start=(tt == 0), stop=(tt == 1))
                mm.then_inc(filled, 1)
                pe.wait_ge(sem("flags"), m + 1)
                nc.tensor.matmul(bank(f"ps{m + 1}", 0)[:, 0:2], const("upper"), flag, start=True, stop=True).then_inc(filled, 1)
                dst = bank(f"rk{m + 1}", 0)
                nc.tensor.matmul(dst[:, 0:NE], const("upper"), sel[:, 0, :], start=True, stop=True)
                nc.tensor.matmul(dst[:, NE:2 * NE], ones, sel[:, 0, :], start=True, stop=False)
                nc.tensor.matmul(dst[:, NE:2 * NE], const("upper"), sel[:, 1, :], start=False, stop=True).then_inc(filled, 1)
                pe.wait_ge(sem("places_ready"), m + 1)
                dst = bank(f"tb{m + 1}", 0)
                place = rstd[:, 0:1]
                for i, (col, rhs) in enumerate(((const(f"group{m}"), place_of), (const(f"off{m}"), place_of),
                                                (ones[:, 0:1], place_of), (place, const(f"first{m}")))):
                    mm = nc.tensor.matmul(dst[:, 64 * i:64 * i + rhs.shape[-1]], col.to_broadcast([P, P]), rhs,
                                          start=True, stop=True)
                mm.then_inc(filled, 1)
                pe.wait_ge(sem("freed_dve"), outs.emptied(f"rk{m + 1}", "dve"))
                zero_sums([b for b in range(4) if b != outs.bank(f"tb{m + 1}", 0)])

            def zero_sums(banks):
                for b in banks:
                    if b < 4:
                        nc.tensor.matmul(ps[:, b, :], pgT[0].bitcast(BF16)[:, 0:P], m_y.bitcast(BF16)[:, 0:512], start=True,
                                         stop=False, skip_group_check=True)

            def mixture(m, h):
                p = f"m{m + 1}_"

                def tokens_in(n):
                    pe.wait_ge(sem(p + "hot"), n + 1)
                    for tt in range(TT):
                        for g in range(2):
                            mm = nc.tensor.matmul(ps[64 * g:64 * g + 64, 6, :], hot[:, tt, :],
                                                  h[:, tt, HALF * g:HALF * g + HALF], start=(tt == 0), stop=(tt == TT - 1))
                    mm.then_inc(sem(p + "gathered"), 1)

                def tokens_turned(n):
                    pe.wait_ge(sem(p + "xg"), n + 1)
                    for i in range(4):
                        mm = nc.tensor.transpose(ps[:, 6, P * i:P * i + P], xg[:, P * i:P * i + P], ident)
                    mm.then_inc(sem(p + "xg_turned"), 1)

                def tokens_out(last_unit=False):
                    for tt in range(TT):
                        for g in range(2):
                            mm = nc.tensor.matmul(ps[:, 2 * tt + g, :], pgT[g][:, P * tt:P * tt + P], m_y, start=False,
                                                  stop=False, skip_group_check=True)
                        if last_unit:
                            mm.then_inc(sem(p + "scattered"), 1)

                def up_pair(loads):
                    for q in range(2):
                        for k in range(KT):
                            if k % 4 == 0:
                                pe.wait_ge(sem(f"ld_gu{q}{k // 4}"), loads)
                            o = P * (k % 4) + 64 * (k // 4) + 32 * q
                            for g in range(2):
                                r = 64 * g + 32 * q
                                mm = nc.tensor.matmul(ps[r:r + 32, 4, 0:256], xgT[:, o:o + 32], gu_w[:, q, k, :, g, :],
                                                      start=(k == 0), stop=(k == KT - 1))
                        mm.then_inc(sem("m1_up_used"), 1)

                def down_pair(loads):
                    for q in range(2):
                        pe.wait_ge(sem(f"ld_dn{q}"), loads)
                    for k in range(FF1 // P):
                        for q in range(2):
                            for g in range(2):
                                r, o = 64 * g + 32 * q, 64 * k + 32 * q
                                mm = nc.tensor.matmul(ps[r:r + 32, 7, :], m_aT[:, o:o + 32],
                                                      dn_w[:, q, k, HALF * g:HALF * g + HALF],
                                                      start=(k == 0), stop=(k == FF1 // P - 1))
                    mm.then_inc(sem(p + "dn_mm"), 1)

                def bias(i, part, bank_, o):
                    for g in range(2):
                        c = o + g * (FF2 if i == 0 else HALF)
                        nc.tensor.matmul(ps[64 * g:64 * g + 64, bank_, :], bsel[i], part[:, c:c + 512],
                                         start=True, stop=False)

                def up_expert(loads):
                    for k in range(KT):
                        pe.wait_ge(sem(f"ld_w1_{k}"), loads)
                        o = P * (k % 4) + 64 * (k // 4)
                        for b in range(2):
                            for g in range(2):
                                c = FF2 * g + 512 * b
                                mm = nc.tensor.matmul(ps[64 * g:64 * g + 64, 4 + b, :], xgT[:, o:o + 64],
                                                      w1_w[:, k, c:c + 512], start=False, stop=(k == KT - 1))
                        mm.then_inc(sem("m2_w1_used"), 1)

                def down_expert(loads):
                    for k in range(FF2 // P):
                        pe.wait_ge(sem(f"ld_w2_{k}"), loads)
                        o = P * (k % 4) + 64 * (k // 4)
                        for g in range(2):
                            mm = nc.tensor.matmul(ps[64 * g:64 * g + 64, 7, :], m_aT[:, o:o + 64],
                                                  w2_w[:, k, HALF * g:HALF * g + HALF], start=False, stop=(k == FF2 // P - 1))
                        mm.then_inc(sem("m2_w2_used"), 1)

                pe.wait_ge(sem("table_ready"), m + 1)
                if m == 1:
                    pe.wait_ge(sem("bias_parts"), 3)
                zero_sums([outs.bank(f"tb{m + 1}", 0)])
                pe.sem_inc(sem(p + "y"), 1)
                pe.sem_inc(sem(p + "pgT"), 2)
                keep_clock(6)
                tokens_in(0)
                keep_clock(6)
                tokens_turned(0)
                last = pe.value_load(table[0:1, TABLE:TABLE + 1], min_val=GROUPS[m] - 1, max_val=TABLE - 5)
                def unit(n, more=True):
                    loads = pe.value_load(table[0:1, bass.ds(n, 1)], min_val=0, max_val=GROUPS[m] - 1) * 16 + 16
                    pe.wait_ge(sem(p + "pgT"), n * 2 + 2)
                    if m == 0:
                        pe.wait_ge(sem(p + "xgT"), n + 1)
                        up_pair(loads)
                        pe.wait_ge(sem("m1_up_used"), n * 2 + 2)
                    else:
                        pe.wait_ge(sem("m2_bsel1"), n + 1)
                        for b in range(2):
                            bias(0, b1p, 4 + b, 512 * b)
                        pe.wait_ge(sem(p + "xgT"), n + 1)
                        up_expert(loads)
                        pe.wait_ge(sem("m2_w1_used"), n * KT + KT)
                    pe.sem_inc(sem(p + "up_mm"), 1)
                    pe.wait_ge(sem(p + "y"), n + 1)
                    tokens_out()
                    pe.wait_ge(sem(p + "act"), n + 1)
                    for i in range(1 if m == 0 else 4):
                        mm = nc.tensor.transpose(ps[:, 4, P * i:P * i + P], m_a[:, P * i:P * i + P], ident)
                    mm.then_inc(sem(p + "a_turned"), 1)
                    if m == 0:
                        pe.wait_ge(sem(p + "aT"), n + 1)
                        down_pair(loads)
                    else:
                        pe.wait_ge(sem("m2_bsel2"), n + 1)
                        bias(1, b2p, 7, 0)
                        pe.wait_ge(sem(p + "aT"), n + 1)
                        down_expert(loads)
                        pe.wait_ge(sem("m2_w2_used"), n * KT + KT)
                        pe.sem_inc(sem(p + "dn_mm"), 1)
                    if more:
                        tokens_in(n + 1)
                    pe.wait_ge(sem(p + "hotg"), n * 2 + 2)
                    for tt in range(TT):
                        mm = nc.tensor.transpose(ps[:, 5, P * tt:P * tt + P], hotg[:, tt].rearrange("p d s -> p (d s)"), ident)
                    mm.then_inc(sem(p + "hot_turned"), 1)
                    if more:
                        tokens_turned(n + 1)

                if m == 0:
                    for tt in range(TT):
                        with pe.Fori(PIECES * tt, PIECES * tt + PIECES) as n:
                            unit(n)
                            o = (n - PIECES * tt) * P + O_RK
                            pe.wait_ge(sem("ld_w_in_2"), 32)
                            for k in range(KT):
                                mm = nc.tensor.matmul(ps[:, 4, 0:P], hTc[:, k, P * tt:P * tt + P], w_in2[:, k, bass.ds(o, P)],
                                                      start=(k == 0), stop=(k == KT - 1))
                            mm.then_inc(sem("pc_mm"), 1)
                            pe.wait_ge(sem("pc_taken"), n + 1)
                with pe.Fori(0 if m else TT * PIECES, last) as n:
                    unit(n)
                unit(last, more=False)
                pe.wait_ge(sem(p + "y"), last + 2)
                pe.wait_ge(sem(p + "pgT"), last * 2 + 4)
                tokens_out(last_unit=True)

            pe.wait_ge(sem("hc_ready"), TT)
            for j in range(4):
                turn("hTc", j, quarter(cx[:, j // 2, :], j % 2))
            for j in range(4):
                pe.wait_ge(sem("h1_ready"), j // 2 + 1)
                turn("hT", j, quarter(xs[:, j // 2, :], j % 2))
            route(0, tT, wr1, "hT")
            pe.wait_ge(sem("freed_dve"), outs.emptied("tb1", "dve"))
            mixture(0, xs)

            pe.wait_ge(sem("m1_sums_read"), TT)
            for j in range(4):
                spread("mb", j, j // 2, j % 2, 0)
            for tt in range(TT):
                dst = bank("pc", tt)
                for k in range(KT):
                    mm = nc.tensor.matmul(dst[:, 0:160], hTc[:, k, P * tt:P * tt + P], w_in2[:, k, O_KV:O_RQ],
                                          start=(k == 0), stop=(k == KT - 1))
                mm.then_inc(filled, 1)
            keep_clock(WARM)
            for j in range(4):
                if j % 2 == 0:
                    pe.wait_ge(sem("hn_ready"), j // 2 + 1)
                turn("hT4", j, quarter(hn[:, j // 2, :], j % 2))

            def project(j):
                (o, w), tt = PX[j // 2], j % 2
                pe.wait_ge(freed_act, outs.nth[outs.at["hT4"][2 * tt + 1]])
                dst = bank("px", j)
                for k in range(KT):
                    mm = nc.tensor.matmul(dst[:, 0:w], hTc[:, k, P * tt:P * tt + P], w_in2[:, k, o:o + w],
                                          start=(k == 0), stop=(k == KT - 1))
                mm.then_inc(filled, 1)

            def keys_values(j):
                nc.tensor.matmul(bank("kv", j), cT[:, j // 2, :], wkvu[:, 512 * (j % 2):512 * (j % 2) + 512],
                                 start=True, stop=True).then_inc(filled, 1)

            project(0)
            project(1)
            pe.wait_ge(sem("latents"), TT)
            turn("cT", 0, [cn_[:, 0:P], cn_[:, P:2 * P]])
            project(2)
            pe.wait_ge(sem("latents"), 3 * TT)
            turn("cT", 1, [cn_[:, 2 * P:3 * P], cn_[:, 3 * P:4 * P]])
            turn("cT", 2, quarter(cn_, 1))
            pe.wait_ge(freed_act, outs.nth[outs.at["cT"][0]])
            pe.wait_ge(sem("ld_latent"), 48)
            for j in range(8):
                if j == 4:
                    pe.wait_ge(freed_act, outs.emptied("cT", "act"))
                keys_values(j)
            pe.wait_ge(sem("ld_latent"), 48)
            for j in range(4):
                tt, h = j // 2, j % 2
                dst = bank("qu", j)
                for k in range(2):
                    mm = nc.tensor.matmul(dst[:, 0:4 * QK], cT[:, 4 + 2 * tt + k, :], wqu[:, k, 4 * QK * h:4 * QK * (h + 1)],
                                          start=(k == 0), stop=(k == 1))
                mm.then_inc(filled, 1)
            project(3)
            project(4)
            project(5)
            pe.wait_ge(sem("roped_r"), 1)
            for tt in range(TT):
                turn("rT", tt, [px[:, tt, O_RQ + P * i:O_RQ + P * i + P] for i in range(4)])
            turn("rT", 2, [pc[:, i % 2, 160 + P * (i // 2):160 + P * (i // 2) + P] for i in range(4)])
            project(6)
            project(7)
            pe.wait_ge(freed_act, outs.emptied("rT", "act"))
            for j in range(2 * RH):
                h, half = j // 2, j % 2
                r = slice(64 * (h % 2), 64 * (h % 2) + 64)
                dst = bank("rs", j)
                for i in range(2):
                    k = 2 * half + i
                    mm = nc.tensor.matmul(dst[:, S * i:S * i + S], rkT[r, h // 2, P * k:P * k + P], rqT[r, h // 2, :],
                                          start=True, stop=True)
                mm.then_inc(filled, 1)
            pe.wait_ge(sem("kq_ready"), 1)
            for j in range(12):
                tile, h = j // 2, j % 2
                x = K2[:, tile] if tile < 4 else Q2[:, tile - 4]
                turn("kqT", j, [x[:, 4 * h + i, :] for i in range(4)])
            pe.wait_ge(sem("freed_dve"), outs.emptied("rs", "dve"))
            pe.wait_ge(freed_act, outs.emptied("px", "act"))
            vals = [pc[:, 0, 416:928], pc[:, 1, 416:928], px[:, 0, O_RV:O_RG], px[:, 1, O_RV:O_RG]]
            for tt in range(TT):
                dst = bank("ro", tt)
                for h in range(RH):
                    for k in range(4):
                        mm = nc.tensor.matmul(dst[:, P * h:P * h + P], sd[:, h, k, P * tt:P * tt + P],
                                              vals[k][:, RDV * h:RDV * h + RDV], start=(k == 0), stop=(k == 3))
                mm.then_inc(filled, 1)
            pe.wait_ge(freed_act, outs.emptied("kqT", "act"))
            pe.wait_ge(sem("freed_dve"), outs.emptied("kqT", "dve"))

            def scores(h):
                for qt in range(TT):
                    nc.tensor.matmul(bank("s2", 2 * h + qt), qT2[:, h, P * qt:P * qt + P], kT2[:, h, :],
                                     start=True, stop=True).then_inc(filled, 1)

            def turn_weights(h):
                for qt in range(TT):
                    s = 2 * h + qt
                    pe.wait_ge(sem("E2_ready" if qt == 0 else "E2_ready_act"), h + 1)
                    turn("eT", s, quarter(E2[:, s, :], 0))

            def heads_out(h):
                pe.wait_ge(sem("freed_dve"), outs.nth[outs.at["eT"][2 * h + 2]])
                pe.wait_ge(freed_act, outs.nth[outs.at["eT"][2 * h + 3]])
                m, o = h // 4, S * (h // 2 % 2)
                for k in range(4):
                    for i in range(2):
                        mm = nc.tensor.matmul(ps[64 * i:64 * i + 64, 6 + m, o:o + S], V2[:, k, 64 * (h + i):64 * (h + i) + 64],
                                              ET2[:, (h + i) % 4, k, :], start=(k == 0), stop=(k == 3))
                mm.then_inc(sem("oT2_pair"), 1)
                if h % 4 == 2:
                    pe.wait_ge(sem("oT2_pair"), h // 2 + 1)
                    pe.sem_inc(sem("oT2_mm"), 1)

            def project_out(j, first, last):
                tt, h = j // 2, j % 2
                dst = bank("wo2", j) if first else ps[:, outs.bank("wo2", j), :]
                r = range(KT // 2, KT) if first else range(KT // 2)
                for k in r:
                    mm = nc.tensor.matmul(dst, mixT2[:, k, P * tt:P * tt + P], wo2_w[:, k, 512 * h:512 * h + 512],
                                          start=(first and k == r[0]), stop=(last and k == r[-1]))
                return mm

            for h in range(MH + 2):
                if h < MH:
                    scores(h)
                if h == MH + 1:
                    pe.wait_ge(sem("ro_ready"), TT)
                    for tt in range(TT):
                        turn("rmT", tt, quarter(ro[:, tt, :], 0))
                if h >= 2:
                    turn_weights(h - 2)
                if h >= 4 and h % 2 == 0:
                    heads_out(h - 4)
            for j in range(2):
                spread("mb2", j, 2, j, 0)
            pe.wait_ge(freed_act, outs.emptied("rmT", "act"))
            pe.wait_ge(sem("ld_wo2"), 16)
            project_out(0, True, False)
            heads_out(MH - 2)
            project_out(1, True, False)
            pe.wait_ge(sem("oT2_taken"), 2)
            project_out(0, False, True).then_inc(filled, 1)
            project_out(1, False, True).then_inc(filled, 1)
            for j in range(2, 4):
                project_out(j, True, False)
                project_out(j, False, True).then_inc(filled, 1)
            for j in range(2, 6):
                spread("mb2", j, 5 - j // 2, j % 2, 0)
            pe.wait_ge(sem("hf_ready"), 1)
            for j in range(4):
                if j == 2:
                    pe.wait_ge(sem("hf_ready"), TT)
                turn("hfT", j, quarter(hf[:, j // 2, :], j % 2))
            for j in range(2):
                spread("mb5", j, 5, j, 0)
            route(1, hfT, wr2, "hfT")
            pe.wait_ge(sem("freed_dve"), outs.emptied("tb2", "dve"))
            mixture(1, hf)


def kernel(**inputs):
    import concourse.bacc as _bacc
    from concourse.bass_utils import run_bass_kernel_spmd as _run

    a = {k: np.asarray(v) for k, v in inputs.items()}
    const_at, (consts, early, masks), decay = host_constants()
    arrays = {
        "consts": consts, "early": early, "masks": masks, "decay": decay,
        "x": a["x"][0], "pos": a["positions"][0].reshape(TT, P).T,
        "w_in": a["w_in"][0],
        "vec1": np.concatenate([a["sgu_ln_g"][0], a["sgu_ln_b"][0], a["ln1_g"][0], a["ln1_b"][0], a["ln2_g"][0],
                                a["ln2_b"][0]]),
        "w_spatial": a["w_spatial"][0], "b_spatial": a["b_spatial"][0], "w_out": a["w_out"][0],
        "wr1": np.concatenate([a["w_group"][0], a["w_expert"][0].transpose(1, 0, 2).reshape(D, NE)], 1),
        "rb1": np.concatenate([a["b_group"][0], a["b_expert"][0].reshape(NE)]),
        "w_gate_up": a["w_gate_up"][0].reshape(NE, D, 2 * FF1), "w_down": a["w_down"][0].reshape(NE, FF1, D),
        "cc": np.concatenate([a["c_2"][0].reshape(KT, P), a["c_ctx_2"].reshape(KT, P)], 0),
        "ctx": a["ctx_2"][0], "w_ada_2": a["w_ada_2"][0], "b_ada": a["b_ada_2"][0].reshape(3, 4, 512),
        "w_in_2": a["w_in_2"][0],
        "vec2": np.concatenate([a["g_attn_2"][0], a["g_ffn_2"][0], a["g_q_lora_2"][0], a["g_kv_lora_2"][0],
                                a["g_q_head_2"][0], a["g_k_head_2"][0], a["g_ret_out_2"][0]]),
        "w_q_up_2": a["w_q_up_2"][0], "w_kv_up_2": a["w_kv_up_2"][0],
        "decay_logit": a["ret_decay_logit_2"][0].reshape(2 * RH), "w_out_2": a["w_out_2"][0],
        "wr2": a["w_router_2"][0], "rb2": a["b_router_2"][0],
        "w_mlp1_2": a["w_mlp1_2"][0], "b_mlp1_2": a["b_mlp1_2"][0], "w_mlp2_2": a["w_mlp2_2"][0],
        "b_mlp2_2": a["b_mlp2_2"][0],
    }
    arrays = {f"in_{k}": np.ascontiguousarray(v) for k, v in arrays.items()}
    nc = _bacc.Bacc("TRN2", target_bir_lowering=False, num_devices=1)
    t = {k[3:]: nc.dram_tensor(k, v.shape, mybir.dt.from_np(v.dtype), kind="ExternalInput").ap() for k, v in arrays.items()}
    out = nc.dram_tensor("out_x", (S, D), F32, kind="ExternalOutput").ap()
    build(nc, t, out, const_at)
    r = _run(nc, [arrays], core_ids=[0])
    return r.results[0]["out_x"].reshape(1, S, D)
```
